# Optimizing a Trainium2 kernel written in Bass

```python
import math
import jax, jax.numpy as jnp
from jax import lax
import numpy as np

D_MODEL = 2048
BATCH = 1
SEQ = 512
DEPTH = 1
DEC_BATCH = 8
DEC_SEQ = 1
PAST_LEN = 2048
PAGE_SIZE = 128

MIX_WIDTH = D_MODEL
ATTN_WIDTH = MIX_WIDTH // 2
N_ATTN_HEADS = 8
DV = ATTN_WIDTH // N_ATTN_HEADS
DK = DV // 2
D_INNER = MIX_WIDTH - ATTN_WIDTH
SSM_HEADDIM = 64
N_SSM_HEADS = D_INNER // SSM_HEADDIM
N_GROUPS = 2
HEADS_PER_GROUP = N_SSM_HEADS // N_GROUPS
D_STATE = 128
CONV_W = 4
CONV_DIM = D_INNER + 2 * N_GROUPS * D_STATE
CHUNK = 128
Q_BLOCK = 128
D_FF = 4 * D_MODEL
PLE_DIM = 256
D_PROJ = 3 * ATTN_WIDTH + D_INNER + CONV_DIM + N_SSM_HEADS
NORM_EPS = 1e-6
SUBLN_EPS = 1e-5

kernel_name = "hymba_diffattn_ssd_step"

def _rmsnorm(x, g, eps=NORM_EPS):
    xf = x.astype(jnp.float32)
    y = xf * lax.rsqrt(jnp.mean(xf * xf, axis=-1, keepdims=True) + eps)
    return (y * g.astype(jnp.float32)).astype(x.dtype)

def _alibi_slopes():
    return 2.0 ** (-8.0 * jnp.arange(1, N_ATTN_HEADS + 1, dtype=jnp.float32) / N_ATTN_HEADS)

def _split_proj(u, w_in):
    proj = u @ w_in
    cuts = np.cumsum([ATTN_WIDTH, ATTN_WIDTH, ATTN_WIDTH, D_INNER, CONV_DIM]).tolist()
    q, k, v, z, xbc, dt = jnp.split(proj, cuts, axis=-1)
    lead = u.shape[:-1]
    q = q.reshape(*lead, N_ATTN_HEADS, 2, DK)
    k = k.reshape(*lead, N_ATTN_HEADS, 2, DK)
    v = v.reshape(*lead, N_ATTN_HEADS, DV)
    return q, k, v, z, xbc, dt

def _diff_weights(s, lam):
    p = jax.nn.softmax(s, axis=-1)
    return p[:, :, 0] - lam * p[:, :, 1]

def _prompt_diff_attn(q, k, v, lam):
    b, s = q.shape[:2]
    nb = s // Q_BLOCK
    scale = DK ** -0.5
    slopes = _alibi_slopes()
    kpos = jnp.arange(s)
    qb = jnp.moveaxis(q.reshape(b, nb, Q_BLOCK, N_ATTN_HEADS, 2, DK), 1, 0)
    starts = jnp.arange(nb) * Q_BLOCK

    def one_block(args):
        qblk, st = args
        sc = jnp.einsum('bqhcd,bkhcd->bhcqk', qblk, k).astype(jnp.float32) * scale
        dist = ((st + jnp.arange(Q_BLOCK))[:, None] - kpos[None, :]).astype(jnp.float32)
        bias = jnp.where(dist[None] >= 0, -slopes[:, None, None] * dist[None], -jnp.inf)
        w = _diff_weights(sc + bias[None, :, None], lam)
        return jnp.einsum('bhqk,bkhd->bqhd', w.astype(v.dtype), v)

    o = lax.map(one_block, (qb, starts))
    return jnp.moveaxis(o, 0, 1).reshape(b, s, N_ATTN_HEADS, DV)

def _sample_diff_attn(q, k_new, v_new, k_past, v_past, lam):
    t = q.shape[1]
    p = k_past.shape[1]
    scale = DK ** -0.5
    slopes = _alibi_slopes()
    dist_p = ((p + jnp.arange(t))[:, None] - jnp.arange(p)[None, :]).astype(jnp.float32)
    bias_p = -slopes[:, None, None] * dist_p[None]
    dist_n = (jnp.arange(t)[:, None] - jnp.arange(t)[None, :]).astype(jnp.float32)
    bias_n = jnp.where(dist_n[None] >= 0, -slopes[:, None, None] * dist_n[None], -jnp.inf)
    s_p = jnp.einsum('bqhcd,bkhcd->bhcqk', q, k_past).astype(jnp.float32) * scale + bias_p[None, :, None]
    s_n = jnp.einsum('bqhcd,bkhcd->bhcqk', q, k_new).astype(jnp.float32) * scale + bias_n[None, :, None]
    w = _diff_weights(jnp.concatenate([s_p, s_n], axis=-1), lam).astype(v_new.dtype)
    return (jnp.einsum('bhqk,bkhd->bqhd', w[..., :p], v_past)
            + jnp.einsum('bhqk,bkhd->bqhd', w[..., p:], v_new))

def _attn_out(o, w_sub, lam_init):
    o = _rmsnorm(o, w_sub, SUBLN_EPS) * (1.0 - lam_init)
    return o.reshape(*o.shape[:-2], ATTN_WIDTH)

def _causal_conv(xpad, w, b):
    t = xpad.shape[1] - (CONV_W - 1)
    out = b + sum(xpad[:, j:j + t] * w[j] for j in range(CONV_W))
    return jax.nn.silu(out)

def _ssm_inputs(xbc_act, dt_raw, dt_bias, a_log):
    lead = xbc_act.shape[:-1]
    xs, bm, cm = jnp.split(xbc_act, [D_INNER, D_INNER + N_GROUPS * D_STATE], axis=-1)
    xs = xs.reshape(*lead, N_SSM_HEADS, SSM_HEADDIM).astype(jnp.float32)
    bm = bm.reshape(*lead, N_GROUPS, D_STATE).astype(jnp.float32)
    cm = cm.reshape(*lead, N_GROUPS, D_STATE).astype(jnp.float32)
    dt = jax.nn.softplus(dt_raw.astype(jnp.float32) + dt_bias.astype(jnp.float32))
    a = -jnp.exp(a_log.astype(jnp.float32))
    return xs, bm, cm, dt, a

def _ssd_chunked(xs, dt, a, bm, cm):
    b, s = xs.shape[:2]
    c = s // CHUNK
    xd = (xs * dt[..., None]).reshape(b, c, CHUNK, N_GROUPS, HEADS_PER_GROUP, SSM_HEADDIM)
    da = (dt * a).reshape(b, c, CHUNK, N_GROUPS, HEADS_PER_GROUP).transpose(0, 3, 4, 1, 2)
    a_cs = jnp.cumsum(da, axis=-1)
    bc = bm.reshape(b, c, CHUNK, N_GROUPS, D_STATE)
    cc = cm.reshape(b, c, CHUNK, N_GROUPS, D_STATE)
    causal = jnp.tril(jnp.ones((CHUNK, CHUNK), dtype=bool))
    seg = a_cs[..., :, None] - a_cs[..., None, :]
    lmat = jnp.exp(jnp.where(causal, seg, -jnp.inf))
    cb = jnp.einsum('bclgn,bcsgn->bcgls', cc, bc)
    y_diag = jnp.einsum('bcgls,bgjcls,bcsgjp->bclgjp', cb, lmat, xd)
    decay_states = jnp.exp(a_cs[..., -1:] - a_cs)
    states = jnp.einsum('bcsgn,bgjcs,bcsgjp->cbgjpn', bc, decay_states, xd)
    chunk_decay = jnp.exp(a_cs[..., -1]).transpose(3, 0, 1, 2)

    def step(carry, inp):
        st, dec = inp
        return carry * dec[..., None, None] + st, carry

    init = jnp.zeros((b, N_GROUPS, HEADS_PER_GROUP, SSM_HEADDIM, D_STATE), jnp.float32)
    final, states_in = lax.scan(step, init, (states, chunk_decay))
    y_off = jnp.einsum('bclgn,cbgjpn,bgjcl->bclgjp', cc, states_in, jnp.exp(a_cs))
    y = (y_diag + y_off).reshape(b, s, N_SSM_HEADS, SSM_HEADDIM)
    return y, final.reshape(b, N_SSM_HEADS, SSM_HEADDIM, D_STATE)

def _ssm_recurrent(xs, dt, a, bm, cm, state0):
    db, t = xs.shape[:2]
    xt = jnp.moveaxis(xs.reshape(db, t, N_GROUPS, HEADS_PER_GROUP, SSM_HEADDIM), 1, 0)
    dtt = jnp.moveaxis(dt.reshape(db, t, N_GROUPS, HEADS_PER_GROUP), 1, 0)
    bt = jnp.moveaxis(bm, 1, 0)
    ct = jnp.moveaxis(cm, 1, 0)
    a_gj = a.reshape(N_GROUPS, HEADS_PER_GROUP)

    def step(st, inp):
        x_, d_, b_, c_ = inp
        st = st * jnp.exp(d_ * a_gj)[..., None, None] + jnp.einsum('bgjp,bgn->bgjpn', x_ * d_[..., None], b_)
        return st, jnp.einsum('bgjpn,bgn->bgjp', st, c_)

    st0 = state0.astype(jnp.float32).reshape(db, N_GROUPS, HEADS_PER_GROUP, SSM_HEADDIM, D_STATE)
    final, ys = lax.scan(step, st0, (xt, dtt, bt, ct))
    y = jnp.moveaxis(ys, 0, 1).reshape(db, t, N_SSM_HEADS, SSM_HEADDIM)
    return y, final.reshape(db, N_SSM_HEADS, SSM_HEADDIM, D_STATE)

def _ssm_out(y, xs, d_skip, z, w_norm):
    lead = z.shape[:-1]
    y = y + d_skip.astype(jnp.float32)[:, None] * xs
    g = (y.reshape(*lead, D_INNER) * jax.nn.silu(z.astype(jnp.float32)))
    g = g.reshape(*lead, N_GROUPS, D_INNER // N_GROUPS)
    g = g * lax.rsqrt(jnp.mean(g * g, axis=-1, keepdims=True) + NORM_EPS)
    return (g.reshape(*lead, D_INNER) * w_norm.astype(jnp.float32)).astype(z.dtype)

def _channel_and_ple(h, mix, p_l, w_out, g_ffn, w_up, w_down, w_ple, w_ple_norm, w_ple_gate):
    h = h + mix @ w_out
    u = _rmsnorm(h, g_ffn)
    h = h + jnp.square(jax.nn.relu(u @ w_up)) @ w_down
    e = _rmsnorm(p_l @ w_ple, w_ple_norm) * jax.nn.sigmoid(h @ w_ple_gate)
    return h + e

def setup_inputs(seed: int = 0) -> dict:
    key = jax.random.key(seed)
    kit = iter(jax.random.split(key, 40))

    def nrm(shape, scale):
        return jax.random.normal(next(kit), shape, jnp.float32) * scale

    n_pages = PAST_LEN // PAGE_SIZE
    n_used = DEC_BATCH * n_pages
    n_pool = n_used + max(1, n_used // 4)
    perm = jax.random.permutation(next(kit), n_pool)
    page_table = perm[:n_used].reshape(DEC_BATCH, n_pages).astype(jnp.int32)
    dt0 = jnp.exp(jax.random.uniform(next(kit), (DEPTH, N_SSM_HEADS), jnp.float32,
                                     minval=math.log(1e-3), maxval=math.log(1e-1)))
    dt_bias = dt0 + jnp.log(-jnp.expm1(-dt0))
    a_log = jnp.log(jax.random.uniform(next(kit), (DEPTH, N_SSM_HEADS), jnp.float32, minval=1.0, maxval=16.0))
    return {
        "x_prompt": nrm((BATCH, SEQ, D_MODEL), 1.0),
        "x_sample": nrm((DEC_BATCH, DEC_SEQ, D_MODEL), 1.0),
        "p_prompt": nrm((DEPTH, BATCH, SEQ, PLE_DIM), 1.0),
        "p_sample": nrm((DEPTH, DEC_BATCH, DEC_SEQ, PLE_DIM), 1.0),
        "cache_k": nrm((DEPTH, n_pool, PAGE_SIZE, N_ATTN_HEADS, 2 * DK), 1.0),
        "cache_v": nrm((DEPTH, n_pool, PAGE_SIZE, N_ATTN_HEADS, DV), 1.0),
        "page_table": page_table,
        "state_ssm": nrm((DEPTH, DEC_BATCH, N_SSM_HEADS, SSM_HEADDIM, D_STATE), 0.5),
        "state_conv": nrm((DEPTH, DEC_BATCH, CONV_W - 1, CONV_DIM), 1.0),
        "g_mix": 1.0 + nrm((DEPTH, D_MODEL), 0.02),
        "w_in": nrm((DEPTH, D_MODEL, D_PROJ), D_MODEL ** -0.5),
        "lambda_q1": nrm((DEPTH, DK), 0.1),
        "lambda_k1": nrm((DEPTH, DK), 0.1),
        "lambda_q2": nrm((DEPTH, DK), 0.1),
        "lambda_k2": nrm((DEPTH, DK), 0.1),
        "w_subln": 1.0 + nrm((DEPTH, DV), 0.02),
        "conv_w": nrm((DEPTH, CONV_W, CONV_DIM), CONV_W ** -0.5),
        "conv_b": nrm((DEPTH, CONV_DIM), 0.01),
        "dt_bias": dt_bias,
        "a_log": a_log,
        "d_skip": 1.0 + nrm((DEPTH, N_SSM_HEADS), 0.01),
        "w_ssm_norm": 1.0 + nrm((DEPTH, D_INNER), 0.02),
        "w_out": nrm((DEPTH, MIX_WIDTH, D_MODEL), MIX_WIDTH ** -0.5),
        "g_ffn": 1.0 + nrm((DEPTH, D_MODEL), 0.02),
        "w_up": nrm((DEPTH, D_MODEL, D_FF), D_MODEL ** -0.5),
        "w_down": nrm((DEPTH, D_FF, D_MODEL), 0.5 * D_FF ** -0.5),
        "w_ple": nrm((DEPTH, PLE_DIM, D_MODEL), PLE_DIM ** -0.5),
        "w_ple_norm": 1.0 + nrm((DEPTH, D_MODEL), 0.02),
        "w_ple_gate": nrm((DEPTH, D_MODEL, D_MODEL), D_MODEL ** -0.5),
        "g_final": 1.0 + nrm((D_MODEL,), 0.02),
    }

def reference(x_prompt, x_sample, p_prompt, p_sample, cache_k, cache_v, page_table, state_ssm, state_conv,
              g_mix, w_in, lambda_q1, lambda_k1, lambda_q2, lambda_k2, w_subln, conv_w, conv_b, dt_bias, a_log,
              d_skip, w_ssm_norm, w_out, g_ffn, w_up, w_down, w_ple, w_ple_norm, w_ple_gate, g_final):
    db = x_sample.shape[0]
    past = page_table.shape[1] * cache_k.shape[2]
    hp, hs = x_prompt, x_sample
    kp_l, vp_l, sp_l, cp_l, ks_l, vs_l, ss_l, cs_l = [], [], [], [], [], [], [], []
    for i in range(DEPTH):
        lam_init = 0.8 - 0.6 * math.exp(-0.3 * i)
        lam = (jnp.exp(jnp.sum(lambda_q1[i].astype(jnp.float32) * lambda_k1[i].astype(jnp.float32)))
               - jnp.exp(jnp.sum(lambda_q2[i].astype(jnp.float32) * lambda_k2[i].astype(jnp.float32)))
               + lam_init)

        u = _rmsnorm(hp, g_mix[i])
        q, k, v, z, xbc, dt = _split_proj(u, w_in[i])
        o_attn = _attn_out(_prompt_diff_attn(q, k, v, lam), w_subln[i], lam_init)
        xpad = jnp.pad(xbc, ((0, 0), (CONV_W - 1, 0), (0, 0)))
        xs, bm, cm, dtv, a = _ssm_inputs(_causal_conv(xpad, conv_w[i], conv_b[i]), dt, dt_bias[i], a_log[i])
        y, st = _ssd_chunked(xs, dtv, a, bm, cm)
        o_ssm = _ssm_out(y, xs, d_skip[i], z, w_ssm_norm[i])
        mix = jnp.concatenate([o_attn, o_ssm.astype(o_attn.dtype)], axis=-1)
        hp = _channel_and_ple(hp, mix, p_prompt[i], w_out[i], g_ffn[i], w_up[i], w_down[i],
                              w_ple[i], w_ple_norm[i], w_ple_gate[i])
        kp_l.append(k.reshape(*k.shape[:-2], 2 * DK))
        vp_l.append(v)
        sp_l.append(st)
        cp_l.append(xpad[:, -(CONV_W - 1):])

        u = _rmsnorm(hs, g_mix[i])
        q, k, v, z, xbc, dt = _split_proj(u, w_in[i])
        k_past = cache_k[i][page_table].reshape(db, past, N_ATTN_HEADS, 2, DK)
        v_past = cache_v[i][page_table].reshape(db, past, N_ATTN_HEADS, DV)
        o_attn = _attn_out(_sample_diff_attn(q, k, v, k_past, v_past, lam), w_subln[i], lam_init)
        xcat = jnp.concatenate([state_conv[i].astype(xbc.dtype), xbc], axis=1)
        xs, bm, cm, dtv, a = _ssm_inputs(_causal_conv(xcat, conv_w[i], conv_b[i]), dt, dt_bias[i], a_log[i])
        y, st = _ssm_recurrent(xs, dtv, a, bm, cm, state_ssm[i])
        o_ssm = _ssm_out(y, xs, d_skip[i], z, w_ssm_norm[i])
        mix = jnp.concatenate([o_attn, o_ssm.astype(o_attn.dtype)], axis=-1)
        hs = _channel_and_ple(hs, mix, p_sample[i], w_out[i], g_ffn[i], w_up[i], w_down[i],
                              w_ple[i], w_ple_norm[i], w_ple_gate[i])
        ks_l.append(k.reshape(*k.shape[:-2], 2 * DK))
        vs_l.append(v)
        ss_l.append(st)
        cs_l.append(xcat[:, -(CONV_W - 1):])

    y_prompt = _rmsnorm(hp, g_final)
    y_sample = _rmsnorm(hs, g_final)
    k_prompt = jnp.stack(kp_l)
    v_prompt = jnp.stack(vp_l)
    ssm_prompt = jnp.stack(sp_l)
    conv_prompt = jnp.stack(cp_l)
    k_sample = jnp.stack(ks_l)
    v_sample = jnp.stack(vs_l)
    ssm_sample = jnp.stack(ss_l)
    conv_sample = jnp.stack(cs_l)
    return (y_prompt, y_sample, k_prompt, v_prompt, ssm_prompt, conv_prompt, k_sample, v_sample, ssm_sample, conv_sample)


_drawn_inputs = setup_inputs


def setup_inputs(seed=0):
    import zlib

    import numpy as np

    out = dict(_drawn_inputs(seed))
    spreads = {}
    factors = {'lambda_k1': 3.791,
     'lambda_k2': 3.411,
     'w_subln': 23.078,
     'conv_b': 3.754,
     'd_skip': 64.0,
     'w_ssm_norm': 17.459,
     'g_ffn': 6.354,
     'w_ple_norm': 62.536,
     'g_final': 8.095}
    for name, (base, spread) in spreads.items():
        noise = np.random.default_rng([zlib.crc32(name.encode()), seed]).standard_normal(out[name].shape)
        drawn = base * np.exp(spread * noise) if base else spread * noise
        out[name] = __import__('jax').numpy.asarray(drawn.astype(out[name].dtype))
    for name, factor in factors.items():
        out[name] = (out[name] * factor).astype(out[name].dtype)
    return out
```

```python
from contextlib import ExitStack

import concourse.bass as bass
from concourse import mybir

F32 = mybir.dt.float32
F32R = mybir.dt.float32r
I32 = mybir.dt.int32
ALU = mybir.AluOpType
ACT = mybir.ActivationFunctionType
AX = mybir.AxisListType.X

P = 128
D_MODEL = 2048
KT = D_MODEL // P
SEQ = 512
NB = 8
T = SEQ + NB
HALF = T // 2
QB = SEQ // P
PAST = 2048
PAGES = PAST // P
POOL = NB * PAGES + NB * PAGES // 4
AW = 1024
NH = 8
DK = 64
SCALE = DK ** -0.5
SLOPES = [2.0 ** -(h + 1) for h in range(NH)]
LAM_INIT = 0.2
NSH = 16
HD = 64
NS = 128
CONV_DIM = 1536
CW = 4
CT = CONV_DIM // P
D_PROJ = 3 * AW + 1024 + CONV_DIM + NSH
D_FF = 4 * D_MODEL
CHUNKS = D_FF // 512
PLE = 256
EPS = 1e-6
EPS_SUB = 1e-5
NEG = -1.0e30
LOW = -3.0e38

TQ, TK, TV, TX = 0, 8, 16, 24
TB_, TC_ = 8, 10
CX = TX
TZ = 16
TY = 8
JOBS = CT + 8
PT = 36

SL_DT = 4 * 22
SL_OUT = SL_DT + 2
SL_MLP = SL_OUT + 32
SL_PLE = SL_MLP + 16 * CHUNKS
SL_GATE = SL_PLE + 8
SL_ALL = SL_GATE + 32
G_DT = 22
G_OUT = 23
G_MLP = G_OUT + 8
G_PLE = G_MLP + 10 * CHUNKS
G_GATE = G_PLE + 8


def at(c, k, i):
    return c if i is None else i * k + c


class Chain:

    def __init__(self, eng, sem):
        self.eng, self.sem, self.n = eng, sem, 0

    def __call__(self, ins):
        ins.then_inc(self.sem, 1)
        self.n = self.n + 1
        self.eng.wait_ge(self.sem, self.n)


def build(nc, d, d_out):
    ctx = ExitStack()
    with ctx:
        base = (nc.sbuf_base + 31) // 32 * 32
        sizes = [("RAW", 8192), ("WH", 8192), ("WL", 8192), ("UH", 33280), ("UL", 33280),
                 ("PJ", PT * T * 4), ("XX", 37504), ("CC", 9216)]
        off, pos = {}, base
        for name, n in sizes:
            off[name] = pos
            pos += n

        def sb(name, shape, dt, where, delta=0):
            return nc.alloc_sbuf_tensor_at(name, [P] + shape, dt, offset=off[where] + delta)[:]

        raw = sb("raw", [2, 1024], F32, "RAW")
        wh = sb("wh", [2, 1024], F32R, "WH")
        wl = sb("wl", [2, 1024], F32R, "WL")
        uh = sb("uh", [KT, T], F32R, "UH")
        ul = sb("ul", [KT, T], F32R, "UL")
        pj = sb("pj", [PT, T], F32, "PJ")
        cpos = [0]

        def const(name, shape, dt=F32):
            n = 4
            for s in shape:
                n *= s
            t = sb(name, shape, dt, "CC", cpos[0])
            cpos[0] += (n + 31) // 32 * 32
            assert cpos[0] <= 9216, cpos
            return t

        ident = const("ident", [P])
        ones = const("ones", [P])
        causal = const("causal", [P])
        rstd = const("rstd", [T])
        gcol = const("gcol", [85])
        cwcol = const("cwcol", [CW * CT])
        cst = const("cst", [CT, NB * 3])
        dtt = const("dtt", [T])
        lamc = const("lamc", [4, DK])
        lams = const("lams", [8])
        epsc = const("epsc", [2])
        ssx = const("ssx", [8])
        hcol = const("hcol", [4])
        rowm = const("rowm", [NB])
        nmx = const("nmx", [3, 2])
        sums = const("sums", [3, 2])
        ptab = const("ptab", [NB * PAGES], I32)
        rsum = const("rsum", [3, 2])
        xt = sb("xt", [QB, D_MODEL], F32, "PJ")
        xs = sb("xs", [D_MODEL], F32, "PJ", 32768)
        junk = sb("junk", [D_MODEL], F32, "XX")
        rdiag = sb("rdiag", [QB, P], F32, "XX", 8192)
        grow = sb("grow", [P], F32, "XX", 16384)
        cwrow = sb("cwrow", [P], F32, "XX", 16896)
        cstrow = sb("cstrow", [CONV_DIM], F32, "XX", 17408)
        kpage = sb("kpage", [4, AW], F32, "XX")
        sc = sb("sc", [NB, PAGES + 1, 16], F32, "XX", 16384)
        qbc = sb("qbc", [2, AW], F32, "XX", 25088)
        zst = sb("zst", [2, T], F32, "XX", 33280)
        qtok1 = sb("qtok1", [AW], F32, "XX", 33280)
        xsg = sb("xsg", [KT, NB], F32, "XX", 24576)
        vpage = sb("vpage", [4, AW], F32, "XX")
        se = sb("se", [3, 2, SEQ], F32, "XX", 25088)
        ktok = sb("ktok", [QB, AW], F32, "UH")
        wt = sb("wt", [2, QB, SEQ], F32, "UH")
        vtok = sb("vtok", [QB, AW], F32, "UH", 16384)
        qtok = sb("qtok", [AW], F32, "UH", 32768)
        kstok = sb("kstok", [AW], F32, "UH", 36864)
        vstok = sb("vstok", [AW], F32, "UH", 40960)
        xbtok = sb("xbtok", [CONV_DIM], F32, "UH", 45056)
        dist = sb("dist", [896], F32, "UH", 51200)
        alibi = sb("alibi", [896], F32, "UH", 54784)
        wd = sb("wd", [NB, PAGES + 1, NH], F32, "UH", 58368)
        dbias = sb("dbias", [PAGES, 16], F32, "UH", 62720)
        dmx = sb("dmx", [P], F32, "UH", 63744)
        ddiag = sb("ddiag", [P], F32, "UH", 64256)
        drc = sb("drc", [P], F32, "UH", 64768)
        ddist = sb("ddist", [PAGES], F32, "UH", 65280)
        dm1 = sb("dm1", [1], F32, "UH", 65344)
        sn = sb("sn", [16], F32, "UH", 65376)
        bcb = sb("bcb", [4, NB, NS], F32, "XX")
        stt = sb("stt", [2, NB, NS], F32, "XX", 16384)
        bx = sb("bx", [NB, NS], F32, "XX", 24576)
        tmp = sb("tmp", [2, T], F32, "XX", 28672)
        acs = sb("acs", [SEQ], F32, "XX", 32832)
        mpos = [34880]

        def misc(name, shape):
            n = 4
            for s in shape:
                n *= s
            t = sb(name, shape, F32, "XX", mpos[0])
            mpos[0] += (n + 31) // 32 * 32
            assert mpos[0] <= 37376
            return t

        dtk = misc("dtk", [QB, NSH])
        ack = misc("ack", [QB, NSH])
        dsk = misc("dsk", [QB, NSH])
        decb = misc("decb", [NSH, QB])
        ecol = misc("ecol", [8, 17])
        ecat = misc("ecat", [17])
        xdt = misc("xdt", [8, NB])
        ysd = misc("ysd", [8, NB])
        bcrow = sb("bcrow", [4, NS], F32, "XX", 24576)
        xd = sb("xd", [QB, AW], F32, "UH")
        xdd = sb("xdd", [QB, AW], F32, "UH", 16384)
        sall = sb("sall", [QB, AW], F32, "UH", 32768)
        btok = sb("btok", [QB, 2, NS], F32, "UH", 49152)
        cbt = sb("cbt", [2, QB, P], F32, "UH", 53248)
        dl = sb("dl", [2, QB, P], F32, "UH", 57344)
        cd = sb("cd", [2, QB, P], F32, "UH", 61440)
        fst = sb("fst", [8, NS], F32, "UH", 49152)
        zpad = sb("zpad", [2, 4, 120], F32, "XX", 16384)
        wnew = sb("wnew", [64], F32, "XX", 22272)
        oacc = sb("oacc", [AW], F32, "XX", 16384)
        yb = sb("yb", [3, T], F32, "UH", 32768)
        eb = sb("eb", [2, T], F32, "UH", 39008)
        sp5 = [sb(f"sp{i}", [T], F32, "UH", 16384 + 2080 * i) for i in range(5)]
        cs4 = sb("cs4", [CT, NB, 3], F32, "UH", 43168)
        csr = sb("csr", [CT, NB], F32, "UH", 44320)
        hT = pj[:, 0:KT, :]
        eT = pj[:, KT:2 * KT, :]
        xt3 = sb("xt3", [QB, D_MODEL], F32, "PJ", KT * T * 4)
        xs3 = sb("xs3", [D_MODEL], F32, "PJ", 2 * KT * T * 4)
        yt = sb("yt", [QB, D_MODEL], F32, "PJ", KT * T * 4)
        ys = sb("ys", [D_MODEL], F32, "PJ", 2 * KT * T * 4)
        hh = sb("hh", [2, 4, T], F32R, "PJ", KT * T * 4)
        hl = sb("hl", [2, 4, T], F32R, "PJ", (KT + 8) * T * 4)
        sq = sb("sq", [2, T], F32, "XX")
        tm = sb("tm", [2, T], F32, "XX", 4160)
        acc = sb("acc", [T], F32, "XX", 8320)
        ph = sb("ph", [2, T], F32R, "XX", 10400)
        pl = sb("pl", [2, T], F32R, "XX", 14560)
        ptok = sb("ptok", [QB, PLE], F32, "XX", 18720)
        pstok = sb("pstok", [PLE], F32, "XX", 22816)
        ps = ctx.enter_context(nc.psum_tensor("ps", [P, 8, 512], F32))

        G_MIX, G_FFN, G_PLN, G_FIN, G_SSM, G_SUB, G_CB = 0, 16, 32, 48, 64, 72, 73

        q_scr = nc.dram_tensor("q_scr", (NB, AW), F32, kind="Internal").ap()
        z_scr = nc.dram_tensor("z_scr", (8, P, T), F32, kind="Internal").ap()
        bc_scr = nc.dram_tensor("bc_scr", (NB, 4, NS), F32, kind="Internal").ap()

        names = {}

        def sem(name):
            names[name] = ctx.enter_context(nc.semaphore(name))
            return names[name]

        raw_landed = [sem("raw_landed0"), sem("raw_landed1")]
        hi_ready, lo_ready, w_used = sem("hi_ready"), sem("lo_ready"), sem("w_used")
        group_free = sem("group_free")
        dve_step, act_step, pool_step = sem("dve_step"), sem("act_step"), sem("pool_step")
        s_x = sem("x_landed")
        s_xs, s_small = sem("xs_landed"), sem("small_landed")
        s_const, s_gt, s_gc = sem("consts_ready"), sem("gain_turned"), sem("gain_copied")
        s_ss, s_rt = sem("squares_summed"), sem("rstd_by_token")
        s_rb, s_rd = sem("rstd_spread"), sem("rstd_copied")
        s_xT, s_uh, s_ul = sem("x_turned"), sem("u_hi"), sem("u_lo")
        s_xsT, s_us = sem("xs_turned"), sem("us_done")
        s_qt, s_qtc, s_qscr, s_qbc = sem("q_turned"), sem("q_rows"), sem("q_stored"), sem("q_spread")
        s_pt = sem("page_table_landed")
        s_kp = [sem(f"k_landed{i}") for i in range(4)]
        s_km, s_kr = sem("k_multiplied"), sem("k_reduced")
        s_zst, s_zout = sem("z_staged"), sem("z_stored")
        s_dtf = sem("dt_projected")
        s_kt, s_vt, s_kto, s_vto = sem("k_turned"), sem("v_turned"), sem("k_rows"), sem("v_rows")
        s_rt3 = sem("rows_turned")
        s_kso, s_vso = sem("ks_rows"), sem("vs_xb_rows")
        s_out = sem("outputs_stored")
        s_kst_out = sem("k_prompt_stored")
        s_qre = sem("q_reloaded")
        s_dc = sem("dist_ready")
        s_dv, s_dp, s_dex = sem("dec_vector_steps"), sem("dec_tensor_steps"), sem("dec_exp")
        s_vp = [sem(f"v_landed{i}") for i in range(4)]
        s_vu, s_wz = sem("v_used"), sem("page_weights_placed")
        s_nv = sem("new_values_added")
        s_dos, s_dor = sem("dec_out_selected"), sem("dec_out_copied")
        s_lam, s_lame = sem("lam_products"), sem("lam_exp")
        a_s, a_b, a_nm, a_e = sem("scores"), sem("biased"), sem("neg_max"), sem("exp_done")
        a_rs, a_e1, a_w, a_t = sem("inv_sum"), sem("second_scaled"), sem("weights"), sem("w_turned")
        a_wt, a_o, a_oc = sem("w_turned_copied"), sem("attn_out"), sem("attn_out_copied")
        c_dv, c_de = sem("conv_dec_sum"), sem("conv_dec_exp")
        c_i, c_v, c_e, c_p, c_m = (sem("conv_first"), sem("conv_sum"), sem("conv_exp"),
                                  sem("conv_plus"), sem("conv_act"))
        d_v, d_s = sem("dt_vector_steps"), sem("dt_scalar_steps")
        e_t, e_c, e_dx = sem("turned_steps"), sem("copied_steps"), sem("decay_exp_states")
        e_xt, e_xd, e_xdd = sem("x_rows_turned"), sem("x_rows"), sem("x_rows_decayed")
        e_bc, e_cb, e_cbc = sem("b_rows"), sem("cb_product"), sem("cb_copied")
        e_st, e_sm, e_sc = sem("states"), sem("state_decayed"), sem("state_ready")
        f_a, f_d, f_e, f_c = sem("acs_spread"), sem("seg"), sem("seg_exp"), sem("acs_exp")
        f_m, f_cm, f_y, f_yc = sem("mask_product"), sem("c_decayed"), sem("y_product"), sem("y_ready")
        f_ft, f_fc = sem("final_turned"), sem("final_copied")
        g_bc, g_bs, g_bb = sem("bc_rows"), sem("bc_stored"), sem("bc_spread")
        g_xd = sem("x_dt")
        g_in = [sem("st_landed0"), sem("st_landed1")]
        g_a, g_b, g_n, g_c, g_r = (sem("st_decayed"), sem("b_times_x"), sem("st_new"), sem("st_times_c"),
                                  sem("st_reduced"))
        g_out = [sem("st_stored0"), sem("st_stored1")]
        z_in, g_y, z_y = sem("z_landed"), sem("dec_y_ready"), sem("gated")
        z_q, z_s, z_rt, z_o, z_h, z_l = (sem("gated_sq"), sem("gated_sum"), sem("gated_rms"),
                                        sem("gated_norm"), sem("mix_hi"), sem("mix_lo"))
        h_x, h_p, h_pt, h_pc = sem("x3_landed"), sem("p_landed"), sem("p_turned"), sem("p_hi")
        h_pl = sem("p_lo")
        h_e, h_q, h_a = sem("h_ready"), sem("sq_ready"), sem("sq_added")
        h_s, h_rt, h_r = sem("norm_sum"), sem("norm_root"), sem("norm_ready")
        m_t, m_q, m_l = sem("relu_scaled"), sem("hidden_hi"), sem("hidden_lo")
        p_e = sem("e_ready")
        x_c = sem("gate_clamped")
        x_e, x_p, x_r, x_m, x_h = (sem("gate_exp"), sem("gate_plus"), sem("gate_recip"),
                                  sem("gate_times_e"), sem("h_final"))
        y_s, y_t, y_c = sem("y_scaled"), sem("y_turned"), sem("y_copied_act")
        y_d = sem("y_copied_dve")
        y_out = sem("y_stored")

        block = ctx.enter_context(nc.Block())

        def wcols(w, row, col, rows=512, cols=256):
            return w[bass.ds(row, rows), bass.ds(col, cols)].rearrange("(k p) n -> p k n", p=P)

        w_in, w_out, w_up, w_down = d["w_in"][0], d["w_out"][0], d["w_up"][0], d["w_down"][0]
        w_ple, w_gate = d["w_ple"][0], d["w_ple_gate"][0]
        halves = lambda ap: ap.rearrange("p (h n) -> p h n", h=2)
        GB = [0, 4]

        def bank_view(g, m):
            b = GB[g % 2] + 2 * m
            return ps[:, b:b + 2, 0:HALF]

        def group_view(g):
            b = GB[g % 2]
            return ps[:, b:b + 4, 0:HALF].rearrange("p (m h) n -> p m h n", h=2)

        @block.sync
        def _(sp):
            for q in range(QB):
                sp.dma_start(xt[:, q, :], d["x_prompt"][0, q * P:(q + 1) * P, :]).then_inc(s_x, 16)
            sp.dma_start(xs[0:NB, :], d["x_sample"][:, 0, :]).then_inc(s_xs, 16)

            def load(src, c, per=0, i=None, elems=1024, k=4):
                sp.wait_ge(lo_ready, at(c + 1, per, i))
                dst = raw[:, c % 2, 0:elems].rearrange("p (k n) -> p k n", k=k)
                sp.dma_start(dst, src).then_inc(raw_landed[c % 2], 16)

            def load_in(c, i=None, per=8):
                g, k = c // 4, c % 4
                load(wcols(w_in, 512 * k, at(256 * g, 64 * per, i)), c, per, i)

            def pages(c, i):
                for pg in range(2 * c, 2 * c + 2):
                    idx = sp.value_load(ptab[0:1, bass.ds(at(pg, 32, i), 1)], min_val=0, max_val=POOL - 1)
                    sp.wait_ge(s_kr, at(pg + 1, 32, i))
                    sp.dma_start(kpage[:, pg % 4, :], d["cache_k"][0][bass.ds(idx, 1)]
                                 .rearrange("o t h d -> (o t) (h d)")).then_inc(s_kp[pg % 4], 16)

            def spread_q(b, i):
                if b:
                    sp.wait_ge(s_km, at(16 * (b - 1) + 1, 32, i))
                sp.dma_start(qbc[:, b % 2], q_scr[bass.ds(at(b, 2, i), 1), :].to_broadcast([P, AW]))\
                    .then_inc(s_qbc, 16)

            sp.dma_start(ptab[0:1, :], d["page_table"].rearrange("b g -> (b g)").unsqueeze(0)).then_inc(s_pt, 16)
            for c in range(4):
                load_in(c)
            sp.wait_ge(s_pt, 16)
            with sp.Fori(0, 2) as i:
                for j in range(8):
                    load_in(4 + j, i)
            sp.wait_ge(s_qscr, 16)
            spread_q(0, None)
            pages(0, None)
            with sp.Fori(0, 3) as i:
                for j in range(16):
                    if j % 8 == 4:
                        spread_q(j // 8 + 1, i)
                    pages(j + 1, i)
                    load_in(20 + j, i, 16)
            for j in range(48, 64):
                if j == 52:
                    spread_q(7, None)
                if j < 63:
                    pages(j + 1, None)
                load_in(20 + j)
            for c in range(84, SL_DT):
                load_in(c)
            for c in range(2):
                sp.wait_ge(lo_ready, SL_DT + c + 1)
                sp.dma_start(raw[:, c % 2, :].rearrange("p (k n) -> p k n", k=8)[:, :, 0:NSH],
                             wcols(w_in, 1024 * c, D_PROJ - NSH, 1024, NSH)).then_inc(raw_landed[c % 2], 16)

            def load_out(c, i=None):
                g, k = (c - SL_OUT) // 4, (c - SL_OUT) % 4
                load(wcols(w_out, 512 * k, at(256 * g, 256, i)), c, 4, i)

            for c in range(SL_OUT, SL_OUT + 2):
                load_out(c)
            sp.wait_ge(w_used, SL_OUT + 2)
            sp.dma_start(qtok[0:NB, :], q_scr).then_inc(s_qre, 16)
            sp.wait_ge(s_kto, NH)
            sp.dma_start(d_out["k_prompt"][0, 0].rearrange("(q p) h d -> p q (h d)", p=P), ktok)\
                .then_inc(s_kst_out, 16)
            sp.wait_ge(s_vto, NH)
            sp.dma_start(d_out["v_prompt"][0, 0].rearrange("(q p) h d -> p q (h d)", p=P), vtok)\
                .then_inc(s_out, 16)
            sp.wait_ge(s_kso, 1)
            sp.dma_start(d_out["k_sample"][0, :, 0].rearrange("b h d -> b (h d)"), kstok[0:NB, :])\
                .then_inc(s_out, 16)
            sp.wait_ge(s_vso, 1)
            sp.dma_start(d_out["v_sample"][0, :, 0].rearrange("b h d -> b (h d)"), vstok[0:NB, :])\
                .then_inc(s_out, 16)
            sp.wait_ge(s_vso, 2)
            sp.dma_start(d_out["conv_prompt"][0, 0], xbtok[0:3, :]).then_inc(s_out, 16)
            sp.dma_start(d_out["conv_sample"][0, :, 2], xbtok[3:11, :]).then_inc(s_out, 16)
            sp.dma_start(d_out["conv_sample"][0, :, 0:2], d["state_conv"][0, :, 1:3]).then_inc(s_out, 16)
            sp.wait_ge(s_zout, 16 * 5)
            sp.dma_start(pj[:, TZ:TZ + 8, :], z_scr.rearrange("t p n -> p t n")).then_inc(z_in, 16)
            sp.wait_ge(s_kr, 4 + NB * PAGES)
            with sp.Fori(0, NB) as i:
                for pg in range(PAGES):
                    idx = sp.value_load(ptab[0:1, bass.ds(at(pg, PAGES, i), 1)], min_val=0, max_val=POOL - 1)
                    sp.wait_ge(s_vu, at(pg + 1, PAGES, i))
                    sp.dma_start(vpage[:, pg % 4, :], d["cache_v"][0][bass.ds(idx, 1)]
                                 .rearrange("o t h d -> (o t) (h d)")).then_inc(s_vp[pg % 4], 16)
            src = d["state_ssm"][0].rearrange("b h p n -> (h p) b n")
            dst = d_out["ssm_sample"][0].rearrange("b h p n -> (h p) b n")
            sp.wait_ge(s_dor, 2)
            for t in range(2):
                sp.dma_start(stt[:, t], src[t * P:(t + 1) * P]).then_inc(g_in[t], 16)
            for c in range(SL_OUT + 2, SL_OUT + 4):
                load_out(c)
            for t in range(8):
                sp.wait_ge(g_n, t + 1)
                sp.dma_start(dst[t * P:(t + 1) * P], stt[:, t % 2]).then_inc(g_out[t % 2], 16)
                if t < 6:
                    sp.wait_ge(g_c, t + 1)
                    sp.wait_ge(g_out[t % 2], 16 * (t // 2 + 1))
                    sp.dma_start(stt[:, t % 2], src[(t + 2) * P:(t + 3) * P]).then_inc(g_in[t % 2], 16)
            sp.wait_ge(f_fc, 1)
            sp.dma_start(d_out["ssm_prompt"][0, 0].rearrange("(t h) p n -> (h p) t n", h=2), fst)\
                .then_inc(s_out, 16)
            sp.wait_ge(g_r, 8)
            sp.wait_ge(g_out[0], 16 * 4)
            sp.wait_ge(g_out[1], 16 * 4)
            sp.dma_start(ptok, d["p_prompt"][0, 0].rearrange("(q p) n -> p q n", p=P)).then_inc(h_p, 16)
            sp.dma_start(pstok[0:NB, :], d["p_sample"][0, :, 0]).then_inc(h_p, 16)
            sp.wait_ge(z_s, NH + 2)
            sp.wait_ge(f_yc, 8)
            sp.wait_ge(g_y, 1)
            for q in range(QB):
                sp.dma_start(xt3[:, q, :], d["x_prompt"][0, q * P:(q + 1) * P, :]).then_inc(h_x, 16)
            sp.dma_start(xs3[0:NB, :], d["x_sample"][:, 0, :]).then_inc(h_x, 16)
            with sp.Fori(0, 7) as i:
                for j in range(4):
                    load_out(SL_OUT + 4 + j, i)

            def load_up(n, chunk, per_c, per_n, i):
                for j in range(8):
                    g, k = j // 4, j % 4
                    load(wcols(w_up, 512 * k, at(512 * chunk + 256 * g, 512 * per_c, i)), n + j, per_n, i)

            def load_down(n, chunk, per_c, per_n, i):
                for j in range(8):
                    load(wcols(w_down, at(512 * chunk, 512 * per_c, i), 256 * j), n + j, per_n, i)

            load_up(SL_MLP, 0, 0, 0, None)
            with sp.Fori(0, (CHUNKS - 2) // 2) as i:
                load_up(SL_MLP + 8, 1, 2, 32, i)
                load_down(SL_MLP + 16, 0, 2, 32, i)
                load_up(SL_MLP + 24, 2, 2, 32, i)
                load_down(SL_MLP + 32, 1, 2, 32, i)
            n = SL_PLE - 24
            load_up(n, CHUNKS - 1, 0, 0, None)
            load_down(n + 8, CHUNKS - 2, 0, 0, None)
            load_down(n + 16, CHUNKS - 1, 0, 0, None)
            for g in range(8):
                load(wcols(w_ple, 0, 256 * g, 256), SL_PLE + g, elems=512, k=2)
            with sp.Fori(0, 8) as i:
                for j in range(4):
                    load(wcols(w_gate, 512 * j, at(0, 256, i)), SL_GATE + j, 4, i)
            for q in range(QB):
                sp.wait_ge(y_c, 2 * (q + 1))
                sp.wait_ge(y_d, 2 * (q + 1))
                sp.dma_start(d_out["y_prompt"][0, q * P:(q + 1) * P, :], yt[:, q, :]).then_inc(y_out, 16)
            sp.wait_ge(y_c, 2 * QB + 2)
            sp.wait_ge(y_d, 2 * QB + 2)
            sp.dma_start(d_out["y_sample"][:, 0, :], ys[0:NB, :]).then_inc(y_out, 16)
            sp.wait_ge(y_out, 16 * (QB + 1))
            sp.wait_ge(s_out, 16 * 7)
            sp.wait_ge(s_kst_out, 16)

        @block.scalar
        def _(act):
            A = act.activation
            chain = Chain(act, act_step)
            act.sem_inc(s_zout, 16)
            vec = lambda name: d[name][0].rearrange("(t p) -> t p", p=P)
            act.dma_start(grow[G_MIX:G_MIX + 16], vec("g_mix")).then_inc(s_small, 16)
            act.dma_start(grow[G_FFN:G_FFN + 16], vec("g_ffn")).then_inc(s_small, 16)
            act.dma_start(grow[G_PLN:G_PLN + 16], vec("w_ple_norm")).then_inc(s_small, 16)
            act.dma_start(grow[G_FIN:G_FIN + 16], d["g_final"].rearrange("(t p) -> t p", p=P))\
                .then_inc(s_small, 16)
            act.dma_start(grow[G_SSM:G_SSM + 8], vec("w_ssm_norm")).then_inc(s_small, 16)
            act.dma_start(grow[G_SUB:G_SUB + 1], vec("w_subln")).then_inc(s_small, 16)
            act.dma_start(grow[G_CB:G_CB + CT], vec("conv_b")).then_inc(s_small, 16)
            act.dma_start(cwrow[0:CW * CT], d["conv_w"][0].rearrange("j (t p) -> (j t) p", p=P))\
                .then_inc(s_small, 16)
            act.dma_start(cstrow[0:NB * 3], d["state_conv"][0].rearrange("b j n -> (b j) n"))\
                .then_inc(s_small, 16)
            for n, name in enumerate(("dt_bias", "a_log", "d_skip")):
                act.dma_start(hcol[0:NSH, (0, 1, 3)[n]:(0, 1, 3)[n] + 1],
                              d[name][0].rearrange("(h o) -> h o", o=1)).then_inc(s_small, 16)
            for n, name in enumerate(("lambda_q1", "lambda_k1", "lambda_q2", "lambda_k2")):
                act.dma_start(lamc[:, n, :], d[name][0:1, :].to_broadcast([P, DK])).then_inc(s_small, 16)

            def hi(c, per=0, i=None):
                act.wait_ge(raw_landed[c % 2], at(16 * (c // 2 + 1), 8 * per, i))
                act.wait_ge(w_used, at(c + 1, per, i))
                A(wh[:, c % 2], raw[:, c % 2], ACT.Copy).then_inc(hi_ready, 1)

            act.wait_ge(s_x, 16 * QB)
            for q in range(QB):
                chain(A(junk, xt[:, q, :], ACT.Square, accum_out=ssx[:, q:q + 1]))
            act.wait_ge(s_xs, 16)
            chain(A(junk[0:NB], xs[0:NB, :], ACT.Square, accum_out=ssx[0:NB, 4:5]))
            act.wait_ge(s_const, 4)
            A(ssx[:, 0:4], ssx[:, 0:4], ACT.Sqrt, bias=epsc[:, 0:1], scale=1.0 / D_MODEL).then_inc(s_ss, 1)
            A(ssx[0:NB, 4:5], ssx[0:NB, 4:5], ACT.Sqrt, bias=epsc[0:NB, 0:1], scale=1.0 / D_MODEL)\
                .then_inc(s_ss, 1)
            act.wait_ge(s_gc, 2)
            for k in range(KT):
                act.wait_ge(s_xT, k + 1)
                A(uh[:, k, 0:SEQ], ps[:, k % 4, :], ACT.Copy, scale=gcol[:, G_MIX + k:G_MIX + k + 1])\
                    .then_inc(s_uh, 1)
                if k == 1:
                    hi(0)
                if k == 3:
                    hi(1)
            def hi8(c, i):
                for j in range(8):
                    hi(c + j, 8, i)

            with act.Fori(0, 2) as i:
                hi8(2, i)
            act.wait_ge(s_qt, 1)
            A(qtok1[0:NB, :].rearrange("p (b n) -> p b n", b=2), ps[0:NB, 0:2, :], ACT.Copy)\
                .then_inc(s_qtc, 1)
            act.wait_ge(s_qtc, 1)
            act.dma_start(q_scr, qtok1[0:NB, :]).then_inc(s_qscr, 16)
            with act.Fori(0, 4) as i:
                hi8(18, i)
            with act.Fori(0, 2) as i:
                for m in range(2):
                    for j in range(4):
                        hi(50 + 4 * m + j, 8, i)
                    act.wait_ge(s_zst, at(m + 1, 2, i))
                    act.dma_start(z_scr[bass.ds(at(2 * m, 4, i), 2)].rearrange("t p n -> p t n"), zst)\
                        .then_inc(s_zout, 16)
            with act.Fori(0, 3) as i:
                hi8(66, i)
            hi(SL_OUT)
            hi(SL_OUT + 1)
            for t in range(NH):
                act.wait_ge(s_kt, t + 1)
                A(ktok[:, :, t * P:(t + 1) * P], ps[:, 2 * t % 4, :].rearrange("p (q n) -> p q n", q=QB),
                  ACT.Copy).then_inc(s_kto, 1)
            act.wait_ge(s_rt3, 1)
            A(kstok[0:NB, :].rearrange("p (b n) -> p b n", b=2), ps[0:NB, 4:6, :], ACT.Copy)\
                .then_inc(s_kso, 1)
            act.wait_ge(s_lam, 2)
            A(lams[:, 0:2], lams[:, 0:2], ACT.Exp).then_inc(s_lame, 1)
            act.wait_ge(s_dv, 3)
            A(sc, sc, ACT.Exp, scale=SCALE).then_inc(s_dex, 1)
            UN = NH * QB

            def a_exp(u):
                n = (u % QB + 1) * P
                act.wait_ge(a_nm, u + 1)
                for c in range(2):
                    A(se[:, u % 3, c, 0:n], se[:, u % 3, c, 0:n], ACT.Exp, bias=nmx[:, u % 3, c:c + 1],
                      scale=SCALE, accum_out=sums[:, u % 3, c:c + 1]).then_inc(a_e, 1)

            def a_second(u):
                n = (u % QB + 1) * P
                act.wait_ge(a_rs, u + 1)
                A(se[:, u % 3, 1, 0:n], se[:, u % 3, 1, 0:n], ACT.Copy, scale=rsum[:, u % 3, 1:2])\
                    .then_inc(a_e1, 1)

            def a_wcopy(u):
                h, q = u // QB, u % QB
                act.wait_ge(a_t, u + 1)
                if h >= 2:
                    act.wait_ge(a_o, h - 1)
                else:
                    act.wait_ge(s_kst_out, 16)
                A(wt[:, h % 2, 0:q + 1, q * P:(q + 1) * P],
                  ps[:, 3 + u % 2, 0:(q + 1) * P].rearrange("p (k n) -> p k n", n=P), ACT.Copy)\
                    .then_inc(a_wt, 1)

            def a_out(h):
                act.wait_ge(a_o, h + 1)
                A(pj[:, TQ + h, 0:SEQ], ps[:, 5, :], ACT.Copy).then_inc(a_oc, 1)

            def a_tap(j):
                if j == 0:
                    act.wait_ge(s_out, 16 * 6)
                if j >= 3:
                    act.wait_ge(c_m, j - 2)
                A(yb[:, j % 3, 0:SEQ], pj[:, TX + j, 0:SEQ], ACT.Identity,
                  bias=gcol[:, G_CB + j:G_CB + j + 1],
                  scale=cwcol[:, 3 * CT + j:3 * CT + j + 1]).then_inc(c_i, 1)

            def a_sigmoid(j):
                if j >= 2:
                    act.wait_ge(c_m, j - 1)
                if j < CT:
                    if j == 0:
                        act.wait_ge(s_nv, 1)
                        act.wait_ge(s_out, 16 * 6)
                    act.wait_ge(c_v, j + 1)
                    A(eb[:, j % 2, 0:SEQ], yb[:, j % 3, 0:SEQ], ACT.Exp, scale=-1.0).then_inc(c_e, 1)
                else:
                    if j == CT:
                        act.wait_ge(z_in, 16)
                    A(eb[:, j % 2], pj[:, TZ + j - CT, :], ACT.Exp, scale=-1.0).then_inc(c_e, 1)

            for s in range(UN + 5):
                if s < UN:
                    a_exp(s)
                if 1 <= s <= UN:
                    a_second(s - 1)
                if 3 <= s < UN + 3:
                    a_wcopy(s - 3)
                if s >= 8 and s % QB == 0:
                    a_out((s - 8) // QB)
                if 3 <= s < CT + 3:
                    a_tap(s - 3)
                if 5 <= s < JOBS + 5:
                    a_sigmoid(s - 5)
                if s == 4:
                    act.wait_ge(c_dv, 1)
                    A(csr, pj[:, TX:TX + CT, SEQ:T], ACT.Exp, scale=-1.0).then_inc(c_de, 1)
            act.wait_ge(d_v, 1)
            A(sp5[1][0:NSH], sp5[1][0:NSH], ACT.Exp, scale=-1.0).then_inc(d_s, 1)
            act.wait_ge(s_small, 16 * 16)
            A(hcol[0:NSH, 2:3], hcol[0:NSH, 1:2], ACT.Exp).then_inc(d_s, 1)
            act.wait_ge(d_v, 2)
            A(sp5[3][0:NSH], sp5[2][0:NSH], ACT.Ln).then_inc(d_s, 1)
            act.wait_ge(d_v, 3)
            A(ecat[0:NSH, 0:NB], sp5[4][0:NSH, SEQ:T], ACT.Exp).then_inc(d_s, 1)
            act.wait_ge(e_t, 3)
            A(decb, ps[:, 1, 256:320].rearrange("p (h c) -> p h c", c=QB), ACT.Exp).then_inc(e_dx, 1)
            act.wait_ge(e_c, 4)
            A(dsk, dsk, ACT.Exp).then_inc(e_dx, 1)
            act.wait_ge(e_t, 4)
            A(bcrow[0:NB], ps[0:NB, 5, :].rearrange("p (k n) -> p k n", k=4), ACT.Copy).then_inc(g_bc, 1)
            act.wait_ge(g_bc, 1)
            act.dma_start(bc_scr, bcrow[0:NB]).then_inc(g_bs, 16)
            act.wait_ge(g_bs, 16)
            act.wait_ge(s_vu, 16 * NB + 4)
            for k in range(4):
                act.dma_start(bcb[:, k], bc_scr[:, k].unsqueeze(0).to_broadcast([P, NB, NS]))\
                    .then_inc(g_bb, 16)
            for g in range(2):
                act.wait_ge(e_t, g + 5)
                A(btok[:, :, g, :], ps[:, g, :].rearrange("p (c n) -> p c n", c=QB), ACT.Copy)\
                    .then_inc(e_bc, 1)
            for h in range(NSH):
                act.wait_ge(f_d, h + 1)
                if h >= 2:
                    act.wait_ge(f_y, h - 1)
                A(cd[:, h % 2], ps[:, 4 + h % 2, :].rearrange("p (c n) -> p c n", c=QB), ACT.Exp)\
                    .then_inc(f_c, 1)
                A(dl[:, h % 2], dl[:, h % 2], ACT.Exp).then_inc(f_e, 1)
                t = h // 2
                if h % 2 == 0:
                    if t == 0:
                        act.wait_ge(s_dor, 2)
                    if t >= 2:
                        act.wait_ge(z_o, t - 1)
                    A(tmp[:, t % 2], pj[:, TQ + t, :], ACT.Square).then_inc(z_q, 1)
                else:
                    act.wait_ge(z_s, t + 1)
                    A(halves(tmp[:, t % 2]), ps[:, 6:8, 0:HALF], ACT.Sqrt, bias=epsc[:, 1:2], scale=1.0 / P)\
                        .then_inc(z_rt, 1)
            act.wait_ge(f_ft, 1)
            A(fst, ps[:, 0:2, :].rearrange("p b (t n) -> p (b t) n", n=NS), ACT.Copy).then_inc(f_fc, 1)
            for t in range(NH):
                act.wait_ge(z_o, t + 1)
                A(uh[:, t], pj[:, TQ + t, :], ACT.Copy).then_inc(z_h, 1)
            for t in range(8):
                act.wait_ge(z_y, t + 1)
                A(pj[:, TZ + t, :], pj[:, TY + t, :], ACT.Square).then_inc(z_q, 1)
            for g in range(2):
                act.wait_ge(z_s, NH + g + 1)
                A(halves(tmp[:, g]), ps[:, 2 * g:2 * g + 2, 0:HALF], ACT.Sqrt, bias=epsc[:, 0:1],
                  scale=1.0 / 512).then_inc(z_rt, 1)
            for t in range(8):
                act.wait_ge(z_o, NH + t + 1)
                A(uh[:, 8 + t], pj[:, TY + t, :], ACT.Copy).then_inc(z_h, 1)
            for k in range(2):
                act.wait_ge(h_pt, k + 1)
                A(ph[:, k, 0:SEQ], ps[:, 2 * k, :], ACT.Copy).then_inc(h_pc, 1)
                A(ph[:, k, SEQ:T], ps[:, 2 * k + 1, 0:NB], ACT.Copy).then_inc(h_pc, 1)

            def square(c, per, i):
                act.wait_ge(h_e, at(c + 1, per, i))
                act.wait_ge(h_a, at(c + 1, per, i))
                src = hT[:, bass.ds(at(2 * c, 2 * per, i), 2), :] if i is not None else hT[:, 2 * c:2 * c + 2, :]
                A(sq, src, ACT.Square).then_inc(h_q, 1)

            with act.Fori(0, 8) as i:
                for j in range(4):
                    hi(SL_OUT + 2 + j, 4, i)
                square(0, 1, i)
            for k in range(KT):
                if k == 0:
                    act.wait_ge(w_used, SL_MLP + 2)
                A(uh[:, k], hT[:, k], ACT.Copy, scale=gcol[:, G_FFN + k:G_FFN + k + 1]).then_inc(s_uh, 1)
            act.wait_ge(h_s, 1)
            A(halves(rstd), ps[:, 0:2, 0:HALF], ACT.Sqrt, bias=epsc[:, 0:1], scale=1.0 / D_MODEL)\
                .then_inc(h_rt, 1)

            def hidden(c, per, i, slot, m):
                act.wait_ge(m_t, at(2 * (c + 1), 2 * per, i))
                act.wait_ge(m_l, at(c + 1, per, i))
                chain(A(sq, tm, ACT.Square))
                A(hh[:, slot, 2 * m:2 * m + 2], sq, ACT.Copy).then_inc(m_q, 1)

            def up(n, c, per_n, per_c, i, slot):
                for m in range(2):
                    for j in range(1, 5):
                        hi(n + 4 * m + j, per_n, i)
                    hidden(c + m, per_c, i, slot, m)

            def down(n, per_n, i):
                for j in range(1, 9):
                    hi(n + j, per_n, i)

            b = SL_MLP + 2
            hi(b)
            up(b, 0, 0, 0, None, 0)
            steps = chain.n
            with act.Fori(0, (CHUNKS - 2) // 2) as i:
                chain.n = i * 4 + steps
                up(b + 8, 2, 32, 4, i, 1)
                down(b + 16, 32, i)
                up(b + 24, 4, 32, 4, i, 0)
                down(b + 32, 32, i)
            chain.n = steps + 4 * (CHUNKS - 2) // 2
            up(SL_PLE - 22, 2 * CHUNKS - 2, 0, 0, None, 1)
            down(SL_PLE - 14, 0, None)
            for j in range(1, 8):
                hi(SL_PLE - 6 + j)
            for g in range(8):
                hi(SL_PLE + 2 + g)
                if g == 0:
                    act.wait_ge(h_e, 8 + 8 * CHUNKS)
                A(uh[:, 2 * g:2 * g + 2], hT[:, 2 * g:2 * g + 2], ACT.Copy).then_inc(s_uh, 1)
                act.wait_ge(p_e, g + 1)
                act.wait_ge(h_a, 8 + g + 1)
                if g == 0:
                    act.wait_ge(m_l, 2 * CHUNKS + 1)
                A(sq, eT[:, 2 * g:2 * g + 2], ACT.Square).then_inc(h_q, 1)
            act.wait_ge(h_s, 2)
            A(halves(rstd), ps[:, 0:2, 0:HALF], ACT.Sqrt, bias=epsc[:, 0:1], scale=1.0 / D_MODEL)\
                .then_inc(h_rt, 1)

            def gate(c, per, i):
                act.wait_ge(x_c, at(c + 1, per, i))
                A(tm, tm, ACT.Exp, scale=-1.0).then_inc(x_e, 1)

            def gate_sq(c, per, i):
                act.wait_ge(x_h, at(c + 2, per, i))
                act.wait_ge(h_a, at(16 + c + 1, per, i))
                src = hT[:, bass.ds(at(2 * c, 2 * per, i), 2), :] if i is not None else hT[:, 2 * c:2 * c + 2, :]
                A(sq, src, ACT.Square).then_inc(h_q, 1)

            for j in range(4):
                hi(SL_GATE + 2 + j)
            with act.Fori(0, 3) as i:
                for m in range(2):
                    gate(m, 2, i)
                    hi(SL_GATE + 6 + 4 * m, 8, i)
                    gate_sq(m, 2, i)
                    for j in range(1, 4):
                        hi(SL_GATE + 6 + 4 * m + j, 8, i)
            for m in range(2):
                gate(6 + m, 0, None)
                if m == 0:
                    hi(SL_ALL - 2)
                gate_sq(6 + m, 0, None)
                if m == 0:
                    hi(SL_ALL - 1)
            act.wait_ge(h_s, 3)
            A(halves(rstd), ps[:, 0:2, 0:HALF], ACT.Sqrt, bias=epsc[:, 0:1], scale=1.0 / D_MODEL)\
                .then_inc(h_rt, 1)
            for q in range(QB + 1):
                for r in (0, 2):
                    u = 4 * q + r
                    act.wait_ge(y_t, u + 1)
                    dst = yt[:, q, r * 512:(r + 1) * 512] if q < QB else ys[0:NB, r * 512:(r + 1) * 512]
                    src = ps[:, 2 + u % 6, :] if q < QB else ps[0:NB, 2 + u % 6, :]
                    A(dst, src, ACT.Copy).then_inc(y_c, 1)

        @block.gpsimd
        def _(pool):
            step = Chain(pool, pool_step)
            pool.sem_inc(s_km, 1)
            step(pool.memset(ident, 0.0))
            step(pool.affine_select(out=ident, in_=ident, compare_op=ALU.not_equal, fill=1.0, base=0,
                                    pattern=[[-1, P]], channel_multiplier=1))
            step(pool.memset(causal, 0.0))
            step(pool.affine_select(out=causal, in_=causal, compare_op=ALU.is_ge, fill=NEG, base=0,
                                    pattern=[[1, P]], channel_multiplier=-1))
            step(pool.memset(rowm[0:NB], NEG))
            pool.affine_select(out=rowm[0:NB], in_=rowm[0:NB], compare_op=ALU.not_equal, fill=0.0, base=0,
                               pattern=[[-1, NB]], channel_multiplier=1).then_inc(s_const, 1)
            pool.memset(ones, 1.0).then_inc(s_const, 1)
            pool.memset(epsc[:, 0:1], EPS).then_inc(s_const, 1)
            pool.memset(epsc[:, 1:2], EPS_SUB).then_inc(s_const, 1)
            with pool.Fori(0, NB // 2) as i:
                for b in range(2):
                    pool.wait_ge(s_qbc, at(16 * (b + 1), 32, i))
                    for pg in range(PAGES * b, PAGES * (b + 1)):
                        s = pg % 4
                        pool.wait_ge(s_kp[s], at(16 * (pg // 4 + 1), 8 * PAGES, i))
                        pool.tensor_tensor(kpage[:, s], kpage[:, s], qbc[:, b], ALU.mult).then_inc(s_km, 1)
            pool.wait_ge(w_used, SL_OUT + 2)
            pool.iota(dist, pattern=[[1, 896]], base=-384, channel_multiplier=-1,
                      allow_small_or_imprecise_dtypes=True).then_inc(s_dc, 1)
            pool.iota(ddist, pattern=[[P, PAGES]], base=-PAST, channel_multiplier=1,
                      allow_small_or_imprecise_dtypes=True).then_inc(s_dc, 1)
            pool.wait_ge(s_dc, 2)
            pool.affine_select(out=dist, in_=dist, compare_op=ALU.is_ge, fill=NEG, base=384,
                               pattern=[[-1, 896]], channel_multiplier=1).then_inc(s_dc, 1)
            for h in range(NH):
                pool.tensor_scalar(dbias[:, :, 2 * h:2 * h + 2],
                                   ddist.unsqueeze(2).to_broadcast([P, PAGES, 2]),
                                   SLOPES[h] / SCALE, 1.0, ALU.mult, ALU.mult).then_inc(s_dc, 1)
            pool.memset(sc[:, :, PAGES, :], NEG).then_inc(s_dc, 1)
            for j in range(JOBS):
                n = SEQ if j < CT else T
                pool.wait_ge(c_e, j + 1)
                pool.tensor_scalar(eb[:, j % 2, 0:n], eb[:, j % 2, 0:n], 3.0e38, 1.0, ALU.min, ALU.add)\
                    .then_inc(c_p, 1)
            for c in range(QB):
                pool.wait_ge(e_xd, 8)
                pool.wait_ge(e_dx, 2)
                pool.tensor_tensor(xdd[:, c].rearrange("p (h n) -> p h n", h=NSH),
                                   xd[:, c].rearrange("p (h n) -> p h n", h=NSH),
                                   dsk[:, c].unsqueeze(2).to_broadcast([P, NSH, HD]), ALU.mult)\
                    .then_inc(e_xdd, 1)
            for c in range(1, QB):
                pool.wait_ge(e_sc, c)
                pool.tensor_tensor(sall[:, c].rearrange("p (h n) -> p h n", h=NSH),
                                   sall[:, c - 1].rearrange("p (h n) -> p h n", h=NSH),
                                   decb[:, :, c].unsqueeze(2).to_broadcast([P, NSH, HD]), ALU.mult)\
                    .then_inc(e_sm, 1)
            for h in range(NSH):
                g, t = h // 8, h // 2
                if h == 0:
                    pool.wait_ge(e_cbc, 2)
                pool.wait_ge(f_c, h + 1)
                pool.tensor_tensor(cd[:, h % 2], cd[:, h % 2],
                                   pj[:, CX + TC_ + g, 0:SEQ].rearrange("p (c n) -> p c n", c=QB),
                                   ALU.mult).then_inc(f_cm, 1)
                pool.wait_ge(f_e, h + 1)
                pool.tensor_tensor(dl[:, h % 2], dl[:, h % 2], cbt[:, g], ALU.mult).then_inc(f_m, 1)
                if h % 2 == 0:
                    if t == 0:
                        pool.wait_ge(g_bb, 16 * 4)
                        pool.wait_ge(g_xd, 1)
                    else:
                        pool.wait_ge(g_r, t)
                    pool.tensor_tensor(bx, bcb[:, t // 4], xdt[:, t].unsqueeze(2).to_broadcast([P, NB, NS]),
                                       ALU.mult).then_inc(g_b, 1)
                else:
                    pool.wait_ge(g_n, t + 1)
                    pool.tensor_tensor(bx, stt[:, t % 2], bcb[:, 2 + t // 4], ALU.mult).then_inc(g_c, 1)
            pool.wait_ge(g_y, 1)
            pool.wait_ge(f_yc, 8)
            pool.wait_ge(c_m, JOBS)
            for t in range(8):
                pool.tensor_tensor(pj[:, TY + t, :], pj[:, TY + t, :], pj[:, TZ + t, :], ALU.mult)\
                    .then_inc(z_y, 1)
            pool.wait_ge(z_l, KT)
            step(pool.memset(acc, 0.0))
            pool.sem_inc(h_a, 1)

            def add_squares(c, per, i):
                pool.wait_ge(h_q, at(c + 1, per, i))
                step(pool.tensor_tensor(acc, acc, sq[:, 0], ALU.add))
                ins = pool.tensor_tensor(acc, acc, sq[:, 1], ALU.add)
                ins.then_inc(h_a, 1)
                pool.wait_ge(h_a, at(c + 2, per, i))

            n0 = step.n
            with pool.Fori(0, 8) as i:
                step.n = i * 1 + n0
                add_squares(0, 1, i)
            step.n = n0 + 8
            pool.wait_ge(h_rt, 1)
            step(pool.memset(acc, 0.0))
            n0 = step.n
            with pool.Fori(0, 8) as i:
                step.n = i * 1 + n0
                add_squares(8, 1, i)
            step.n = n0 + 8
            pool.wait_ge(h_rt, 2)
            step(pool.memset(acc, 0.0))
            n0 = step.n
            with pool.Fori(0, 8) as i:
                pool.wait_ge(x_e, at(1, 1, i))
                pool.tensor_tensor(tm, tm, ones[:, 0:1].unsqueeze(2).to_broadcast([P, 2, T]), ALU.add)\
                    .then_inc(x_p, 1)
                pool.wait_ge(x_r, at(1, 1, i))
                pool.tensor_tensor(tm, tm, eT[:, bass.ds(i * 2, 2), :], ALU.mult).then_inc(x_m, 1)
                step.n = i * 1 + n0
                add_squares(16, 1, i)

        @block.tensor
        def _(pe):
            pe.sem_inc(w_used, 2)
            pe.sem_inc(s_vu, 4)
            pe.sem_inc(group_free, 2)
            mm = pe.matmul
            pe.wait_ge(s_const, 4)
            pe.wait_ge(s_small, 16 * 16)
            pe.transpose(ps[:, 4, 0:85], grow[0:85, :], ident[0:85, 0:85]).then_inc(s_gt, 1)
            pe.transpose(ps[:, 5, 0:48], cwrow[0:48, :], ident[0:48, 0:48]).then_inc(s_gt, 1)
            for t in range(CT):
                last = pe.transpose(ps[:, 6, 24 * t:24 * t + 24], cstrow[0:24, t * P:(t + 1) * P],
                                    ident[0:24, 0:24])
            last.then_inc(s_gt, 1)
            pe.wait_ge(s_xs, 16)
            for k in range(KT):
                last = pe.transpose(ps[:, 7, 8 * k:8 * k + 8], xs[0:NB, k * P:(k + 1) * P],
                                    ident[0:NB, 0:NB])
            last.then_inc(s_xsT, 1)
            pe.wait_ge(s_x, 16 * QB)
            for k in range(KT):
                if k >= 4:
                    pe.wait_ge(s_ul, k - 3)
                for q in range(QB):
                    last = pe.transpose(ps[:, k % 4, q * P:(q + 1) * P], xt[:, q, k * P:(k + 1) * P], ident)
                last.then_inc(s_xT, 1)
            pe.wait_ge(s_gc, 4)
            pe.wait_ge(s_rt, 5)
            for q in range(QB):
                mm(ps[:, 4, q * P:(q + 1) * P], ones, rdiag[:, q, :], start=True, stop=True)
            mm(ps[:, 5, 0:NB], ones[0:NB, :], junk[0:NB, 0:NB], start=True, stop=True).then_inc(s_rb, 1)
            pe.wait_ge(s_rd, 2)
            pe.wait_ge(s_ul, KT)
            pe.wait_ge(s_us, 1)

            def slab(c, per, i, kts, ms, first, last, bank, kstep, mstep=P, inc=None):
                pe.wait_ge(lo_ready, at(c + 3, per, i))
                s = c % 2
                n = len(kts)
                for x, (k, xh, xl) in enumerate(kts):
                    for m in range(ms):
                        a = k * kstep + m * mstep
                        h_, l_ = wh[:, s, a:a + P], wl[:, s, a:a + P]
                        st, en = first and x == 0, last and x == n - 1
                        for f in range(2):
                            mm(ps[:, bank + 2 * m + f, 0:HALF], h_, xh[:, f * HALF:(f + 1) * HALF],
                               start=st, stop=False)
                            mm(ps[:, bank + 2 * m + f, 0:HALF], h_, xl[:, f * HALF:(f + 1) * HALF],
                               start=False, stop=False)
                        for f in range(2):
                            z = mm(ps[:, bank + 2 * m + f, 0:HALF], l_, xh[:, f * HALF:(f + 1) * HALF],
                                   start=False, stop=en)
                z.then_inc(w_used, 1)

            def group(n, g, per_n, per_g, i):
                pe.wait_ge(group_free, at(g + 1, per_g, i))
                for j in range(4):
                    slab(n + j, per_n, i, [(k, uh[:, 4 * j + k], ul[:, 4 * j + k]) for k in range(4)], 2,
                         j == 0, j == 3, GB[g % 2], 256)

            with pe.Fori(0, 2) as i:
                group(0, 0, 8, 2, i)
                group(4, 1, 8, 2, i)
            pe.wait_ge(group_free, 6)
            for t in range(NH):
                last = pe.transpose(ps[0:NB, t // 4, t % 4 * P:(t % 4 + 1) * P], pj[:, TQ + t, SEQ:T], ident)
            last.then_inc(s_qt, 1)
            pe.wait_ge(s_qtc, 1)
            with pe.Fori(0, 9) as i:
                group(16, 4, 8, 2, i)
                group(20, 5, 8, 2, i)
            pe.wait_ge(group_free, G_DT + 1)
            for j in range(2):
                slab(SL_DT + j, 0, None, [(k, uh[:, 8 * j + k], ul[:, 8 * j + k]) for k in range(8)], 1,
                     j == 0, j == 1, GB[G_DT % 2], P)
            pe.wait_ge(group_free, G_OUT + 2)
            for t in range(NH):
                for base_t, b, got, out in ((TK, 2 * t % 4, s_kto, s_kt), (TV, (2 * t + 1) % 4, s_vto, s_vt)):
                    if t >= 2:
                        pe.wait_ge(got, t - 1)
                    for q in range(QB):
                        last = pe.transpose(ps[:, b, q * P:(q + 1) * P], pj[:, base_t + t, q * P:(q + 1) * P],
                                            ident)
                    last.then_inc(out, 1)
            for base_t, b, out in ((TK, 4, s_rt3), (TV, 6, s_rt3)):
                for t in range(NH):
                    last = pe.transpose(ps[0:NB, b + t // 4, t % 4 * P:(t % 4 + 1) * P],
                                        pj[:, base_t + t, SEQ:T], ident)
                last.then_inc(out, 1)
            pe.wait_ge(s_kso, 1)
            pe.wait_ge(s_vso, 1)
            for t in range(CT):
                last = pe.transpose(ps[0:NB + 3, 4 + t // 4, t % 4 * P:(t % 4 + 1) * P],
                                    pj[:, TX + t, SEQ - 3:T], ident)
            last.then_inc(s_rt3, 1)
            pe.wait_ge(s_dv, 1)
            pe.wait_ge(s_kto, NH)
            pe.wait_ge(s_vto, NH)
            pe.transpose(ps[:, 0, 0:P], dmx, ident).then_inc(s_dp, 1)
            pe.wait_ge(s_dv, 2)
            mm(ps[:, 1, 0:P], ones, ddiag, start=True, stop=True).then_inc(s_dp, 1)
            pe.wait_ge(s_dv, 4)
            mm(ps[:, 2, 0:P], ones, dmx, start=True, stop=True).then_inc(s_dp, 1)
            UN = NH * QB

            def scores(u):
                h, q = u // QB, u % QB
                n = (q + 1) * P
                for c in range(2):
                    j = 2 * u + c
                    if j >= 3:
                        pe.wait_ge(a_b, j - 2)
                    mm(ps[:, j % 3, 0:n], pj[64 * c:64 * c + 64, TQ + h, q * P:(q + 1) * P],
                       pj[64 * c:64 * c + 64, TK + h, 0:n], start=True, stop=True).then_inc(a_s, 1)

            def turn(u):
                q = u % QB
                pe.wait_ge(a_w, u + 1)
                if u >= 2:
                    pe.wait_ge(a_wt, u - 1)
                for k in range(q + 1):
                    last = pe.transpose(ps[:, 3 + u % 2, k * P:(k + 1) * P],
                                        se[:, u % 3, 0, k * P:(k + 1) * P], ident)
                last.then_inc(a_t, 1)

            def values(h):
                pe.wait_ge(a_wt, 4 * (h + 1))
                if h >= 1:
                    pe.wait_ge(a_oc, h)
                for k in range(QB):
                    last = mm(ps[:, 5, k * P:SEQ], vtok[:, k, h * P:(h + 1) * P],
                              wt[:, h % 2, k, k * P:SEQ], start=(k == 0), stop=(k == QB - 1))
                last.then_inc(a_o, 1)

            def page_values(n):
                b = n // PAGES
                if n % 4 == 0:
                    pe.wait_ge(s_wz, n // 4 + 2)
                pe.wait_ge(s_vp[n % 4], 16 * (n // 4 + 1))
                for f in range(2):
                    last = mm(ps[0:64, 6 + f, :], zpad[:, n // 4 % 2, n % 4, 56 - 8 * b:120 - 8 * b],
                              vpage[:, n % 4, f * 512:(f + 1) * 512], start=False, stop=(n == NB * PAGES - 1))
                last.then_inc(s_vu, 1)

            pe.wait_ge(s_wz, 1)
            for f in range(2):
                last = mm(ps[0:64, 6 + f, :], wnew[0:NB, :], vstok[0:NB, f * 512:(f + 1) * 512],
                          start=True, stop=False)
            last.then_inc(s_nv, 1)
            pe.wait_ge(s_vso, 2)
            for s in range(UN + 5):
                pages = iter(range(4 * s, min(4 * s + 4, NB * PAGES)))
                if s < UN:
                    scores(s)
                    page_values(next(pages))
                if 2 <= s < UN + 2:
                    turn(s - 2)
                if s < UN:
                    page_values(next(pages))
                if s >= 7 and s % QB == 3:
                    values(s // QB - 1)
                for n in pages:
                    page_values(n)
            pe.wait_ge(s_dor, 1)
            for h in range(NH):
                last = mm(ps[:, 7, NB * h:NB * (h + 1)], oacc[0:64, h * P:(h + 1) * P], ident[0:64, h:64:NH],
                          start=True, stop=True)
            last.then_inc(s_dos, 1)
            pe.wait_ge(d_v, 4)
            pe.wait_ge(a_oc, NH)
            pe.wait_ge(d_s, 4)
            for c in range(QB):
                pe.transpose(ps[:, 0, c * NSH:(c + 1) * NSH], dtt[0:NSH, c * P:(c + 1) * P], ident[0:NSH, 0:NSH])
                last = pe.transpose(ps[:, 0, 64 + c * NSH:64 + (c + 1) * NSH], acs[0:NSH, c * P:(c + 1) * P],
                                    ident[0:NSH, 0:NSH])
            last.then_inc(e_t, 1)
            for h in range(NSH):
                r0 = HD * (h % 2)
                last = mm(ps[r0:r0 + HD, 1, 17 * (h // 2):17 * (h // 2) + 17],
                          ident[0:NSH, h:h + 1].to_broadcast([NSH, HD]), ecat[0:NSH, :], start=True, stop=True)
            last.then_inc(e_t, 1)
            for h in range(NSH):
                last = mm(ps[:, 1, 256 + QB * h:256 + QB * (h + 1)], ident[0:NSH, h:h + 1].to_broadcast([NSH, P]),
                          acs[0:NSH, P - 1:SEQ:P], start=True, stop=True)
            last.then_inc(e_t, 1)
            pe.wait_ge(c_m, CT)
            for k in range(4):
                last = pe.transpose(ps[0:NB, 5, k * P:(k + 1) * P], pj[:, CX + 8 + k, SEQ:T], ident)
            last.then_inc(e_t, 1)
            pe.wait_ge(e_c, 4)
            pe.wait_ge(e_dx, 1)
            for g in range(2):
                for c in range(QB):
                    last = pe.transpose(ps[:, g, c * P:(c + 1) * P],
                                        pj[:, CX + TB_ + g, c * P:(c + 1) * P], ident)
                last.then_inc(e_t, 1)
            for t in range(8):
                if t >= 2:
                    pe.wait_ge(e_xd, t - 1)
                for c in range(QB):
                    last = pe.transpose(ps[:, 2 + t % 2, c * P:(c + 1) * P],
                                        pj[:, CX + t, c * P:(c + 1) * P], ident)
                last.then_inc(e_xt, 1)
            pe.wait_ge(g_bc, 1)
            for g in range(2):
                for c in range(QB):
                    last = mm(ps[:, 4 + g, c * P:(c + 1) * P], pj[:, CX + TB_ + g, c * P:(c + 1) * P],
                              pj[:, CX + TC_ + g, c * P:(c + 1) * P], start=True, stop=True)
                last.then_inc(e_cb, 1)
            pe.wait_ge(e_bc, 2)
            pe.wait_ge(e_dx, 2)
            pe.wait_ge(e_c, 4)
            pe.wait_ge(e_xd, 8)
            for c in range(QB):
                pe.wait_ge(e_xdd, c + 1)
                if c >= 2:
                    pe.wait_ge(e_sc, c - 1)
                for g in range(2):
                    last = mm(ps[:, 2 * (c % 2) + g, :], btok[:, c, g, :], xdd[:, c, g * 512:(g + 1) * 512],
                              start=True, stop=True)
                last.then_inc(e_st, 1)

            def spread(h):
                if h >= 2:
                    pe.wait_ge(f_c, h - 1)
                    pe.wait_ge(f_d, h - 1)
                mm(ps[:, 4 + h % 2, :], ident[0:NSH, h:h + 1].to_broadcast([NSH, P]), acs[0:NSH, :],
                   start=True, stop=True).then_inc(f_a, 1)

            def y_head(h):
                pe.wait_ge(f_m, h + 1)
                pe.wait_ge(f_cm, h + 1)
                t = h // 2
                if h % 2 == 0 and t >= 2:
                    pe.wait_ge(f_yc, t - 1)
                r = 64 * (h % 2)
                for c in range(QB):
                    out = ps[r:r + 64, 2 + t % 2, c * P:(c + 1) * P]
                    last = mm(out, xd[:, c, h * HD:(h + 1) * HD], dl[:, h % 2, c, :], start=True, stop=(c == 0))
                    if c:
                        last = mm(out, sall[:, c - 1, h * HD:(h + 1) * HD], cd[:, h % 2, c, :],
                                  start=False, stop=True)
                last.then_inc(f_y, 1)

            pe.wait_ge(e_cbc, 2)
            pe.wait_ge(e_sc, QB)
            for s in range(NSH + 1):
                if s < NSH:
                    spread(s)
                if s >= 1:
                    y_head(s - 1)
                if s % 2:
                    t = s // 2
                    pe.wait_ge(z_q, t + 1)
                    if t >= 1:
                        pe.wait_ge(z_rt, t)
                    for f in range(2):
                        last = mm(ps[:, 6 + f, 0:HALF], ones, tmp[:, t % 2, f * HALF:(f + 1) * HALF],
                                  start=True, stop=True)
                    last.then_inc(z_s, 1)
            for t in range(8):
                last = pe.transpose(ps[:, t // 4, t % 4 * P:(t % 4 + 1) * P], sall[:, QB - 1, t * P:(t + 1) * P],
                                    ident)
            last.then_inc(f_ft, 1)
            def out_slab(g, j):
                slab(SL_OUT + 4 * g + j, 0, None, [(k, uh[:, 4 * j + k], ul[:, 4 * j + k]) for k in range(4)],
                     2, j == 0, j == 3, GB[(G_OUT + g) % 2], 256)

            pe.wait_ge(group_free, G_OUT + 1)
            pe.wait_ge(z_rt, NH)
            for j in range(2):
                pe.wait_ge(z_l, 4 * (j + 1))
                out_slab(0, j)
            pe.wait_ge(f_fc, 1)
            pe.wait_ge(f_yc, 8)
            for t in range(8):
                pe.wait_ge(z_q, NH + t + 1)
                b = 2 * (t // 4)
                for f in range(2):
                    last = mm(ps[:, b + f, 0:HALF], ones, pj[:, TZ + t, f * HALF:(f + 1) * HALF],
                              start=(t % 4 == 0), stop=(t % 4 == 3))
                if t % 4 == 3:
                    last.then_inc(z_s, 1)
            pe.wait_ge(h_p, 32)
            pe.wait_ge(z_rt, NH + 2)
            for k in range(2):
                for q in range(QB):
                    pe.transpose(ps[:, 2 * k, q * P:(q + 1) * P], ptok[:, q, k * P:(k + 1) * P], ident)
                pe.transpose(ps[:, 2 * k + 1, 0:NB], pstok[0:NB, k * P:(k + 1) * P], ident[0:NB, 0:NB])\
                    .then_inc(h_pt, 1)
            def residual(g, m0):
                for m in range(2):
                    col = (2 * m0 + m) * P
                    b = GB[g % 2] + 2 * m
                    for q in range(QB):
                        x_ = xt3[:, q, col:col + P]
                        lo_c, hi_c = q * P, (q + 1) * P
                        for f in range(2):
                            a0, a1 = max(lo_c, f * HALF), min(hi_c, (f + 1) * HALF)
                            if a0 < a1:
                                mm(ps[:, b + f, a0 - f * HALF:a1 - f * HALF], x_, ident[:, a0 - lo_c:a1 - lo_c],
                                   start=False, stop=False)
                    mm(ps[:, b + 1, SEQ - HALF:HALF], xs3[0:NB, col:col + P], ident[0:NB, 0:NB],
                       start=False, stop=False)

            for g in range(8):
                if g == 1:
                    pe.wait_ge(h_pc, 4)
                    pe.wait_ge(h_pl, 4)
                if g:
                    pe.wait_ge(group_free, G_OUT + g + 1)
                for j in range(4):
                    if g == 0 and j < 2:
                        continue
                    if g == 0:
                        pe.wait_ge(z_l, 4 * (j + 1))
                    if j == 3:
                        if g == 0:
                            pe.wait_ge(h_x, 16 * 5)
                        residual(G_OUT + g, g)
                    out_slab(g, j)

            def norm_sum(g_free, n):
                pe.wait_ge(group_free, g_free)
                for f in range(2):
                    last = mm(ps[:, f, 0:HALF], ones, acc[:, f * HALF:(f + 1) * HALF], start=True, stop=True)
                last.then_inc(h_s, 1)

            pe.wait_ge(group_free, G_MLP + 2)
            pe.wait_ge(h_a, 9)
            norm_sum(G_MLP + 2, 1)
            pe.wait_ge(s_ul, 2 * KT)
            def up(n, g, per_n, per_g, i, first=False):
                group(n, g, per_n, per_g, i)
                if first:
                    pe.wait_ge(h_rt, 1)
                group(n + 4, g + 1, per_n, per_g, i)

            def down(n, g, per_n, per_g, i, slot, c, per_c):
                pe.wait_ge(m_l, at(2 * c + 3, 2 * per_c, i))
                for j in range(8):
                    pe.wait_ge(group_free, at(g + j + 1, per_g, i))
                    slab(n + j, per_n, i, [(k, hh[:, slot, k], hl[:, slot, k]) for k in range(4)], 2,
                         True, True, GB[(g + j) % 2], 256)

            up(SL_MLP, G_MLP, 0, 0, None, True)
            with pe.Fori(0, (CHUNKS - 2) // 2) as i:
                n, g = SL_MLP + 8, G_MLP + 2
                up(n, g, 32, 20, i)
                down(n + 8, g + 2, 32, 20, i, 0, 0, 2)
                up(n + 16, g + 10, 32, 20, i)
                down(n + 24, g + 12, 32, 20, i, 1, 1, 2)
            n, g = SL_PLE - 24, G_PLE - 18
            up(n, g, 0, 0, None)
            down(n + 8, g + 2, 0, 0, None, 0, CHUNKS - 2, 0)
            down(n + 16, g + 10, 0, 0, None, 1, CHUNKS - 1, 0)
            for g in range(8):
                pe.wait_ge(group_free, G_PLE + g + 1)
                slab(SL_PLE + g, 0, None, [(k, ph[:, k], pl[:, k]) for k in range(2)], 2, True, True,
                     GB[(G_PLE + g) % 2], 256)
            pe.wait_ge(h_a, 17)
            pe.wait_ge(s_ul, 2 * KT + 8)
            pe.wait_ge(group_free, G_GATE + 2)
            norm_sum(G_GATE + 2, 2)
            group(SL_GATE, G_GATE, 0, 0, None)
            pe.wait_ge(h_rt, 2)
            group(SL_GATE + 4, G_GATE + 1, 0, 0, None)
            with pe.Fori(0, 3) as i:
                group(SL_GATE + 8, G_GATE + 2, 8, 2, i)
                group(SL_GATE + 12, G_GATE + 3, 8, 2, i)
            pe.wait_ge(h_a, 25)
            norm_sum(G_GATE + 10, 3)
            u = 0
            for q in range(QB + 1):
                for r in range(4):
                    if u >= 6:
                        v = u - 6
                        if v % 2 == 0:
                            pe.wait_ge(y_c, v // 2 + 1)
                        else:
                            pe.wait_ge(y_d, v // 2 + 1)
                    for k in range(4):
                        kt = 4 * r + k
                        if q == 0:
                            pe.wait_ge(y_s, kt + 1)
                        if q < QB:
                            last = pe.transpose(ps[:, 2 + u % 6, k * P:(k + 1) * P], hT[:, kt, q * P:(q + 1) * P],
                                                ident)
                        else:
                            last = pe.transpose(ps[0:NB, 2 + u % 6, k * P:(k + 1) * P], hT[:, kt, SEQ:T], ident)
                    last.then_inc(y_t, 1)
                    u += 1

        @block.vector
        def _(dve):
            tt, stt_, ts = dve.tensor_tensor, dve.scalar_tensor_tensor, dve.tensor_scalar
            link = Chain(dve, dve_step)
            dve.sem_inc(lo_ready, 2)
            dve.sem_inc(s_kr, 4)

            def lo(c, per=0, i=None):
                dve.wait_ge(hi_ready, at(c + 1, per, i))
                tt(wl[:, c % 2], raw[:, c % 2], wh[:, c % 2].bitcast(F32), ALU.subtract).then_inc(lo_ready, 1)

            dve.wait_ge(s_gt, 3)
            dve.tensor_copy(gcol, ps[:, 4, 0:85]).then_inc(s_gc, 1)
            dve.tensor_copy(cwcol, ps[:, 5, 0:48]).then_inc(s_gc, 1)
            dve.tensor_copy(cst, ps[:, 6, 0:288].rearrange("p (t n) -> p t n", t=CT)).then_inc(s_gc, 1)
            dve.wait_ge(s_xsT, 1)
            dve.wait_ge(s_gc, 3)
            xs_T = ps[:, 7, 0:P].rearrange("p (k n) -> p k n", k=KT)
            g_bcast = gcol[:, G_MIX:G_MIX + KT].unsqueeze(2).to_broadcast([P, KT, NB])
            link(tt(xsg, xs_T, g_bcast, ALU.mult))
            link(dve.tensor_copy(uh[:, :, SEQ:T], xsg))
            tt(ul[:, :, SEQ:T], xsg, uh[:, :, SEQ:T].bitcast(F32), ALU.subtract).then_inc(s_us, 1)
            ts(gcol[:, G_SUB:G_SUB + 1], gcol[:, G_SUB:G_SUB + 1], 1.0 - LAM_INIT, None, ALU.mult)\
                .then_inc(s_gc, 1)
            dve.wait_ge(s_ss, 2)
            link(dve.reciprocal(ssx[:, 0:4], ssx[:, 0:4]))
            link(dve.reciprocal(ssx[0:NB, 4:5], ssx[0:NB, 4:5]))
            for q in range(QB):
                ts(rdiag[:, q, :], ident, ssx[:, q:q + 1], None, ALU.mult).then_inc(s_rt, 1)
            ts(junk[0:NB, 0:NB], ident[0:NB, 0:NB], ssx[0:NB, 4:5], None, ALU.mult).then_inc(s_rt, 1)
            for k in range(KT):
                dve.wait_ge(s_uh, k + 1)
                stt_(ul[:, k, 0:SEQ], ps[:, k % 4, :], gcol[:, G_MIX + k:G_MIX + k + 1],
                     uh[:, k, 0:SEQ].bitcast(F32), ALU.mult, ALU.subtract).then_inc(s_ul, 1)
                if k == 2:
                    lo(0)
                if k == 4:
                    lo(1)
            dve.wait_ge(s_rb, 1)
            dve.tensor_copy(rstd[:, 0:SEQ], ps[:, 4, :]).then_inc(s_rd, 1)
            dve.tensor_copy(rstd[:, SEQ:T], ps[:, 5, 0:NB]).then_inc(s_rd, 1)
            dve.wait_ge(s_rd, 2)
            r_b = halves(rstd).unsqueeze(1).to_broadcast([P, 2, 2, HALF])

            def evac(g, per, i, dst):
                dve.wait_ge(w_used, at(4 * (g + 1) + 2, 4 * per, i))
                tt(dst.rearrange("p m (h n) -> p m h n", h=2), group_view(g), r_b, ALU.mult)\
                    .then_inc(group_free, 1)

            def keys(b0, i, j):
                for pg in range(2 * j, 2 * j + 2):
                    dve.wait_ge(s_km, at(16 * b0 + pg + 2, 16, i))
                    dve.tensor_reduce(sc[:, bass.ds(at(b0, 1, i), 1), pg, :],
                                      kpage[:, pg % 4].rearrange("p (c n) -> p c n", n=DK).unsqueeze(1),
                                      AX, ALU.add).then_inc(s_kr, 1)

            def tiles(c, k, i):
                return pj[:, bass.ds(at(c, k, i), 2), :]

            with dve.Fori(0, 2) as i:
                for j in range(8):
                    lo(2 + j, 8, i)
                    if j % 4 == 3:
                        evac(j // 4, 2, i, tiles(2 * (j // 4), 4, i))
            with dve.Fori(0, 4) as i:
                for j in range(8):
                    lo(18 + j, 8, i)
                    keys(0, i, j)
                    if j % 4 == 3:
                        evac(4 + j // 4, 2, i, tiles(8 + 2 * (j // 4), 4, i))
            with dve.Fori(0, 2) as i:
                for j in range(8):
                    lo(50 + j, 8, i)
                    keys(4, i, j)
                    if j % 4 == 3:
                        m = j // 4
                        if m == 0:
                            dve.wait_ge(s_zout, at(16, 32, i))
                        else:
                            dve.wait_ge(s_zout, at(32, 32, i))
                        dve.wait_ge(w_used, at(4 * (12 + m + 1) + 2, 8, i))
                        tt(zst.rearrange("p m (h n) -> p m h n", h=2), group_view(m), r_b, ALU.mult)\
                            .then_inc(s_zst, 1)
                        dve.wait_ge(s_zst, at(m + 1, 2, i))
                        dve.sem_inc(group_free, 1)
            with dve.Fori(0, 2) as i:
                for j in range(8):
                    lo(66 + j, 8, i)
                    keys(6, i, j)
                    if j % 4 == 3:
                        evac(16 + j // 4, 2, i, tiles(24 + 2 * (j // 4), 4, i))
            for j in range(8):
                lo(82 + j)
                if j % 4 == 3:
                    evac(20 + j // 4, 0, None, pj[:, 32 + 2 * (j // 4):34 + 2 * (j // 4), :])
            dve.wait_ge(w_used, SL_OUT + 2)
            tt(halves(dtt[0:NSH]), ps[0:NSH, 0:2, 0:HALF], halves(rstd[0:NSH]), ALU.mult).then_inc(group_free, 1)
            for t in range(NH):
                dve.wait_ge(s_vt, t + 1)
                dve.tensor_copy(vtok[:, :, t * P:(t + 1) * P],
                                ps[:, (2 * t + 1) % 4, :].rearrange("p (q n) -> p q n", q=QB)).then_inc(s_vto, 1)
            dve.wait_ge(s_rt3, 2)
            dve.tensor_copy(vstok[0:NB, :].rearrange("p (b n) -> p b n", b=2), ps[0:NB, 6:8, :])\
                .then_inc(s_vso, 1)
            dve.wait_ge(s_rt3, 3)
            dve.tensor_copy(xbtok[0:11, :].rearrange("p (b n) -> p b n", b=3), ps[0:11, 4:7, :])\
                .then_inc(s_vso, 1)
            dve.wait_ge(s_small, 16 * 16)
            for n in range(2):
                dve.tensor_tensor_reduce(lamc[:, 2 * n, :], lamc[:, 2 * n, :], lamc[:, 2 * n + 1, :], 1.0, 0.0,
                                         ALU.mult, ALU.add, lams[:, n:n + 1]).then_inc(s_lam, 1)
            dve.wait_ge(s_lame, 1)
            link(tt(lams[:, 2:3], lams[:, 1:2], lams[:, 0:1], ALU.subtract))
            link(ts(lams[:, 3:4], lams[:, 2:3], -LAM_INIT, None, ALU.add))
            dve.wait_ge(s_qre, 16)
            dve.wait_ge(s_kso, 1)
            link(tt(qtok[0:NB, :], qtok[0:NB, :], kstok[0:NB, :], ALU.mult))
            link(dve.tensor_reduce(sn[0:NB, :], qtok[0:NB, :].rearrange("p (c n) -> p c n", n=DK), AX, ALU.add))
            dve.wait_ge(s_dc, 12)
            dve.wait_ge(s_kr, 4 + NB * PAGES)
            scf = sc.rearrange("p b g c -> p b (g c)")
            link(tt(scf[:, :, 0:256], scf[:, :, 0:256],
                    dbias.rearrange("p g c -> p (g c)").unsqueeze(1).to_broadcast([P, NB, 256]), ALU.add))
            link(tt(sc[0:NB, :, PAGES, :], sn[0:NB, :].unsqueeze(1).to_broadcast([NB, NB, 16]),
                    rowm[0:NB, :].unsqueeze(2).to_broadcast([NB, NB, 16]), ALU.add))
            by_head = sc.rearrange("p b g c -> p b c g")
            dm = lambda t: t.rearrange("p (b c) -> p b c", b=NB)
            dve.tensor_reduce(dm(dmx), by_head, AX, ALU.max).then_inc(s_dv, 1)
            dve.wait_ge(s_dp, 1)
            link(dve.tensor_reduce(dm1, ps[:, 0, 0:P], AX, ALU.max))
            ts(ddiag, ident, dm1[:, 0:1], -1.0, ALU.mult, ALU.mult).then_inc(s_dv, 1)
            dve.wait_ge(s_dp, 2)
            nb = dm(ps[:, 1, 0:P]).unsqueeze(2).to_broadcast([P, NB, PAGES + 1, 16])
            tt(sc, sc, nb, ALU.add).then_inc(s_dv, 1)
            dve.wait_ge(s_dex, 1)
            dve.tensor_reduce(dm(dmx), by_head, AX, ALU.add).then_inc(s_dv, 1)
            dve.wait_ge(s_dp, 3)
            link(dve.reciprocal(drc, ps[:, 2, 0:P]))
            odd = drc.rearrange("p (n c) -> p n c", c=2)[:, :, 1]
            link(ts(odd, odd, lams[:, 3:4], None, ALU.mult))
            link(tt(sc, sc, dm(drc).unsqueeze(2).to_broadcast([P, NB, PAGES + 1, 16]), ALU.mult))
            pair = sc.rearrange("p b g (h c) -> p (b g h) c", c=2)
            tt(wd.rearrange("p b g h -> p (b g h)"), pair[:, :, 0], pair[:, :, 1], ALU.add).then_inc(s_dv, 1)
            dve.wait_ge(s_dv, 5)
            dve.wait_ge(s_zout, 16 * 5)
            UN = NH * QB

            def biased(u):
                h, q = u // QB, u % QB
                n = (q + 1) * P
                if q == 0:
                    link(ts(alibi, dist, SLOPES[h] / SCALE, None, ALU.mult))
                if u >= 3:
                    dve.wait_ge(a_t, u - 2)
                x0 = 384 - q * P
                for c in range(2):
                    dve.wait_ge(a_s, 2 * u + c + 1)
                    dve.tensor_tensor_reduce(se[:, u % 3, c, 0:n], ps[:, (2 * u + c) % 3, 0:n],
                                             alibi[:, x0:x0 + n], 1.0, LOW, ALU.add, ALU.max,
                                             nmx[:, u % 3, c:c + 1]).then_inc(a_b, 1)
                dve.wait_ge(a_b, 2 * u + 2)
                ts(nmx[:, u % 3, :], nmx[:, u % 3, :], -SCALE, None, ALU.mult).then_inc(a_nm, 1)

            def inverse(u):
                dve.wait_ge(a_e, 2 * u + 2)
                link(dve.reciprocal(rsum[:, u % 3, :], sums[:, u % 3, :]))
                ts(rsum[:, u % 3, 1:2], rsum[:, u % 3, 1:2], lams[:, 3:4], None, ALU.mult).then_inc(a_rs, 1)

            def weights(u):
                n = (u % QB + 1) * P
                dve.wait_ge(a_e1, u + 1)
                stt_(se[:, u % 3, 0, 0:n], se[:, u % 3, 0, 0:n], rsum[:, u % 3, 0:1], se[:, u % 3, 1, 0:n],
                     ALU.mult, ALU.add).then_inc(a_w, 1)

            def place(n):
                if n >= 2:
                    dve.wait_ge(s_vu, 4 + 4 * (n - 1))
                p0 = 4 * (n % 4)
                dve.tensor_copy(zpad[:, n % 2, :, 56:64], wd[:, n // 4, p0:p0 + 4, :]).then_inc(s_wz, 1)

            link(dve.memset(zpad, 0.0))
            dve.tensor_copy(wnew[0:NB].rearrange("p (b h) -> p b h", h=NH), wd[0:NB, :, PAGES, :])\
                .then_inc(s_wz, 1)
            place(0)

            lo(SL_OUT)
            lo(SL_OUT + 1)

            def taps(j):
                dve.wait_ge(c_i, j + 1)
                for k in (2, 1, 0):
                    back = 3 - k
                    y_ = yb[:, j % 3, back:SEQ]
                    ins = stt_(y_, pj[:, TX + j, 0:SEQ - back], cwcol[:, k * CT + j:k * CT + j + 1], y_,
                               ALU.mult, ALU.add)
                    if k:
                        link(ins)
                    else:
                        ins.then_inc(c_v, 1)

            def silu(j):
                dve.wait_ge(c_p, j + 1)
                n = SEQ if j < CT else T
                e_ = eb[:, j % 2, 0:n]
                link(dve.reciprocal(e_, e_))
                if j < CT:
                    tt(pj[:, TX + j, 0:SEQ], yb[:, j % 3, 0:SEQ], e_, ALU.mult).then_inc(c_m, 1)
                else:
                    z_ = pj[:, TZ + j - CT, :]
                    tt(z_, z_, e_, ALU.mult).then_inc(c_m, 1)

            cw = cwcol.rearrange("p (j t) -> p t j", t=CT)
            xnew = pj[:, TX:TX + CT, SEQ:T]

            for s in range(UN + 2):
                if s < UN:
                    biased(s)
                if 1 <= s <= UN:
                    inverse(s - 1)
                if s >= 2:
                    weights(s - 2)
                if s + 1 < 4 * NB:
                    place(s + 1)
                if s == 3:
                    dve.wait_ge(s_out, 16 * 6)
                    dve.wait_ge(s_nv, 1)
                    link(tt(cs4, cst.rearrange("p t (b j) -> p t b j", j=3),
                            cw[:, :, 0:3].unsqueeze(2).to_broadcast([P, CT, NB, 3]), ALU.mult))
                    link(dve.tensor_reduce(csr, cs4, AX, ALU.add))
                    link(tt(csr, csr, gcol[:, G_CB:G_CB + CT].unsqueeze(2).to_broadcast([P, CT, NB]), ALU.add))
                    link(tt(xnew, xnew, cw[:, :, 3:4].to_broadcast([P, CT, NB]), ALU.mult))
                    tt(xnew, xnew, csr, ALU.add).then_inc(c_dv, 1)
                if s == 5:
                    dve.wait_ge(c_de, 1)
                    link(ts(csr, csr, 3.0e38, 1.0, ALU.min, ALU.add))
                    link(dve.reciprocal(csr, csr))
                    link(tt(xnew, xnew, csr, ALU.mult))
                if 4 <= s < CT + 4:
                    taps(s - 4)
                if 6 <= s < JOBS + 6:
                    silu(s - 6)
            dve.wait_ge(s_vu, 4 + NB * PAGES)
            dve.tensor_copy(oacc[0:64].rearrange("p (f n) -> p f n", f=2), ps[0:64, 6:8, :]).then_inc(s_dor, 1)
            dve.wait_ge(s_dos, 1)
            dve.wait_ge(a_oc, NH)
            dve.tensor_copy(pj[:, TQ:TQ + NH, SEQ:T],
                            ps[:, 7, 0:64].rearrange("p (h b) -> p h b", h=NH)).then_inc(s_dor, 1)
            X, E, U, L, M = [v[0:NSH] for v in sp5]
            link(ts(X, dtt[0:NSH], hcol[0:NSH, 0:1], None, ALU.add))
            stt_(E, X, -1.0, X, ALU.mult, ALU.max).then_inc(d_v, 1)
            dve.wait_ge(d_s, 2)
            ts(U, E, 1.0, None, ALU.add).then_inc(d_v, 1)
            dve.wait_ge(d_s, 3)
            link(ts(U, U, -1.0, None, ALU.add))
            link(ts(M, U, 0.0, None, ALU.is_equal))
            link(tt(U, U, M, ALU.add))
            link(tt(L, L, M, ALU.add))
            link(dve.reciprocal(U, U))
            link(tt(L, L, U, ALU.mult))
            link(tt(L, L, E, ALU.mult))
            link(stt_(dtt[0:NSH], X, 0.0, L, ALU.max, ALU.add))
            link(ts(hcol[0:NSH, 2:3], hcol[0:NSH, 2:3], -1.0, None, ALU.mult))
            ts(M, dtt[0:NSH], hcol[0:NSH, 2:3], None, ALU.mult).then_inc(d_v, 1)
            dve.wait_ge(d_v, 3)
            link(dve.memset(U, 1.0))
            for c in range(QB):
                link(dve.tensor_tensor_scan(acs[0:NSH, c * P:(c + 1) * P], U[:, c * P:(c + 1) * P],
                                            M[:, c * P:(c + 1) * P], 0.0, ALU.mult, ALU.add))
            link(dve.tensor_copy(ecat[0:NSH, NB:2 * NB], dtt[0:NSH, SEQ:T]))
            dve.tensor_copy(ecat[0:NSH, 16:17], hcol[0:NSH, 3:4]).then_inc(d_v, 1)
            dve.wait_ge(e_t, 1)
            dve.tensor_copy(dtk, ps[:, 0, 0:64].rearrange("p (c h) -> p c h", h=NSH)).then_inc(e_c, 1)
            dve.tensor_copy(ack, ps[:, 0, 64:128].rearrange("p (c h) -> p c h", h=NSH)).then_inc(e_c, 1)
            dve.wait_ge(e_t, 3)
            dve.wait_ge(e_dx, 1)
            dve.tensor_copy(ecol, ps[:, 1, 0:136].rearrange("p (t n) -> p t n", n=17)).then_inc(e_c, 1)
            dve.wait_ge(e_c, 2)
            tt(dsk, ps[:, 1, 256:320].rearrange("p (h c) -> p c h", c=QB), ack, ALU.subtract).then_inc(e_c, 1)
            dve.wait_ge(e_c, 4)
            tt(xdt, pj[:, CX:CX + 8, SEQ:T], ecol[:, :, NB:2 * NB], ALU.mult).then_inc(g_xd, 1)
            for t in range(8):
                dve.wait_ge(e_xt, t + 1)
                tt(xd[:, :, t * P:(t + 1) * P].rearrange("p c (h n) -> p c h n", h=2),
                   ps[:, 2 + t % 2, :].rearrange("p (c h n) -> p c h n", c=QB, h=2),
                   dtk[:, :, 2 * t:2 * t + 2].unsqueeze(3).to_broadcast([P, QB, 2, HD]), ALU.mult)\
                    .then_inc(e_xd, 1)
            for g in range(2):
                dve.wait_ge(e_cb, g + 1)
                dve.tensor_copy(cbt[:, g], ps[:, 4 + g, :].rearrange("p (c n) -> p c n", c=QB)).then_inc(e_cbc, 1)
            for c in range(QB):
                src = ps[:, 2 * (c % 2):2 * (c % 2) + 2, :]
                dst = sall[:, c].rearrange("p (b n) -> p b n", b=2)
                dve.wait_ge(e_st, c + 1)
                if c == 0:
                    dve.tensor_copy(dst, src).then_inc(e_sc, 1)
                else:
                    dve.wait_ge(e_sm, c)
                    tt(dst, dst, src, ALU.add).then_inc(e_sc, 1)
            for s in range(NSH + 2):
                if s < NSH:
                    h = s
                    dve.wait_ge(f_a, h + 1)
                    if h >= 2:
                        dve.wait_ge(f_y, h - 1)
                    for c in range(QB):
                        ins = stt_(dl[:, h % 2, c], ps[:, 4 + h % 2, c * P:(c + 1) * P], ack[:, c, h:h + 1],
                                   causal, ALU.subtract, ALU.add)
                    ins.then_inc(f_d, 1)
                if s % 2 == 1 and s >= 3:
                    t = (s - 3) // 2
                    dve.wait_ge(f_y, 2 * t + 2)
                    stt_(pj[:, TY + t, 0:SEQ], pj[:, CX + t, 0:SEQ], ecol[:, t, 16:17], ps[:, 2 + t % 2, :],
                         ALU.mult, ALU.add).then_inc(f_yc, 1)
                if s % 2 == 1 and s < NSH:
                    t = s // 2
                    dve.wait_ge(g_in[t % 2], 16 * (t // 2 + 1))
                    link(tt(stt[:, t % 2], stt[:, t % 2],
                            ecol[:, t, 0:NB].unsqueeze(2).to_broadcast([P, NB, NS]), ALU.mult))
                    dve.wait_ge(g_b, t + 1)
                    tt(stt[:, t % 2], stt[:, t % 2], bx, ALU.add).then_inc(g_n, 1)
                if s % 2 == 0 and s >= 2:
                    t = s // 2 - 1
                    dve.wait_ge(g_c, t + 1)
                    dve.tensor_reduce(ysd[:, t], bx, AX, ALU.add).then_inc(g_r, 1)
                    dve.wait_ge(z_rt, t + 1)
                    link(dve.reciprocal(tmp[:, t % 2], tmp[:, t % 2]))
                    o_ = pj[:, TQ + t, :]
                    stt_(o_, o_, gcol[:, G_SUB:G_SUB + 1], tmp[:, t % 2], ALU.mult, ALU.mult).then_inc(z_o, 1)
            dsx = xdt
            dve.wait_ge(g_r, 8)
            link(tt(dsx, pj[:, CX:CX + 8, SEQ:T], ecol[:, :, 16:17].to_broadcast([P, 8, NB]), ALU.mult))
            tt(pj[:, TY:TY + 8, SEQ:T], dsx, ysd, ALU.add).then_inc(g_y, 1)
            for t in range(NH):
                if t == NH - 1:
                    dve.wait_ge(s_out, 16 * 7)
                dve.wait_ge(z_h, t + 1)
                tt(ul[:, t], pj[:, TQ + t, :], uh[:, t].bitcast(F32), ALU.subtract).then_inc(z_l, 1)
            dve.wait_ge(z_rt, NH + 2)
            for g in range(2):
                link(dve.reciprocal(tmp[:, g], tmp[:, g]))
            for t in range(8 + 1):
                if t < 8:
                    y_ = pj[:, TY + t, :]
                    stt_(y_, y_, gcol[:, G_SSM + t:G_SSM + t + 1], tmp[:, t // 4], ALU.mult, ALU.mult)\
                        .then_inc(z_o, 1)
                if t >= 1:
                    dve.wait_ge(z_h, NH + t)
                    tt(ul[:, 7 + t], pj[:, TY + t - 1, :], uh[:, 7 + t].bitcast(F32), ALU.subtract)\
                        .then_inc(z_l, 1)
            for k in range(2):
                dve.wait_ge(h_pc, 2 * k + 2)
                tt(pl[:, k, 0:SEQ], ps[:, 2 * k, :], ph[:, k, 0:SEQ].bitcast(F32), ALU.subtract).then_inc(h_pl, 1)
                tt(pl[:, k, SEQ:T], ps[:, 2 * k + 1, 0:NB], ph[:, k, SEQ:T].bitcast(F32), ALU.subtract)\
                    .then_inc(h_pl, 1)
            for g in range(8):
                for j in range(4):
                    lo(SL_OUT + 2 + 4 * g + j)
                dve.wait_ge(w_used, SL_OUT + 4 * (g + 1) + 2)
                dve.tensor_copy(hT[:, 2 * g:2 * g + 2].rearrange("p m (h n) -> p m h n", h=2),
                                group_view(G_OUT + g)).then_inc(h_e, 1)
                dve.wait_ge(h_e, g + 1)
                dve.sem_inc(group_free, 1)
            for k in range(KT):
                dve.wait_ge(s_uh, KT + k + 1)
                stt_(ul[:, k], hT[:, k], gcol[:, G_FFN + k:G_FFN + k + 1], uh[:, k].bitcast(F32),
                     ALU.mult, ALU.subtract).then_inc(s_ul, 1)
            dve.wait_ge(h_rt, 1)
            link(dve.reciprocal(rstd, rstd))
            dve.sem_inc(m_l, 1)

            def relu(n, g, c, per_n, per_c, i):
                dve.wait_ge(w_used, at(n, per_n, i))
                for m in range(2):
                    stt_(halves(tm[:, m]), bank_view(g, m), 0.0, halves(rstd), ALU.max, ALU.mult)\
                        .then_inc(m_t, 1)
                dve.wait_ge(m_t, at(2 * c + 2, 2 * per_c, i))
                dve.sem_inc(group_free, 1)

            def hidden_lo(c, per_c, i, slot, m):
                dve.wait_ge(m_q, at(c + 1, per_c, i))
                tt(hl[:, slot, 2 * m:2 * m + 2], sq, hh[:, slot, 2 * m:2 * m + 2].bitcast(F32), ALU.subtract)\
                    .then_inc(m_l, 1)

            def up(n, g, c, per_n, per_c, i, slot):
                for m in range(2):
                    for j in range(1, 4):
                        lo(n + 4 * m + j, per_n, i)
                    relu(n + 4 * m + 4, g + m, c + m, per_n, per_c, i)
                    lo(n + 4 * m + 4, per_n, i)
                    hidden_lo(c + m, per_c, i, slot, m)

            def down_add(n, g, j, per_n, i):
                dve.wait_ge(w_used, at(n + j + 1, per_n, i))
                x_ = hT[:, 2 * j:2 * j + 2].rearrange("p m (h n) -> p m h n", h=2)
                tt(x_, x_, group_view(g + j), ALU.add).then_inc(group_free, 1)

            def down(n, g, per_n, i):
                for j in range(8):
                    down_add(n, g, j, per_n, i)
                    lo(n + j + 1, per_n, i)

            b = SL_MLP + 2
            lo(b)
            up(b, G_MLP, 0, 0, 0, None, 0)
            with dve.Fori(0, (CHUNKS - 2) // 2) as i:
                g = G_MLP + 2
                up(b + 8, g, 2, 32, 4, i, 1)
                down(b + 16, g + 2, 32, i)
                up(b + 24, g + 10, 4, 32, 4, i, 0)
                down(b + 32, g + 12, 32, i)
            g = G_PLE - 18
            up(SL_PLE - 22, g, 2 * CHUNKS - 2, 0, 0, None, 1)
            down(SL_PLE - 14, g + 2, 0, None)
            for j in range(8):
                down_add(SL_PLE - 6, g + 10, j, 0, None)
                if j < 7:
                    lo(SL_PLE - 6 + j + 1)
            dve.wait_ge(group_free, G_PLE + 2)
            dve.sem_inc(h_e, 8 * CHUNKS)
            for g in range(8):
                lo(SL_PLE + 2 + g)
                dve.wait_ge(s_uh, 2 * KT + g + 1)
                tt(ul[:, 2 * g:2 * g + 2], hT[:, 2 * g:2 * g + 2], uh[:, 2 * g:2 * g + 2].bitcast(F32),
                   ALU.subtract).then_inc(s_ul, 1)
                dve.wait_ge(w_used, SL_PLE + g + 3)
                dve.tensor_copy(eT[:, 2 * g:2 * g + 2].rearrange("p m (h n) -> p m h n", h=2),
                                group_view(G_PLE + g)).then_inc(p_e, 1)
                dve.wait_ge(p_e, g + 1)
                dve.sem_inc(group_free, 1)
            dve.wait_ge(h_rt, 2)
            link(dve.reciprocal(rstd, rstd))
            for k in range(KT):
                ins = stt_(eT[:, k], eT[:, k], gcol[:, G_PLN + k:G_PLN + k + 1], rstd, ALU.mult, ALU.mult)
                link(ins)
                if k == 3:
                    lo(SL_GATE + 2)
                if k == 11:
                    lo(SL_GATE + 3)
            dve.sem_inc(x_h, 1)

            def gate(c, per, i):
                dve.wait_ge(w_used, at(SL_GATE + 4 * (c + 1) + 2, 4 * per, i))
                dve.wait_ge(x_h, at(c + 1, per, i))
                ts(tm.rearrange("p m (h n) -> p m h n", h=2), group_view(G_GATE + c), -87.0, None, ALU.max)\
                    .then_inc(x_c, 1)
                dve.wait_ge(x_c, at(c + 1, per, i))
                dve.sem_inc(group_free, 1)
                dve.wait_ge(x_p, at(c + 1, per, i))
                dve.reciprocal(tm, tm).then_inc(x_r, 1)

            def gate_add(c, per, i):
                dve.wait_ge(x_m, at(c + 1, per, i))
                x_ = hT[:, bass.ds(at(2 * c, 2 * per, i), 2), :] if i is not None else hT[:, 2 * c:2 * c + 2, :]
                tt(x_, x_, tm, ALU.add).then_inc(x_h, 1)

            lo(SL_GATE + 4)
            lo(SL_GATE + 5)
            with dve.Fori(0, 3) as i:
                for m in range(2):
                    gate(m, 2, i)
                    lo(SL_GATE + 6 + 4 * m, 8, i)
                    gate_add(m, 2, i)
                    for j in range(1, 4):
                        lo(SL_GATE + 6 + 4 * m + j, 8, i)
            for m in range(2):
                gate(6 + m, 0, None)
                if m == 0:
                    lo(SL_ALL - 2)
                gate_add(6 + m, 0, None)
                if m == 0:
                    lo(SL_ALL - 1)
            dve.wait_ge(h_rt, 3)
            link(dve.reciprocal(rstd, rstd))
            for k in range(KT):
                stt_(hT[:, k], hT[:, k], gcol[:, G_FIN + k:G_FIN + k + 1], rstd, ALU.mult, ALU.mult)\
                    .then_inc(y_s, 1)
            for q in range(QB + 1):
                for r in (1, 3):
                    u = 4 * q + r
                    dve.wait_ge(y_t, u + 1)
                    dst = yt[:, q, r * 512:(r + 1) * 512] if q < QB else ys[0:NB, r * 512:(r + 1) * 512]
                    src = ps[:, 2 + u % 6, :] if q < QB else ps[0:NB, 2 + u % 6, :]
                    dve.tensor_copy(dst, src).then_inc(y_d, 1)


INPUTS = ["x_prompt", "x_sample", "p_prompt", "p_sample", "cache_k", "cache_v", "page_table", "state_ssm",
          "state_conv", "g_mix", "w_in", "lambda_q1", "lambda_k1", "lambda_q2", "lambda_k2", "w_subln",
          "conv_w", "conv_b", "dt_bias", "a_log", "d_skip", "w_ssm_norm", "w_out", "g_ffn", "w_up",
          "w_down", "w_ple", "w_ple_norm", "w_ple_gate", "g_final"]
OUTPUTS = [("y_prompt", (1, SEQ, D_MODEL)), ("y_sample", (NB, 1, D_MODEL)),
           ("k_prompt", (1, 1, SEQ, NH, P)), ("v_prompt", (1, 1, SEQ, NH, P)),
           ("ssm_prompt", (1, 1, NSH, HD, NS)), ("conv_prompt", (1, 1, CW - 1, CONV_DIM)),
           ("k_sample", (1, NB, 1, NH, P)), ("v_sample", (1, NB, 1, NH, P)),
           ("ssm_sample", (1, NB, NSH, HD, NS)), ("conv_sample", (1, NB, CW - 1, CONV_DIM))]


def kernel(**inputs):
    import numpy as np
    import concourse.bacc as bacc
    from concourse.bass_utils import run_bass_kernel_spmd

    nc = bacc.Bacc("TRN2", target_bir_lowering=False, num_devices=1)
    arrays, ins, outs = {}, {}, {}
    for name in INPUTS:
        a = np.ascontiguousarray(inputs[name])
        arrays[f"in_{name}"] = a
        ins[name] = nc.dram_tensor(f"in_{name}", a.shape, mybir.dt.from_np(a.dtype), kind="ExternalInput").ap()
    for name, shape in OUTPUTS:
        outs[name] = nc.dram_tensor(f"out_{name}", shape, F32, kind="ExternalOutput").ap()
    build(nc, ins, outs)
    r = run_bass_kernel_spmd(nc, [arrays], core_ids=[0])
    return tuple(r.results[0][f"out_{name}"] for name, _ in OUTPUTS)
```

```python
from contextlib import ExitStack

import concourse.bass as bass
from concourse import mybir

F32 = mybir.dt.float32
F32R = mybir.dt.float32r
I32 = mybir.dt.int32
ALU = mybir.AluOpType
ACT = mybir.ActivationFunctionType
AX = mybir.AxisListType.X

P = 128
D_MODEL = 2048
KT = D_MODEL // P
SEQ = 512
NB = 8
T = SEQ + NB
HALF = T // 2
QB = SEQ // P
PAST = 2048
PAGES = PAST // P
POOL = NB * PAGES + NB * PAGES // 4
AW = 1024
NH = 8
DK = 64
SCALE = DK ** -0.5
SLOPES = [2.0 ** -(h + 1) for h in range(NH)]
LAM_INIT = 0.2
NSH = 16
HD = 64
NS = 128
CONV_DIM = 1536
CW = 4
CT = CONV_DIM // P
D_PROJ = 3 * AW + 1024 + CONV_DIM + NSH
D_FF = 4 * D_MODEL
CHUNKS = D_FF // 512
PLE = 256
EPS = 1e-6
EPS_SUB = 1e-5
NEG = -1.0e30
LOW = -3.0e38

TQ, TK, TV, TX = 0, 8, 16, 24
TB_, TC_ = 8, 10
CX = TX
TZ = 16
TY = 8
JOBS = CT + 8
PT = 36

SL_DT = 4 * 22
SL_OUT = SL_DT + 2
SL_MLP = SL_OUT + 32
SL_PLE = SL_MLP + 16 * CHUNKS
SL_GATE = SL_PLE + 8
SL_ALL = SL_GATE + 32
G_DT = 22
G_OUT = 23
G_MLP = G_OUT + 8
G_PLE = G_MLP + 10 * CHUNKS
G_GATE = G_PLE + 8


def at(c, k, i):
    return c if i is None else i * k + c


class Chain:

    def __init__(self, eng, sem):
        self.eng, self.sem, self.n = eng, sem, 0

    def __call__(self, ins):
        ins.then_inc(self.sem, 1)
        self.n = self.n + 1
        self.eng.wait_ge(self.sem, self.n)


def build(nc, d, d_out):
    ctx = ExitStack()
    with ctx:
        base = (nc.sbuf_base + 31) // 32 * 32
        sizes = [("RAW", 8192), ("WH", 8192), ("WL", 8192), ("UH", 33280), ("UL", 33280),
                 ("PJ", PT * T * 4), ("XX", 37504), ("CC", 9216)]
        off, pos = {}, base
        for name, n in sizes:
            off[name] = pos
            pos += n

        def sb(name, shape, dt, where, delta=0):
            return nc.alloc_sbuf_tensor_at(name, [P] + shape, dt, offset=off[where] + delta)[:]

        raw = sb("raw", [2, 1024], F32, "RAW")
        wh = sb("wh", [2, 1024], F32R, "WH")
        wl = sb("wl", [2, 1024], F32R, "WL")
        uh = sb("uh", [KT, T], F32R, "UH")
        ul = sb("ul", [KT, T], F32R, "UL")
        pj = sb("pj", [PT, T], F32, "PJ")
        G_MIX, G_FFN, G_PLN, G_SSM, G_SUB, G_CB = 0, 16, 32, 48, 56, 57
        cpos = [0]

        def const(name, shape, dt=F32):
            n = 4
            for s in shape:
                n *= s
            t = sb(name, shape, dt, "CC", cpos[0])
            cpos[0] += (n + 31) // 32 * 32
            assert cpos[0] <= 9216, cpos
            return t

        ident = const("ident", [P])
        ones = const("ones", [P])
        causal = const("causal", [P])
        rstd = const("rstd", [T])
        gcol = const("gcol", [G_CB + CT])
        cwcol = const("cwcol", [CW * CT])
        cst = const("cst", [CT, NB * 3])
        dtt = const("dtt", [T])
        lamc = const("lamc", [4, DK])
        lams = const("lams", [8])
        epsc = const("epsc", [2])
        ssx = const("ssx", [8])
        hcol = const("hcol", [4])
        rowm = const("rowm", [NB])
        nmx = const("nmx", [3, 2])
        sums = const("sums", [3, 2])
        ptab = const("ptab", [NB * PAGES], I32)
        rsum = const("rsum", [3, 2])
        xt = sb("xt", [QB, D_MODEL], F32, "PJ")
        xs = sb("xs", [D_MODEL], F32, "PJ", 32768)
        junk = sb("junk", [D_MODEL], F32, "XX")
        rdiag = sb("rdiag", [QB, P], F32, "XX", 8192)
        grow = sb("grow", [P], F32, "XX", 16384)
        cwrow = sb("cwrow", [P], F32, "XX", 16896)
        cstrow = sb("cstrow", [CONV_DIM], F32, "XX", 17408)
        kpage = sb("kpage", [4, AW], F32, "XX")
        sc = sb("sc", [NB, PAGES + 1, 16], F32, "XX", 16384)
        qbc = sb("qbc", [2, AW], F32, "XX", 25088)
        zst = sb("zst", [2, T], F32, "XX", 33280)
        qtok1 = sb("qtok1", [AW], F32, "XX", 33280)
        xsg = sb("xsg", [KT, NB], F32, "XX", 24576)
        vpage = sb("vpage", [4, AW], F32, "XX")
        se = sb("se", [3, 2, SEQ], F32, "XX", 20480)
        ktok = sb("ktok", [QB, AW], F32, "UH")
        wt = sb("wt", [2, QB, SEQ], F32, "UH")
        vtok = sb("vtok", [QB, AW], F32, "UH", 16384)
        qtok = sb("qtok", [AW], F32, "UH", 32768)
        kstok = sb("kstok", [AW], F32, "UH", 36864)
        vstok = sb("vstok", [AW], F32, "UH", 40960)
        xbtok = sb("xbtok", [CONV_DIM], F32, "UH", 45056)
        dist = sb("dist", [896], F32, "UH", 51200)
        alibi = sb("alibi", [896], F32, "UH", 54784)
        wd = sb("wd", [NB, PAGES + 1, NH], F32, "UH", 58368)
        dbias = sb("dbias", [PAGES, 16], F32, "UH", 62720)
        dmx = sb("dmx", [P], F32, "UH", 63744)
        ddiag = sb("ddiag", [P], F32, "UH", 64256)
        drc = sb("drc", [P], F32, "UH", 64768)
        ddist = sb("ddist", [PAGES], F32, "UH", 65280)
        dm1 = sb("dm1", [1], F32, "UH", 65344)
        sn = sb("sn", [16], F32, "UH", 65376)
        bcb = sb("bcb", [4, NB, NS], F32, "XX")
        stt = sb("stt", [2, NB, NS], F32, "XX", 16384)
        bx = sb("bx", [NB, NS], F32, "XX", 24576)
        tmp = sb("tmp", [2, T], F32, "XX", 28672)
        acs = sb("acs", [SEQ], F32, "XX", 32832)
        mpos = [34880]

        def misc(name, shape):
            n = 4
            for s in shape:
                n *= s
            t = sb(name, shape, F32, "XX", mpos[0])
            mpos[0] += (n + 31) // 32 * 32
            assert mpos[0] <= 37376
            return t

        dtk = misc("dtk", [QB, NSH])
        ack = misc("ack", [QB, NSH])
        dsk = misc("dsk", [QB, NSH])
        decb = misc("decb", [NSH, QB])
        ecol = misc("ecol", [8, 17])
        ecat = misc("ecat", [17])
        xdt = misc("xdt", [8, NB])
        ysd = misc("ysd", [8, NB])
        bcrow = sb("bcrow", [4, NS], F32, "XX", 24576)
        xd = sb("xd", [QB, AW], F32, "UH")
        xdd = sb("xdd", [QB, AW], F32, "UH", 16384)
        sall = sb("sall", [QB, AW], F32, "UH", 32768)
        btok = sb("btok", [QB, 2, NS], F32, "UH", 49152)
        cbt = sb("cbt", [2, QB, P], F32, "UH", 53248)
        dl = [sb(f"dl{i}", [QB, P], F32, w, o) for i, (w, o) in
              enumerate((("UH", 57344), ("UH", 59392), ("XX", 28672)))]
        cd = [sb(f"cd{i}", [QB, P], F32, w, o) for i, (w, o) in
              enumerate((("UH", 61440), ("UH", 63488), ("XX", 30720)))]
        fst = sb("fst", [8, NS], F32, "UH", 49152)
        zpad = sb("zpad", [2, 4, 120], F32, "XX", 16384)
        wnew = sb("wnew", [64], F32, "XX", 20224)
        oacc = sb("oacc", [AW], F32, "XX", 16384)
        yb = sb("yb", [3, T], F32, "UH", 32768)
        eb = sb("eb", [2, T], F32, "UH", 39008)
        hq = sb("hq", [SEQ], F32, "UH", 43168)
        sp5 = [sb(f"sp{i}", [T], F32, "UH", 32768 + 2080 * i) for i in range(5)]
        cs4 = sb("cs4", [CT, NB, 3], F32, "UH", 43168)
        csr = sb("csr", [CT, NB], F32, "UH", 44320)
        hT = pj[:, 0:KT, :]
        eT = pj[:, KT:2 * KT, :]
        xt3 = sb("xt3", [QB, D_MODEL], F32, "PJ", KT * T * 4)
        xs3 = sb("xs3", [D_MODEL], F32, "PJ", 2 * KT * T * 4)
        yt = sb("yt", [QB, D_MODEL], F32, "PJ", KT * T * 4)
        ys = sb("ys", [D_MODEL], F32, "PJ", 2 * KT * T * 4)
        hh = sb("hh", [2, 4, T], F32R, "PJ", KT * T * 4)
        hl = sb("hl", [2, 4, T], F32R, "PJ", (KT + 8) * T * 4)
        sq = sb("sq", [2, T], F32, "XX")
        tm = sb("tm", [2, T], F32, "XX", 4160)
        acc = sb("acc", [T], F32, "XX", 8320)
        ph = sb("ph", [2, T], F32R, "XX", 10400)
        pl = sb("pl", [2, T], F32R, "XX", 14560)
        ptok = sb("ptok", [QB, PLE], F32, "XX", 18720)
        pstok = sb("pstok", [PLE], F32, "XX", 22816)
        gfin = sb("gfin", [D_MODEL], F32, "XX", 10400)
        ps = ctx.enter_context(nc.psum_tensor("ps", [P, 8, 512], F32))


        q_scr = nc.dram_tensor("q_scr", (NB, AW), F32, kind="Internal").ap()
        z_scr = nc.dram_tensor("z_scr", (8, P, T), F32, kind="Internal").ap()
        bc_scr = nc.dram_tensor("bc_scr", (NB, 4, NS), F32, kind="Internal").ap()

        names = {}

        def sem(name):
            names[name] = ctx.enter_context(nc.semaphore(name))
            return names[name]

        raw_landed = [sem("raw_landed0"), sem("raw_landed1")]
        hi_ready, lo_ready, w_used = sem("hi_ready"), sem("lo_ready"), sem("w_used")
        group_free = sem("group_free")
        dve_step, act_step, pool_step = sem("dve_step"), sem("act_step"), sem("pool_step")
        s_x = sem("x_landed")
        s_xs, s_small = sem("xs_landed"), sem("small_landed")
        s_const, s_gt, s_gc = sem("consts_ready"), sem("gain_turned"), sem("gain_copied")
        s_ss, s_rt = sem("squares_summed"), sem("rstd_by_token")
        s_rb, s_rd = sem("rstd_spread"), sem("rstd_copied")
        s_xT, s_uh, s_ul = sem("x_turned"), sem("u_hi"), sem("u_lo")
        s_xsT, s_us = sem("xs_turned"), sem("us_done")
        s_qt, s_qtc, s_qscr, s_qbc = sem("q_turned"), sem("q_rows"), sem("q_stored"), sem("q_spread")
        s_pt = sem("page_table_landed")
        s_kp = [sem(f"k_landed{i}") for i in range(4)]
        s_km, s_kr = sem("k_multiplied"), sem("k_reduced")
        s_zst, s_zout = sem("z_staged"), sem("z_stored")
        s_kt, s_vt, s_kto, s_vto = sem("k_turned"), sem("v_turned"), sem("k_rows"), sem("v_rows")
        s_rt3 = sem("rows_turned")
        s_kso, s_vso = sem("ks_rows"), sem("vs_xb_rows")
        s_out = sem("outputs_stored")
        s_kst_out = sem("k_prompt_stored")
        s_qre = sem("q_reloaded")
        s_dc = sem("dist_ready")
        s_dv, s_dp, s_dex = sem("dec_vector_steps"), sem("dec_tensor_steps"), sem("dec_exp")
        s_vp = [sem(f"v_landed{i}") for i in range(4)]
        s_vu, s_wz = sem("v_used"), sem("page_weights_placed")
        s_nv = sem("new_values_added")
        s_dos, s_dor = sem("dec_out_selected"), sem("dec_out_copied")
        s_lam, s_lame = sem("lam_products"), sem("lam_exp")
        a_s, a_b, a_nm, a_e = sem("scores"), sem("biased"), sem("neg_max"), sem("exp_done")
        a_rs, a_e1, a_w, a_t = sem("inv_sum"), sem("second_scaled"), sem("weights"), sem("w_turned")
        a_wt, a_o, a_oc = sem("w_turned_copied"), sem("attn_out"), sem("attn_out_copied")
        n_q, n_s, n_rt, n_o = sem("head_sq"), sem("head_sum"), sem("head_root"), sem("head_normed")
        c_dv, c_de = sem("conv_dec_sum"), sem("conv_dec_exp")
        c_i, c_v, c_e, c_p, c_m = (sem("conv_first"), sem("conv_sum"), sem("conv_exp"),
                                  sem("conv_plus"), sem("conv_act"))
        d_v, d_s = sem("dt_vector_steps"), sem("dt_scalar_steps")
        e_t, e_c, e_dx = sem("turned_steps"), sem("copied_steps"), sem("decay_exp_states")
        e_xt, e_xd, e_xdd = sem("x_rows_turned"), sem("x_rows"), sem("x_rows_decayed")
        e_bc, e_cb, e_cbc = sem("b_rows"), sem("cb_product"), sem("cb_copied")
        e_st, e_sm, e_sc = sem("states"), sem("state_decayed"), sem("state_ready")
        f_a, f_d, f_e, f_c = sem("acs_spread"), sem("seg"), sem("seg_exp"), sem("acs_exp")
        f_m, f_cm, f_y, f_yc = sem("mask_product"), sem("c_decayed"), sem("y_product"), sem("y_ready")
        f_ft, f_fc = sem("final_turned"), sem("final_copied")
        g_bc, g_bs, g_bb = sem("bc_rows"), sem("bc_stored"), sem("bc_spread")
        g_xd = sem("x_dt")
        g_in = [sem("st_landed0"), sem("st_landed1")]
        g_b, g_n, g_c, g_r = (sem("b_times_x"), sem("st_new"), sem("st_times_c"),
                                  sem("st_reduced"))
        g_out = [sem("st_stored0"), sem("st_stored1")]
        z_in, g_y, z_y = sem("z_landed"), sem("dec_y_ready"), sem("gated")
        z_q, z_s, z_rt, z_o, z_h, z_l = (sem("gated_sq"), sem("gated_sum"), sem("gated_rms"),
                                        sem("gated_norm"), sem("mix_hi"), sem("mix_lo"))
        h_x, h_p, h_pt, h_pc = sem("x3_landed"), sem("p_landed"), sem("p_turned"), sem("p_hi")
        h_pl = sem("p_lo")
        h_e, h_q, h_a = sem("h_ready"), sem("sq_ready"), sem("sq_added")
        h_s, h_rt = sem("norm_sum"), sem("norm_root")
        m_t, m_q, m_l = sem("relu_scaled"), sem("hidden_hi"), sem("hidden_lo")
        p_e = sem("e_ready")
        x_c = sem("gate_clamped")
        x_e, x_p, x_r, x_m, x_h = (sem("gate_exp"), sem("gate_plus"), sem("gate_recip"),
                                  sem("gate_times_e"), sem("h_final"))
        y_g, y_s, y_t, y_c = sem("gfin_landed"), sem("y_rstd"), sem("y_turned"), sem("y_copied_act")
        y_p, y_d = sem("y_gained_pool"), sem("y_copied_dve")
        Y_BANKS = (4, 5, 6, 7, 1, 2, 3)

        def y_quarter(u):
            q, r_ = u // 4, u % 4
            n = P if q < QB else NB
            dst = yt[:, q] if q < QB else ys[0:NB]
            c0, c1 = r_ * 512, (r_ + 1) * 512
            return ps[0:n, Y_BANKS[u % 7], :], dst[:, c0:c1], ssx[0:n, q:q + 1], gfin[0:n, c0:c1]

        y_out = sem("y_stored")

        block = ctx.enter_context(nc.Block())

        def wcols(w, row, col, rows=512, cols=256):
            return w[bass.ds(row, rows), bass.ds(col, cols)].rearrange("(k p) n -> p k n", p=P)

        w_in, w_out, w_up, w_down = d["w_in"][0], d["w_out"][0], d["w_up"][0], d["w_down"][0]
        w_ple, w_gate = d["w_ple"][0], d["w_ple_gate"][0]
        halves = lambda ap: ap.rearrange("p (h n) -> p h n", h=2)
        GB = [0, 4]

        def bank_view(g, m):
            b = GB[g % 2] + 2 * m
            return ps[:, b:b + 2, 0:HALF]

        def group_view(g):
            b = GB[g % 2]
            return ps[:, b:b + 4, 0:HALF].rearrange("p (m h) n -> p m h n", h=2)

        @block.sync
        def _(sp):
            for q in range(QB):
                sp.dma_start(xt[:, q, :], d["x_prompt"][0, q * P:(q + 1) * P, :]).then_inc(s_x, 16)
            sp.dma_start(xs[0:NB, :], d["x_sample"][:, 0, :]).then_inc(s_xs, 16)

            def load(src, c, per=0, i=None, elems=1024, k=4):
                sp.wait_ge(lo_ready, at(c + 1, per, i))
                dst = raw[:, c % 2, 0:elems].rearrange("p (k n) -> p k n", k=k)
                sp.dma_start(dst, src).then_inc(raw_landed[c % 2], 16)

            def load_in(c, i=None, per=8):
                g, k = c // 4, c % 4
                load(wcols(w_in, 512 * k, at(256 * g, 64 * per, i)), c, per, i)

            def pages(c, i):
                for pg in range(2 * c, 2 * c + 2):
                    idx = sp.value_load(ptab[0:1, bass.ds(at(pg, 32, i), 1)], min_val=0, max_val=POOL - 1)
                    sp.wait_ge(s_kr, at(pg + 1, 32, i))
                    sp.dma_start(kpage[:, pg % 4, :], d["cache_k"][0][bass.ds(idx, 1)]
                                 .rearrange("o t h d -> (o t) (h d)")).then_inc(s_kp[pg % 4], 16)

            def spread_q(b, i):
                if b:
                    sp.wait_ge(s_km, at(16 * (b - 1) + 1, 32, i))
                sp.dma_start(qbc[:, b % 2], q_scr[bass.ds(at(b, 2, i), 1), :].to_broadcast([P, AW]))\
                    .then_inc(s_qbc, 16)

            sp.dma_start(ptab[0:1, :], d["page_table"].rearrange("b g -> (b g)").unsqueeze(0)).then_inc(s_pt, 16)
            for c in range(4):
                load_in(c)
            sp.wait_ge(s_pt, 16)
            with sp.Fori(0, 2) as i:
                for j in range(8):
                    load_in(4 + j, i)
            sp.wait_ge(s_qscr, 16)
            spread_q(0, None)
            pages(0, None)
            with sp.Fori(0, 3) as i:
                for j in range(16):
                    if j % 8 == 4:
                        spread_q(j // 8 + 1, i)
                    pages(j + 1, i)
                    load_in(20 + j, i, 16)
            for j in range(48, 64):
                if j == 52:
                    spread_q(7, None)
                if j < 63:
                    pages(j + 1, None)
                load_in(20 + j)
            for c in range(84, SL_DT):
                load_in(c)
            for c in range(2):
                sp.wait_ge(lo_ready, SL_DT + c + 1)
                sp.dma_start(raw[:, c % 2, :].rearrange("p (k n) -> p k n", k=8)[:, :, 0:NSH],
                             wcols(w_in, 1024 * c, D_PROJ - NSH, 1024, NSH)).then_inc(raw_landed[c % 2], 16)

            def load_out(c, i=None):
                g, k = (c - SL_OUT) // 4, (c - SL_OUT) % 4
                load(wcols(w_out, 512 * k, at(256 * g, 256, i)), c, 4, i)

            for c in range(SL_OUT, SL_OUT + 2):
                load_out(c)
            sp.wait_ge(w_used, SL_OUT + 2)
            sp.dma_start(qtok[0:NB, :], q_scr).then_inc(s_qre, 16)
            sp.wait_ge(s_kto, NH)
            sp.dma_start(d_out["k_prompt"][0, 0].rearrange("(q p) h d -> p q (h d)", p=P), ktok)\
                .then_inc(s_kst_out, 16)
            sp.wait_ge(s_vto, NH)
            sp.dma_start(d_out["v_prompt"][0, 0].rearrange("(q p) h d -> p q (h d)", p=P), vtok)\
                .then_inc(s_out, 16)
            sp.wait_ge(s_kso, 1)
            sp.dma_start(d_out["k_sample"][0, :, 0].rearrange("b h d -> b (h d)"), kstok[0:NB, :])\
                .then_inc(s_out, 16)
            sp.wait_ge(s_vso, 1)
            sp.dma_start(d_out["v_sample"][0, :, 0].rearrange("b h d -> b (h d)"), vstok[0:NB, :])\
                .then_inc(s_out, 16)
            sp.wait_ge(s_vso, 2)
            sp.dma_start(d_out["conv_prompt"][0, 0], xbtok[0:3, :]).then_inc(s_out, 16)
            sp.dma_start(d_out["conv_sample"][0, :, 2], xbtok[3:11, :]).then_inc(s_out, 16)
            sp.dma_start(d_out["conv_sample"][0, :, 0:2], d["state_conv"][0, :, 1:3]).then_inc(s_out, 16)
            sp.wait_ge(s_zout, 16 * 5)
            sp.dma_start(pj[:, TZ:TZ + 8, :], z_scr.rearrange("t p n -> p t n")).then_inc(z_in, 16)
            sp.wait_ge(s_kr, 4 + NB * PAGES)
            with sp.Fori(0, NB) as i:
                for pg in range(PAGES):
                    idx = sp.value_load(ptab[0:1, bass.ds(at(pg, PAGES, i), 1)], min_val=0, max_val=POOL - 1)
                    sp.wait_ge(s_vu, at(pg + 1, PAGES, i))
                    sp.dma_start(vpage[:, pg % 4, :], d["cache_v"][0][bass.ds(idx, 1)]
                                 .rearrange("o t h d -> (o t) (h d)")).then_inc(s_vp[pg % 4], 16)
            src = d["state_ssm"][0].rearrange("b h p n -> (h p) b n")
            dst = d_out["ssm_sample"][0].rearrange("b h p n -> (h p) b n")
            sp.wait_ge(s_dor, 2)
            for t in range(2):
                sp.dma_start(stt[:, t], src[t * P:(t + 1) * P]).then_inc(g_in[t], 16)
            for c in range(SL_OUT + 2, SL_OUT + 4):
                load_out(c)
            sp.wait_ge(f_fc, 1)
            sp.dma_start(d_out["ssm_prompt"][0, 0].rearrange("(t h) p n -> (h p) t n", h=2), fst)\
                .then_inc(s_out, 16)
            for t in range(8):
                sp.wait_ge(g_n, t + 1)
                sp.dma_start(dst[t * P:(t + 1) * P], stt[:, t % 2]).then_inc(g_out[t % 2], 16)
                if t < 6:
                    sp.wait_ge(g_c, t + 1)
                    sp.wait_ge(g_out[t % 2], 16 * (t // 2 + 1))
                    sp.dma_start(stt[:, t % 2], src[(t + 2) * P:(t + 3) * P]).then_inc(g_in[t % 2], 16)
            sp.wait_ge(g_r, 8)
            sp.wait_ge(g_out[0], 16 * 4)
            sp.wait_ge(g_out[1], 16 * 4)
            sp.dma_start(ptok, d["p_prompt"][0, 0].rearrange("(q p) n -> p q n", p=P)).then_inc(h_p, 16)
            sp.dma_start(pstok[0:NB, :], d["p_sample"][0, :, 0]).then_inc(h_p, 16)
            sp.wait_ge(z_s, 2)
            sp.wait_ge(f_yc, 8)
            sp.wait_ge(g_y, 8)
            for q in range(QB):
                sp.dma_start(xt3[:, q, :], d["x_prompt"][0, q * P:(q + 1) * P, :]).then_inc(h_x, 16)
            sp.dma_start(xs3[0:NB, :], d["x_sample"][:, 0, :]).then_inc(h_x, 16)
            with sp.Fori(0, 7) as i:
                for j in range(4):
                    load_out(SL_OUT + 4 + j, i)

            def load_up(n, chunk, per_c, per_n, i):
                for j in range(8):
                    g, k = j // 4, j % 4
                    load(wcols(w_up, 512 * k, at(512 * chunk + 256 * g, 512 * per_c, i)), n + j, per_n, i)

            def load_down(n, chunk, per_c, per_n, i):
                for j in range(8):
                    load(wcols(w_down, at(512 * chunk, 512 * per_c, i), 256 * j), n + j, per_n, i)

            load_up(SL_MLP, 0, 0, 0, None)
            with sp.Fori(0, (CHUNKS - 2) // 2) as i:
                load_up(SL_MLP + 8, 1, 2, 32, i)
                load_down(SL_MLP + 16, 0, 2, 32, i)
                load_up(SL_MLP + 24, 2, 2, 32, i)
                load_down(SL_MLP + 32, 1, 2, 32, i)
            n = SL_PLE - 24
            load_up(n, CHUNKS - 1, 0, 0, None)
            load_down(n + 8, CHUNKS - 2, 0, 0, None)
            load_down(n + 16, CHUNKS - 1, 0, 0, None)
            for g in range(8):
                load(wcols(w_ple, 0, 256 * g, 256), SL_PLE + g, elems=512, k=2)
            with sp.Fori(0, 8) as i:
                for j in range(4):
                    load(wcols(w_gate, 512 * j, at(0, 256, i)), SL_GATE + j, 4, i)
            sp.wait_ge(w_used, SL_GATE + 2)
            sp.dma_start(gfin, d["g_final"].unsqueeze(0).to_broadcast([P, D_MODEL])).then_inc(y_g, 16)
            for q in range(QB):
                sp.wait_ge(y_p, q + 1)
                sp.wait_ge(y_d, 3 * (q + 1))
                sp.dma_start(d_out["y_prompt"][0, q * P:(q + 1) * P, :], yt[:, q, :]).then_inc(y_out, 16)
            sp.wait_ge(y_p, QB + 1)
            sp.wait_ge(y_d, 3 * (QB + 1))
            sp.dma_start(d_out["y_sample"][:, 0, :], ys[0:NB, :]).then_inc(y_out, 16)
            sp.wait_ge(y_out, 16 * (QB + 1))
            sp.wait_ge(s_out, 16 * 7)
            sp.wait_ge(s_kst_out, 16)

        @block.scalar
        def _(act):
            A = act.activation
            chain = Chain(act, act_step)
            act.sem_inc(s_zout, 16)
            vec = lambda name: d[name][0].rearrange("(t p) -> t p", p=P)
            act.dma_start(grow[G_MIX:G_MIX + 16], vec("g_mix")).then_inc(s_small, 16)
            act.dma_start(grow[G_FFN:G_FFN + 16], vec("g_ffn")).then_inc(s_small, 16)
            act.dma_start(grow[G_PLN:G_PLN + 16], vec("w_ple_norm")).then_inc(s_small, 16)
            act.dma_start(grow[G_SSM:G_SSM + 8], vec("w_ssm_norm")).then_inc(s_small, 16)
            act.dma_start(grow[G_SUB:G_SUB + 1], vec("w_subln")).then_inc(s_small, 16)
            act.dma_start(grow[G_CB:G_CB + CT], vec("conv_b")).then_inc(s_small, 16)
            act.dma_start(cwrow[0:CW * CT], d["conv_w"][0].rearrange("j (t p) -> (j t) p", p=P))\
                .then_inc(s_small, 16)
            act.dma_start(cstrow[0:NB * 3], d["state_conv"][0].rearrange("b j n -> (b j) n"))\
                .then_inc(s_small, 16)
            for n, name in enumerate(("dt_bias", "a_log", "d_skip")):
                act.dma_start(hcol[0:NSH, (0, 1, 3)[n]:(0, 1, 3)[n] + 1],
                              d[name][0].rearrange("(h o) -> h o", o=1)).then_inc(s_small, 16)
            for n, name in enumerate(("lambda_q1", "lambda_k1", "lambda_q2", "lambda_k2")):
                act.dma_start(lamc[:, n, :], d[name][0:1, :].to_broadcast([P, DK])).then_inc(s_small, 16)

            def hi(c, per=0, i=None):
                act.wait_ge(raw_landed[c % 2], at(16 * (c // 2 + 1), 8 * per, i))
                act.wait_ge(w_used, at(c + 1, per, i))
                A(wh[:, c % 2], raw[:, c % 2], ACT.Copy).then_inc(hi_ready, 1)

            act.wait_ge(s_x, 16 * QB)
            for q in range(QB):
                chain(A(junk, xt[:, q, :], ACT.Square, accum_out=ssx[:, q:q + 1]))
            act.wait_ge(s_xs, 16)
            chain(A(junk[0:NB], xs[0:NB, :], ACT.Square, accum_out=ssx[0:NB, 4:5]))
            act.wait_ge(s_const, 4)
            A(ssx[:, 0:4], ssx[:, 0:4], ACT.Sqrt, bias=epsc[:, 0:1], scale=1.0 / D_MODEL).then_inc(s_ss, 1)
            A(ssx[0:NB, 4:5], ssx[0:NB, 4:5], ACT.Sqrt, bias=epsc[0:NB, 0:1], scale=1.0 / D_MODEL)\
                .then_inc(s_ss, 1)
            act.wait_ge(s_gc, 2)
            for k in range(KT):
                act.wait_ge(s_xT, k + 1)
                A(uh[:, k, 0:SEQ], ps[:, k % 4, :], ACT.Copy, scale=gcol[:, G_MIX + k:G_MIX + k + 1])\
                    .then_inc(s_uh, 1)
                if k == 1:
                    hi(0)
                if k == 3:
                    hi(1)
            act.wait_ge(s_lam, 2)
            A(lams[:, 0:2], lams[:, 0:2], ACT.Exp).then_inc(s_lame, 1)
            def hi8(c, i):
                for j in range(8):
                    hi(c + j, 8, i)

            with act.Fori(0, 2) as i:
                hi8(2, i)
            act.wait_ge(s_qt, 1)
            A(qtok1[0:NB, :].rearrange("p (b n) -> p b n", b=2), ps[0:NB, 0:2, :], ACT.Copy)\
                .then_inc(s_qtc, 1)
            act.wait_ge(s_qtc, 1)
            act.dma_start(q_scr, qtok1[0:NB, :]).then_inc(s_qscr, 16)
            with act.Fori(0, 4) as i:
                hi8(18, i)
            with act.Fori(0, 2) as i:
                for m in range(2):
                    for j in range(4):
                        hi(50 + 4 * m + j, 8, i)
                    act.wait_ge(s_zst, at(m + 1, 2, i))
                    act.dma_start(z_scr[bass.ds(at(2 * m, 4, i), 2)].rearrange("t p n -> p t n"), zst)\
                        .then_inc(s_zout, 16)
            with act.Fori(0, 3) as i:
                hi8(66, i)
            hi(SL_OUT)
            hi(SL_OUT + 1)
            act.wait_ge(s_rt3, 1)
            A(kstok[0:NB, :].rearrange("p (b n) -> p b n", b=2), ps[0:NB, 4:6, :], ACT.Copy).then_inc(s_kso, 1)
            act.wait_ge(s_rt3, 2)
            A(vstok[0:NB, :].rearrange("p (b n) -> p b n", b=2), ps[0:NB, 6:8, :], ACT.Copy).then_inc(s_vso, 1)
            for t in range(NH):
                for tok, b, turned, done in ((ktok, 2 * t % 4, s_kt, s_kto), (vtok, (2 * t + 1) % 4, s_vt, s_vto)):
                    act.wait_ge(turned, t + 1)
                    A(tok[:, :, t * P:(t + 1) * P], ps[:, b, :].rearrange("p (q n) -> p q n", q=QB),
                      ACT.Copy).then_inc(done, 1)
                if t == 1:
                    act.wait_ge(s_rt3, 3)
                    A(xbtok[0:11, :].rearrange("p (b n) -> p b n", b=3), ps[0:11, 4:7, :], ACT.Copy)\
                        .then_inc(s_vso, 1)
            act.wait_ge(s_dv, 3)
            A(sc, sc, ACT.Exp, scale=SCALE).then_inc(s_dex, 1)
            UN = NH * QB

            def a_exp(u):
                n = (u % QB + 1) * P
                act.wait_ge(a_nm, u + 1)
                for c in range(2):
                    A(se[:, u % 3, c, 0:n], se[:, u % 3, c, 0:n], ACT.Exp, bias=nmx[:, u % 3, c:c + 1],
                      scale=SCALE, accum_out=sums[:, u % 3, c:c + 1]).then_inc(a_e, 1)

            def a_second(u):
                n = (u % QB + 1) * P
                act.wait_ge(a_rs, u + 1)
                A(se[:, u % 3, 1, 0:n], se[:, u % 3, 1, 0:n], ACT.Copy, scale=rsum[:, u % 3, 1:2])\
                    .then_inc(a_e1, 1)

            def a_wcopy(u):
                h, q = u // QB, u % QB
                act.wait_ge(a_t, u + 1)
                if h >= 2:
                    act.wait_ge(a_o, h - 1)
                else:
                    act.wait_ge(s_kst_out, 16)
                A(wt[:, h % 2, 0:q + 1, q * P:(q + 1) * P],
                  ps[:, 3 + u % 2, 0:(q + 1) * P].rearrange("p (k n) -> p k n", n=P), ACT.Copy)\
                    .then_inc(a_wt, 1)

            def a_out(h):
                act.wait_ge(a_o, h + 1)
                A(pj[:, TQ + h, 0:SEQ], ps[:, 5, :], ACT.Copy).then_inc(a_oc, 1)

            def a_tap(j):
                if j == 0:
                    act.wait_ge(s_out, 16 * 6)
                if j >= 3:
                    act.wait_ge(c_m, j - 2)
                A(yb[:, j % 3, 0:SEQ], pj[:, TX + j, 0:SEQ], ACT.Identity,
                  bias=gcol[:, G_CB + j:G_CB + j + 1],
                  scale=cwcol[:, 3 * CT + j:3 * CT + j + 1]).then_inc(c_i, 1)

            def a_sigmoid(j):
                if j >= 2:
                    act.wait_ge(c_m, j - 1)
                if j < CT:
                    if j == 0:
                        act.wait_ge(s_nv, 1)
                        act.wait_ge(s_out, 16 * 6)
                    act.wait_ge(c_v, j + 1)
                    A(eb[:, j % 2, 0:SEQ], yb[:, j % 3, 0:SEQ], ACT.Exp, scale=-1.0).then_inc(c_e, 1)
                else:
                    if j == CT:
                        act.wait_ge(z_in, 16)
                    A(eb[:, j % 2], pj[:, TZ + j - CT, :], ACT.Exp, scale=-1.0).then_inc(c_e, 1)

            def head_root(h, q_=hq, bank=5, n=SEQ):
                act.wait_ge(n_s, h + 1)
                A(q_[:, 0:n], ps[:, bank, 0:n], ACT.Sqrt, bias=epsc[:, 1:2], scale=1.0 / P).then_inc(n_rt, 1)

            for s in range(UN + 7):
                if s < UN:
                    a_exp(s)
                if 1 <= s <= UN:
                    a_second(s - 1)
                if 3 <= s < UN + 3:
                    a_wcopy(s - 3)
                if s >= 8 and s % QB == 0:
                    h = s // QB - 2
                    a_out(h)
                    if h:
                        act.wait_ge(n_o, h)
                    A(hq, ps[:, 5, :], ACT.Square).then_inc(n_q, 1)
                if 8 <= s < UN + 4 and s % QB == 2:
                    head_root(s // QB - 2)
                if s == 27:
                    act.wait_ge(d_v, 1)
                    A(sp5[1][0:NSH], sp5[1][0:NSH], ACT.Exp, scale=-1.0).then_inc(d_s, 1)
                    A(hcol[0:NSH, 2:3], hcol[0:NSH, 1:2], ACT.Exp).then_inc(d_s, 1)
                if s == 29:
                    act.wait_ge(d_v, 2)
                    A(sp5[3][0:NSH], sp5[2][0:NSH], ACT.Ln).then_inc(d_s, 1)
                if s == UN + 6:
                    act.wait_ge(e_t, 3)
                    A(decb, ps[:, 1, 256:320].rearrange("p (h c) -> p h c", c=QB), ACT.Exp).then_inc(e_dx, 1)
                if s == 33:
                    act.wait_ge(d_v, 3)
                    A(ecat[0:NSH, 0:NB], sp5[4][0:NSH, SEQ:T], ACT.Exp).then_inc(d_s, 1)
                if 3 <= s < CT + 3:
                    a_tap(s - 3)
                if 5 <= s < JOBS + 5:
                    a_sigmoid(s - 5)
                if s == 4:
                    act.wait_ge(c_dv, 1)
                    A(csr, pj[:, TX:TX + CT, SEQ:T], ACT.Exp, scale=-1.0).then_inc(c_de, 1)
            act.wait_ge(e_c, 4)
            A(dsk, dsk, ACT.Exp).then_inc(e_dx, 1)
            act.wait_ge(e_t, 4)
            A(bcrow[0:NB], ps[0:NB, 5, :].rearrange("p (k n) -> p k n", k=4), ACT.Copy).then_inc(g_bc, 1)
            act.wait_ge(g_bc, 1)
            act.dma_start(bc_scr, bcrow[0:NB]).then_inc(g_bs, 16)
            for g in range(2):
                act.wait_ge(e_t, g + 5)
                A(btok[:, :, g, :], ps[:, g, :].rearrange("p (c n) -> p c n", c=QB), ACT.Copy)\
                    .then_inc(e_bc, 1)
            act.wait_ge(s_dor, 2)
            A(tmp[:, 0, 0:64].rearrange("p (h b) -> p h b", b=NB), pj[:, TQ:TQ + NH, SEQ:T], ACT.Square)\
                .then_inc(n_q, 1)
            head_root(NH - 1, bank=6)
            head_root(NH, tmp[:, 0], 7, 64)
            act.wait_ge(g_bs, 16)
            act.wait_ge(s_vu, 16 * NB + 4)
            for k in range(4):
                act.dma_start(bcb[:, k], bc_scr[:, k].unsqueeze(0).to_broadcast([P, NB, NS]))\
                    .then_inc(g_bb, 16)
            act.wait_ge(f_ft, 1)
            A(fst, ps[:, 0:2, :].rearrange("p b (t n) -> p (b t) n", n=NS), ACT.Copy).then_inc(f_fc, 1)
            def gated_square(t):
                act.wait_ge(z_y, t + 1)
                A(pj[:, TZ + t, :], pj[:, TY + t, :], ACT.Square).then_inc(z_q, 1)

            def gated_root(g):
                act.wait_ge(z_s, g + 1)
                A(halves(tmp[:, g]), ps[:, 2 * g:2 * g + 2, 0:HALF], ACT.Sqrt, bias=epsc[:, 0:1],
                  scale=1.0 / 512).then_inc(z_rt, 1)

            for h in range(NSH):
                act.wait_ge(f_d, h + 1)
                if h >= 3:
                    act.wait_ge(f_y, h - 2)
                A(cd[h % 3], ps[:, 4 + h % 4, :].rearrange("p (c n) -> p c n", c=QB), ACT.Exp)\
                    .then_inc(f_c, 1)
                A(dl[h % 3], dl[h % 3], ACT.Exp).then_inc(f_e, 1)
                if h >= 6 and h % 2 == 0:
                    gated_square(h // 2 - 3)
            act.wait_ge(f_y, NSH)
            act.wait_ge(n_o, NH + 1)
            for t in range(NH):
                A(uh[:, t], pj[:, TQ + t, :], ACT.Copy).then_inc(z_h, 1)
                if t == 0:
                    gated_root(0)
                if t == 3:
                    for k in range(5, 8):
                        gated_square(k)
            gated_root(1)
            for t in range(8):
                act.wait_ge(z_o, t + 1)
                A(uh[:, 8 + t], pj[:, TY + t, :], ACT.Copy).then_inc(z_h, 1)
            for k in range(2):
                act.wait_ge(h_pt, k + 1)
                A(ph[:, k, 0:SEQ], ps[:, 2 * k, :], ACT.Copy).then_inc(h_pc, 1)
                A(ph[:, k, SEQ:T], ps[:, 2 * k + 1, 0:NB], ACT.Copy).then_inc(h_pc, 1)

            def square(c, per, i):
                act.wait_ge(h_e, at(c + 1, per, i))
                act.wait_ge(h_a, at(c + 1, per, i))
                src = hT[:, bass.ds(at(2 * c, 2 * per, i), 2), :] if i is not None else hT[:, 2 * c:2 * c + 2, :]
                A(sq, src, ACT.Square).then_inc(h_q, 1)

            with act.Fori(0, 8) as i:
                for j in range(4):
                    hi(SL_OUT + 2 + j, 4, i)
                square(0, 1, i)
            for k in range(KT):
                if k == 0:
                    act.wait_ge(w_used, SL_MLP + 2)
                A(uh[:, k], hT[:, k], ACT.Copy, scale=gcol[:, G_FFN + k:G_FFN + k + 1]).then_inc(s_uh, 1)

            def root(n):
                act.wait_ge(h_s, n)
                A(halves(rstd), ps[:, 0:2, 0:HALF], ACT.Sqrt, bias=epsc[:, 0:1], scale=1.0 / D_MODEL)\
                    .then_inc(h_rt, 1)

            def hidden(c, per, i, slot, m):
                act.wait_ge(m_t, at(2 * (c + 1), 2 * per, i))
                act.wait_ge(m_l, at(c + 1, per, i))
                chain(A(sq, tm, ACT.Square))
                A(hh[:, slot, 2 * m:2 * m + 2], sq, ACT.Copy).then_inc(m_q, 1)

            def up(n, c, per_n, per_c, i, slot, first=False):
                for m in range(2):
                    for j in range(1, 5):
                        if first and m == 0 and j == 4:
                            root(1)
                        hi(n + 4 * m + j, per_n, i)
                    hidden(c + m, per_c, i, slot, m)

            def down(n, per_n, i):
                for j in range(1, 9):
                    hi(n + j, per_n, i)

            b = SL_MLP + 2
            hi(b)
            up(b, 0, 0, 0, None, 0, first=True)
            steps = chain.n
            with act.Fori(0, (CHUNKS - 2) // 2) as i:
                chain.n = i * 4 + steps
                up(b + 8, 2, 32, 4, i, 1)
                down(b + 16, 32, i)
                up(b + 24, 4, 32, 4, i, 0)
                down(b + 32, 32, i)
            chain.n = steps + 4 * (CHUNKS - 2) // 2
            up(SL_PLE - 22, 2 * CHUNKS - 2, 0, 0, None, 1)
            down(SL_PLE - 14, 0, None)
            def h_split(j):
                act.wait_ge(group_free, G_PLE - 8 + j + 3)
                A(uh[:, 2 * j:2 * j + 2], hT[:, 2 * j:2 * j + 2], ACT.Copy).then_inc(s_uh, 1)

            act.wait_ge(w_used, SL_PLE - 16 + 2)
            for j in range(1, 8):
                hi(SL_PLE - 6 + j)
                h_split(j - 1)
            h_split(7)
            for g in range(8):
                hi(SL_PLE + 2 + g)
                act.wait_ge(w_used, SL_PLE + g + 3)
                act.wait_ge(h_a, 8 + g + 1)
                if g == 0:
                    act.wait_ge(m_l, 2 * CHUNKS + 1)
                A(sq.rearrange("p m (h n) -> p m h n", h=2), group_view(G_PLE + g), ACT.Square).then_inc(h_q, 1)

            def gate(c, per, i):
                act.wait_ge(x_c, at(c + 1, per, i))
                A(tm, tm, ACT.Exp, scale=-1.0).then_inc(x_e, 1)

            def gate_sq(c, per, i):
                act.wait_ge(x_h, at(c + 2, per, i))
                act.wait_ge(h_a, at(16 + c + 1, per, i))
                src = hT[:, bass.ds(at(2 * c, 2 * per, i), 2), :] if i is not None else hT[:, 2 * c:2 * c + 2, :]
                A(sq, src, ACT.Square).then_inc(h_q, 1)

            for j in range(4):
                hi(SL_GATE + 2 + j)
            root(2)
            with act.Fori(0, 3) as i:
                for m in range(2):
                    gate(m, 2, i)
                    for j in range(2):
                        hi(SL_GATE + 6 + 4 * m + j, 8, i)
                    gate_sq(m, 2, i)
                    for j in range(2, 4):
                        hi(SL_GATE + 6 + 4 * m + j, 8, i)
            for m in range(2):
                gate(6 + m, 0, None)
                if m == 0:
                    hi(SL_ALL - 2)
                    hi(SL_ALL - 1)
                gate_sq(6 + m, 0, None)
            act.wait_ge(h_s, 3)
            A(ssx[:, 0:QB], ps[:, 0, 0:QB], ACT.Sqrt, bias=epsc[:, 0:1], scale=1.0 / D_MODEL).then_inc(h_rt, 1)
            A(ssx[0:NB, QB:QB + 1], ps[0:NB, 0, QB:QB + 1], ACT.Sqrt, bias=epsc[0:NB, 0:1],
              scale=1.0 / D_MODEL).then_inc(h_rt, 1)
            act.wait_ge(y_s, 2)
            for q in range(QB + 1):
                act.wait_ge(y_t, 4 * q + 1)
                src, dst, rms, _ = y_quarter(4 * q)
                A(dst, src, ACT.Copy, scale=rms).then_inc(y_c, 1)

        @block.gpsimd
        def _(pool):
            step = Chain(pool, pool_step)
            pool.sem_inc(s_km, 1)
            step(pool.memset(ident, 0.0))
            step(pool.affine_select(out=ident, in_=ident, compare_op=ALU.not_equal, fill=1.0, base=0,
                                    pattern=[[-1, P]], channel_multiplier=1))
            step(pool.memset(causal, 0.0))
            step(pool.affine_select(out=causal, in_=causal, compare_op=ALU.is_ge, fill=NEG, base=0,
                                    pattern=[[1, P]], channel_multiplier=-1))
            step(pool.memset(rowm[0:NB], NEG))
            pool.affine_select(out=rowm[0:NB], in_=rowm[0:NB], compare_op=ALU.not_equal, fill=0.0, base=0,
                               pattern=[[-1, NB]], channel_multiplier=1).then_inc(s_const, 1)
            pool.memset(ones, 1.0).then_inc(s_const, 1)
            pool.memset(epsc[:, 0:1], EPS).then_inc(s_const, 1)
            pool.memset(epsc[:, 1:2], EPS_SUB).then_inc(s_const, 1)
            with pool.Fori(0, NB // 2) as i:
                for b in range(2):
                    pool.wait_ge(s_qbc, at(16 * (b + 1), 32, i))
                    for pg in range(PAGES * b, PAGES * (b + 1)):
                        s = pg % 4
                        pool.wait_ge(s_kp[s], at(16 * (pg // 4 + 1), 8 * PAGES, i))
                        pool.tensor_tensor(kpage[:, s], kpage[:, s], qbc[:, b], ALU.mult).then_inc(s_km, 1)
            pool.wait_ge(w_used, SL_OUT + 2)
            pool.iota(dist, pattern=[[1, 896]], base=-384, channel_multiplier=-1,
                      allow_small_or_imprecise_dtypes=True).then_inc(s_dc, 1)
            pool.iota(ddist, pattern=[[P, PAGES]], base=-PAST, channel_multiplier=1,
                      allow_small_or_imprecise_dtypes=True).then_inc(s_dc, 1)
            pool.wait_ge(s_dc, 2)
            pool.affine_select(out=dist, in_=dist, compare_op=ALU.is_ge, fill=NEG, base=384,
                               pattern=[[-1, 896]], channel_multiplier=1).then_inc(s_dc, 1)
            for h in range(NH):
                pool.tensor_scalar(dbias[:, :, 2 * h:2 * h + 2],
                                   ddist.unsqueeze(2).to_broadcast([P, PAGES, 2]),
                                   SLOPES[h] / SCALE, 1.0, ALU.mult, ALU.mult).then_inc(s_dc, 1)
            pool.memset(sc[:, :, PAGES, :], NEG).then_inc(s_dc, 1)
            for j in range(JOBS):
                n = SEQ if j < CT else T
                pool.wait_ge(c_e, j + 1)
                pool.tensor_scalar(eb[:, j % 2, 0:n], eb[:, j % 2, 0:n], 3.0e38, 1.0, ALU.min, ALU.add)\
                    .then_inc(c_p, 1)
            for c in range(QB):
                pool.wait_ge(e_xd, 8)
                pool.wait_ge(e_dx, 2)
                pool.tensor_tensor(xdd[:, c].rearrange("p (h n) -> p h n", h=NSH),
                                   xd[:, c].rearrange("p (h n) -> p h n", h=NSH),
                                   dsk[:, c].unsqueeze(2).to_broadcast([P, NSH, HD]), ALU.mult)\
                    .then_inc(e_xdd, 1)
            for c in range(1, QB):
                pool.wait_ge(e_sc, c)
                pool.tensor_tensor(sall[:, c].rearrange("p (h n) -> p h n", h=NSH),
                                   sall[:, c - 1].rearrange("p (h n) -> p h n", h=NSH),
                                   decb[:, :, c].unsqueeze(2).to_broadcast([P, NSH, HD]), ALU.mult)\
                    .then_inc(e_sm, 1)
            pool.wait_ge(c_m, JOBS)

            def gated(t):
                pool.wait_ge(f_yc, t + 1)
                pool.wait_ge(g_y, t + 1)
                pool.tensor_tensor(pj[:, TY + t, :], pj[:, TY + t, :], pj[:, TZ + t, :], ALU.mult).then_inc(z_y, 1)

            for h in range(NSH):
                g, t = h // 8, h // 2
                if h == 0:
                    pool.wait_ge(e_cbc, 2)
                pool.wait_ge(f_c, h + 1)
                pool.tensor_tensor(cd[h % 3], cd[h % 3],
                                   pj[:, CX + TC_ + g, 0:SEQ].rearrange("p (c n) -> p c n", c=QB),
                                   ALU.mult).then_inc(f_cm, 1)
                pool.wait_ge(f_e, h + 1)
                pool.tensor_tensor(dl[h % 3], dl[h % 3], cbt[:, g], ALU.mult).then_inc(f_m, 1)
                if h % 2 == 0:
                    if t == 0:
                        pool.wait_ge(g_bb, 16 * 4)
                        pool.wait_ge(g_xd, 1)
                    else:
                        pool.wait_ge(g_r, t)
                    pool.tensor_tensor(bx, bcb[:, t // 4], xdt[:, t].unsqueeze(2).to_broadcast([P, NB, NS]),
                                       ALU.mult).then_inc(g_b, 1)
                    if t >= 2:
                        gated(t - 2)
            for t in range(6, 8):
                gated(t)
            pool.wait_ge(z_l, KT)
            step(pool.memset(acc, 0.0))
            pool.sem_inc(h_a, 1)

            def add_squares(c, per, i):
                pool.wait_ge(h_q, at(c + 1, per, i))
                step(pool.tensor_tensor(acc, acc, sq[:, 0], ALU.add))
                ins = pool.tensor_tensor(acc, acc, sq[:, 1], ALU.add)
                ins.then_inc(h_a, 1)
                pool.wait_ge(h_a, at(c + 2, per, i))

            n0 = step.n
            with pool.Fori(0, 8) as i:
                step.n = i * 1 + n0
                add_squares(0, 1, i)
            step.n = n0 + 8
            pool.wait_ge(h_rt, 1)
            step(pool.memset(acc, 0.0))
            n0 = step.n
            with pool.Fori(0, 8) as i:
                step.n = i * 1 + n0
                add_squares(8, 1, i)
            step.n = n0 + 8
            pool.wait_ge(h_rt, 2)
            step(pool.memset(acc, 0.0))
            n0 = step.n
            with pool.Fori(0, 8) as i:
                pool.wait_ge(x_r, at(1, 1, i))
                pool.tensor_tensor(tm, tm, eT[:, bass.ds(i * 2, 2), :], ALU.mult).then_inc(x_m, 1)
                step.n = i * 1 + n0
                add_squares(16, 1, i)
            pool.wait_ge(y_g, 16)
            for q in range(QB + 1):
                pool.wait_ge(y_c, q + 1)
                _, dst, _, gain = y_quarter(4 * q)
                pool.tensor_tensor(dst, dst, gain, ALU.mult).then_inc(y_p, 1)

        @block.tensor
        def _(pe):
            pe.sem_inc(w_used, 2)
            pe.sem_inc(s_vu, 4)
            pe.sem_inc(group_free, 2)
            mm = pe.matmul
            pe.wait_ge(s_const, 4)
            pe.wait_ge(s_small, 16 * 15)
            pe.transpose(ps[:, 4, 0:G_CB + CT], grow[0:G_CB + CT, :], ident[0:G_CB + CT, 0:G_CB + CT]).then_inc(s_gt, 1)
            pe.transpose(ps[:, 5, 0:48], cwrow[0:48, :], ident[0:48, 0:48]).then_inc(s_gt, 1)
            for t in range(CT):
                last = pe.transpose(ps[:, 6, 24 * t:24 * t + 24], cstrow[0:24, t * P:(t + 1) * P],
                                    ident[0:24, 0:24])
            last.then_inc(s_gt, 1)
            pe.wait_ge(s_xs, 16)
            for k in range(KT):
                last = pe.transpose(ps[:, 7, 8 * k:8 * k + 8], xs[0:NB, k * P:(k + 1) * P],
                                    ident[0:NB, 0:NB])
            last.then_inc(s_xsT, 1)
            pe.wait_ge(s_x, 16 * QB)
            for k in range(KT):
                if k >= 4:
                    pe.wait_ge(s_ul, k - 3)
                for q in range(QB):
                    last = pe.transpose(ps[:, k % 4, q * P:(q + 1) * P], xt[:, q, k * P:(k + 1) * P], ident)
                last.then_inc(s_xT, 1)
            pe.wait_ge(s_gc, 4)
            pe.wait_ge(s_rt, 5)
            for q in range(QB):
                mm(ps[:, 4, q * P:(q + 1) * P], ones, rdiag[:, q, :], start=True, stop=True)
            mm(ps[:, 5, 0:NB], ones[0:NB, :], junk[0:NB, 0:NB], start=True, stop=True).then_inc(s_rb, 1)
            pe.wait_ge(s_rd, 2)
            pe.wait_ge(s_ul, KT)
            pe.wait_ge(s_us, 1)

            def slab(c, per, i, kts, ms, first, last, bank, kstep, mstep=P):
                pe.wait_ge(lo_ready, at(c + 3, per, i))
                s = c % 2
                n = len(kts)
                for x, (k, xh, xl) in enumerate(kts):
                    for m in range(ms):
                        a = k * kstep + m * mstep
                        h_, l_ = wh[:, s, a:a + P], wl[:, s, a:a + P]
                        st, en = first and x == 0, last and x == n - 1
                        for f in range(2):
                            mm(ps[:, bank + 2 * m + f, 0:HALF], h_, xh[:, f * HALF:(f + 1) * HALF],
                               start=st, stop=False)
                            mm(ps[:, bank + 2 * m + f, 0:HALF], h_, xl[:, f * HALF:(f + 1) * HALF],
                               start=False, stop=False)
                        for f in range(2):
                            z = mm(ps[:, bank + 2 * m + f, 0:HALF], l_, xh[:, f * HALF:(f + 1) * HALF],
                                   start=False, stop=en)
                z.then_inc(w_used, 1)

            def group(n, g, per_n, per_g, i):
                pe.wait_ge(group_free, at(g + 1, per_g, i))
                for j in range(4):
                    slab(n + j, per_n, i, [(k, uh[:, 4 * j + k], ul[:, 4 * j + k]) for k in range(4)], 2,
                         j == 0, j == 3, GB[g % 2], 256)

            with pe.Fori(0, 2) as i:
                group(0, 0, 8, 2, i)
                group(4, 1, 8, 2, i)
            pe.wait_ge(group_free, 6)
            for t in range(NH):
                last = pe.transpose(ps[0:NB, t // 4, t % 4 * P:(t % 4 + 1) * P], pj[:, TQ + t, SEQ:T], ident)
            last.then_inc(s_qt, 1)
            pe.wait_ge(s_qtc, 1)
            with pe.Fori(0, 9) as i:
                group(16, 4, 8, 2, i)
                group(20, 5, 8, 2, i)
            pe.wait_ge(group_free, G_DT + 1)
            for j in range(2):
                slab(SL_DT + j, 0, None, [(k, uh[:, 8 * j + k], ul[:, 8 * j + k]) for k in range(8)], 1,
                     j == 0, j == 1, GB[G_DT % 2], P)
            pe.wait_ge(group_free, G_OUT + 2)
            for base_t, b, out in ((TK, 4, s_rt3), (TV, 6, s_rt3)):
                for t in range(NH):
                    last = pe.transpose(ps[0:NB, b + t // 4, t % 4 * P:(t % 4 + 1) * P],
                                        pj[:, base_t + t, SEQ:T], ident)
                last.then_inc(out, 1)
            for t in range(NH):
                for base_t, b, got, out in ((TK, 2 * t % 4, s_kto, s_kt), (TV, (2 * t + 1) % 4, s_vto, s_vt)):
                    if t >= 2:
                        pe.wait_ge(got, t - 1)
                    for q in range(QB):
                        last = pe.transpose(ps[:, b, q * P:(q + 1) * P], pj[:, base_t + t, q * P:(q + 1) * P],
                                            ident)
                    last.then_inc(out, 1)
                if t == 1:
                    pe.wait_ge(s_kso, 1)
                    pe.wait_ge(s_vso, 1)
                    for k in range(CT):
                        last = pe.transpose(ps[0:NB + 3, 4 + k // 4, k % 4 * P:(k % 4 + 1) * P],
                                            pj[:, TX + k, SEQ - 3:T], ident)
                    last.then_inc(s_rt3, 1)
                if t == 3:
                    pe.wait_ge(s_dv, 1)
                    pe.transpose(ps[:, 7, 0:P], dmx, ident).then_inc(s_dp, 1)
                if t == 5:
                    pe.wait_ge(s_vso, 2)
                    pe.wait_ge(s_dv, 2)
                    mm(ps[:, 4, 0:P], ones, ddiag, start=True, stop=True).then_inc(s_dp, 1)
            pe.wait_ge(s_dv, 4)
            mm(ps[:, 5, 0:P], ones, dmx, start=True, stop=True).then_inc(s_dp, 1)
            pe.wait_ge(s_kto, NH)
            pe.wait_ge(s_vto, NH)
            UN = NH * QB

            def scores(u):
                h, q = u // QB, u % QB
                n = (q + 1) * P
                for c in range(2):
                    j = 2 * u + c
                    if j >= 3:
                        pe.wait_ge(a_b, j - 2)
                    mm(ps[:, j % 3, 0:n], pj[64 * c:64 * c + 64, TQ + h, q * P:(q + 1) * P],
                       pj[64 * c:64 * c + 64, TK + h, 0:n], start=True, stop=True).then_inc(a_s, 1)

            def turn(u):
                q = u % QB
                pe.wait_ge(a_w, u + 1)
                if u >= 2:
                    pe.wait_ge(a_wt, u - 1)
                for k in range(q + 1):
                    last = pe.transpose(ps[:, 3 + u % 2, k * P:(k + 1) * P],
                                        se[:, u % 3, 0, k * P:(k + 1) * P], ident)
                last.then_inc(a_t, 1)

            def values(h):
                pe.wait_ge(a_wt, 4 * (h + 1))
                if h >= 1:
                    pe.wait_ge(n_rt, h)
                for k in range(QB):
                    last = mm(ps[:, 5, k * P:SEQ], vtok[:, k, h * P:(h + 1) * P],
                              wt[:, h % 2, k, k * P:SEQ], start=(k == 0), stop=(k == QB - 1))
                last.then_inc(a_o, 1)

            def page_values(n):
                b = n // PAGES
                if n % 4 == 0:
                    pe.wait_ge(s_wz, n // 4 + 2)
                pe.wait_ge(s_vp[n % 4], 16 * (n // 4 + 1))
                for f in range(2):
                    last = mm(ps[0:64, 6 + f, :], zpad[:, n // 4 % 2, n % 4, 56 - 8 * b:120 - 8 * b],
                              vpage[:, n % 4, f * 512:(f + 1) * 512], start=False, stop=(n == NB * PAGES - 1))
                last.then_inc(s_vu, 1)

            pe.wait_ge(s_wz, 1)
            for f in range(2):
                last = mm(ps[0:64, 6 + f, :], wnew[0:NB, :], vstok[0:NB, f * 512:(f + 1) * 512],
                          start=True, stop=False)
            last.then_inc(s_nv, 1)
            pe.wait_ge(s_vso, 2)
            def head_sum(h, q_=hq, bank=5, n=SEQ):
                pe.wait_ge(n_q, h + 1)
                mm(ps[:, bank, 0:n], ones, q_[:, 0:n], start=True, stop=True).then_inc(n_s, 1)

            for s in range(UN + 5):
                pages = iter(range(4 * s, min(4 * s + 4, NB * PAGES)))
                if s < UN:
                    scores(s)
                    page_values(next(pages))
                if 2 <= s < UN + 2:
                    turn(s - 2)
                if s < UN:
                    page_values(next(pages))
                if 7 <= s < UN + 5 and s % QB == 3:
                    values(s // QB - 1)
                if s == UN + 4:
                    pe.wait_ge(s_dor, 1)
                    for h in range(NH):
                        last = mm(ps[:, 7, NB * h:NB * (h + 1)], oacc[0:64, h * P:(h + 1) * P], ident[0:64, h:64:NH],
                                  start=True, stop=True)
                    last.then_inc(s_dos, 1)
                    pe.wait_ge(d_v, 4)
                    pe.wait_ge(d_s, 4)
                    for c in range(QB):
                        pe.transpose(ps[:, 0, c * NSH:(c + 1) * NSH], dtt[0:NSH, c * P:(c + 1) * P], ident[0:NSH, 0:NSH])
                        last = pe.transpose(ps[:, 0, 64 + c * NSH:64 + (c + 1) * NSH], acs[0:NSH, c * P:(c + 1) * P],
                                            ident[0:NSH, 0:NSH])
                    last.then_inc(e_t, 1)
                    for h in range(NSH):
                        r0 = HD * (h % 2)
                        last = mm(ps[r0:r0 + HD, 1, 17 * (h // 2):17 * (h // 2) + 17],
                                  ident[0:NSH, h:h + 1].to_broadcast([NSH, HD]), ecat[0:NSH, :], start=True, stop=True)
                    last.then_inc(e_t, 1)
                    for h in range(NSH):
                        last = mm(ps[:, 1, 256 + QB * h:256 + QB * (h + 1)], ident[0:NSH, h:h + 1].to_broadcast([NSH, P]),
                                  acs[0:NSH, P - 1:SEQ:P], start=True, stop=True)
                    last.then_inc(e_t, 1)
                if s >= 9 and s % QB == 1:
                    pe.wait_ge(a_oc, s // QB - 1)
                    head_sum(s // QB - 2)
                for n in pages:
                    page_values(n)
            pe.wait_ge(c_m, CT)
            pe.wait_ge(a_oc, NH)
            pe.wait_ge(n_q, NH)
            for k in range(4):
                last = pe.transpose(ps[0:NB, 5, k * P:(k + 1) * P], pj[:, CX + 8 + k, SEQ:T], ident)
            last.then_inc(e_t, 1)
            pe.wait_ge(e_c, 4)
            pe.wait_ge(e_dx, 1)
            for g in range(2):
                for c in range(QB):
                    last = pe.transpose(ps[:, g, c * P:(c + 1) * P],
                                        pj[:, CX + TB_ + g, c * P:(c + 1) * P], ident)
                last.then_inc(e_t, 1)
            for t in range(8):
                if t >= 2:
                    pe.wait_ge(e_xd, t - 1)
                for c in range(QB):
                    last = pe.transpose(ps[:, 2 + t % 2, c * P:(c + 1) * P],
                                        pj[:, CX + t, c * P:(c + 1) * P], ident)
                last.then_inc(e_xt, 1)
            pe.wait_ge(s_dor, 2)
            head_sum(NH - 1, bank=6)
            head_sum(NH, tmp[:, 0], 7, 64)
            pe.wait_ge(g_bc, 1)
            for g in range(2):
                for c in range(QB):
                    last = mm(ps[:, 4 + g, c * P:(c + 1) * P], pj[:, CX + TB_ + g, c * P:(c + 1) * P],
                              pj[:, CX + TC_ + g, c * P:(c + 1) * P], start=True, stop=True)
                last.then_inc(e_cb, 1)
            pe.wait_ge(e_bc, 2)
            pe.wait_ge(e_dx, 2)
            pe.wait_ge(e_c, 4)
            pe.wait_ge(e_xd, 8)
            for c in range(QB):
                pe.wait_ge(e_xdd, c + 1)
                if c >= 2:
                    pe.wait_ge(e_sc, c - 1)
                for g in range(2):
                    last = mm(ps[:, 2 * (c % 2) + g, :], btok[:, c, g, :], xdd[:, c, g * 512:(g + 1) * 512],
                              start=True, stop=True)
                last.then_inc(e_st, 1)

            def spread(h):
                if h >= 4:
                    pe.wait_ge(f_c, h - 3)
                    pe.wait_ge(f_d, h - 3)
                mm(ps[:, 4 + h % 4, :], ident[0:NSH, h:h + 1].to_broadcast([NSH, P]), acs[0:NSH, :],
                   start=True, stop=True).then_inc(f_a, 1)

            def y_head(h):
                pe.wait_ge(f_m, h + 1)
                pe.wait_ge(f_cm, h + 1)
                t = h // 2
                if h % 2 == 0 and t >= 2:
                    pe.wait_ge(f_yc, t - 1)
                r = 64 * (h % 2)
                for c in range(QB):
                    out = ps[r:r + 64, 2 + t % 2, c * P:(c + 1) * P]
                    last = mm(out, xd[:, c, h * HD:(h + 1) * HD], dl[h % 3][:, c, :], start=True, stop=(c == 0))
                    if c:
                        last = mm(out, sall[:, c - 1, h * HD:(h + 1) * HD], cd[h % 3][:, c, :],
                                  start=False, stop=True)
                last.then_inc(f_y, 1)

            pe.wait_ge(e_cbc, 2)
            pe.wait_ge(e_sc, QB)
            for t in range(8):
                last = pe.transpose(ps[:, t // 4, t % 4 * P:(t % 4 + 1) * P], sall[:, QB - 1, t * P:(t + 1) * P],
                                    ident)
            last.then_inc(f_ft, 1)

            def gated_sum(t):
                pe.wait_ge(z_q, t + 1)
                b = 2 * (t // 4)
                for f in range(2):
                    last = mm(ps[:, b + f, 0:HALF], ones, pj[:, TZ + t, f * HALF:(f + 1) * HALF],
                              start=(t % 4 == 0), stop=(t % 4 == 3))
                if t % 4 == 3:
                    last.then_inc(z_s, 1)

            pe.wait_ge(n_rt, NH + 1)
            for s in range(NSH + 2):
                if s < NSH:
                    spread(s)
                if s >= 2:
                    y_head(s - 2)
                if s >= 8 and s % 2 == 0 and s < 16:
                    if s == 8:
                        pe.wait_ge(f_fc, 1)
                    gated_sum(s // 2 - 4)
            def out_slab(g, j):
                slab(SL_OUT + 4 * g + j, 0, None, [(k, uh[:, 4 * j + k], ul[:, 4 * j + k]) for k in range(4)],
                     2, j == 0, j == 3, GB[(G_OUT + g) % 2], 256)

            pe.wait_ge(group_free, G_OUT + 1)
            pe.wait_ge(f_yc, 8)
            for t in range(4, 8):
                gated_sum(t)
            for j in range(2):
                pe.wait_ge(z_l, 4 * (j + 1))
                out_slab(0, j)
            pe.wait_ge(h_p, 32)
            pe.wait_ge(z_rt, 2)
            for k in range(2):
                for q in range(QB):
                    pe.transpose(ps[:, 2 * k, q * P:(q + 1) * P], ptok[:, q, k * P:(k + 1) * P], ident)
                pe.transpose(ps[:, 2 * k + 1, 0:NB], pstok[0:NB, k * P:(k + 1) * P], ident[0:NB, 0:NB])\
                    .then_inc(h_pt, 1)
            def residual(g, m0):
                for m in range(2):
                    col = (2 * m0 + m) * P
                    b = GB[g % 2] + 2 * m
                    for q in range(QB):
                        x_ = xt3[:, q, col:col + P]
                        lo_c, hi_c = q * P, (q + 1) * P
                        for f in range(2):
                            a0, a1 = max(lo_c, f * HALF), min(hi_c, (f + 1) * HALF)
                            if a0 < a1:
                                mm(ps[:, b + f, a0 - f * HALF:a1 - f * HALF], x_, ident[:, a0 - lo_c:a1 - lo_c],
                                   start=False, stop=False)
                    mm(ps[:, b + 1, SEQ - HALF:HALF], xs3[0:NB, col:col + P], ident[0:NB, 0:NB],
                       start=False, stop=False)

            for g in range(8):
                if g == 1:
                    pe.wait_ge(h_pc, 4)
                    pe.wait_ge(h_pl, 4)
                if g:
                    pe.wait_ge(group_free, G_OUT + g + 1)
                for j in range(4):
                    if g == 0 and j < 2:
                        continue
                    if g == 0:
                        pe.wait_ge(z_l, 4 * (j + 1))
                    if j == 3:
                        if g == 0:
                            pe.wait_ge(h_x, 16 * 5)
                        residual(G_OUT + g, g)
                    out_slab(g, j)

            def norm_sum(g_free, n):
                pe.wait_ge(group_free, g_free)
                for f in range(2):
                    last = mm(ps[:, f, 0:HALF], ones, acc[:, f * HALF:(f + 1) * HALF], start=True, stop=True)
                last.then_inc(h_s, 1)

            def up(n, g, per_n, per_g, i):
                group(n, g, per_n, per_g, i)
                group(n + 4, g + 1, per_n, per_g, i)

            def down(n, g, per_n, per_g, i, slot, c, per_c):
                pe.wait_ge(m_l, at(2 * c + 3, 2 * per_c, i))
                for j in range(8):
                    pe.wait_ge(group_free, at(g + j + 1, per_g, i))
                    slab(n + j, per_n, i, [(k, hh[:, slot, k], hl[:, slot, k]) for k in range(4)], 2,
                         True, True, GB[(g + j) % 2], 256)

            pe.wait_ge(group_free, G_MLP + 1)
            for j in range(4):
                pe.wait_ge(s_ul, KT + 4 * (j + 1))
                slab(SL_MLP + j, 0, None, [(k, uh[:, 4 * j + k], ul[:, 4 * j + k]) for k in range(4)], 2,
                     j == 0, j == 3, GB[G_MLP % 2], 256)
            pe.wait_ge(h_a, 9)
            norm_sum(G_MLP + 2, 1)
            pe.wait_ge(h_rt, 1)
            group(SL_MLP + 4, G_MLP + 1, 0, 0, None)
            with pe.Fori(0, (CHUNKS - 2) // 2) as i:
                n, g = SL_MLP + 8, G_MLP + 2
                up(n, g, 32, 20, i)
                down(n + 8, g + 2, 32, 20, i, 0, 0, 2)
                up(n + 16, g + 10, 32, 20, i)
                down(n + 24, g + 12, 32, 20, i, 1, 1, 2)
            n, g = SL_PLE - 24, G_PLE - 18
            up(n, g, 0, 0, None)
            down(n + 8, g + 2, 0, 0, None, 0, CHUNKS - 2, 0)
            down(n + 16, g + 10, 0, 0, None, 1, CHUNKS - 1, 0)
            for g in range(8):
                pe.wait_ge(group_free, G_PLE + g + 1)
                slab(SL_PLE + g, 0, None, [(k, ph[:, k], pl[:, k]) for k in range(2)], 2, True, True,
                     GB[(G_PLE + g) % 2], 256)
            pe.wait_ge(s_ul, 2 * KT + 8)
            group(SL_GATE, G_GATE, 0, 0, None)
            pe.wait_ge(h_a, 17)
            norm_sum(G_GATE + 2, 2)
            pe.wait_ge(h_rt, 2)
            group(SL_GATE + 4, G_GATE + 1, 0, 0, None)
            with pe.Fori(0, 3) as i:
                group(SL_GATE + 8, G_GATE + 2, 8, 2, i)
                group(SL_GATE + 12, G_GATE + 3, 8, 2, i)
            for u in range(4 * (QB + 1)):
                if u == 0:
                    pe.wait_ge(group_free, G_GATE + 9)
                    pe.wait_ge(x_h, 8)
                if u == 3:
                    pe.wait_ge(x_h, 9)
                if u == 4:
                    pe.wait_ge(group_free, G_GATE + 10)
                    pe.wait_ge(h_a, 25)
                    for q in range(QB):
                        mm(ps[:, 0, q:q + 1], acc[:, q * P:(q + 1) * P], ones[:, 0:1], start=True, stop=True)
                    mm(ps[0:NB, 0, QB:QB + 1], acc[:, SEQ:T], ones[:, 0:1], start=True, stop=True).then_inc(h_s, 1)
                if u >= 7:
                    v = u - 7
                    if v % 4 == 0:
                        pe.wait_ge(y_c, v // 4 + 1)
                    else:
                        pe.wait_ge(y_d, 3 * (v // 4) + v % 4)
                q, r_ = u // 4, u % 4
                out = y_quarter(u)[0]
                for k in range(4):
                    kt = 4 * r_ + k
                    rows = hT[:, kt, q * P:(q + 1) * P] if q < QB else hT[:, kt, SEQ:T]
                    last = pe.transpose(out[:, k * P:(k + 1) * P], rows, ident)
                last.then_inc(y_t, 1)

        @block.vector
        def _(dve):
            tt, stt_, ts = dve.tensor_tensor, dve.scalar_tensor_tensor, dve.tensor_scalar
            link = Chain(dve, dve_step)
            dve.sem_inc(lo_ready, 2)
            dve.sem_inc(s_kr, 4)

            def lo(c, per=0, i=None):
                dve.wait_ge(hi_ready, at(c + 1, per, i))
                tt(wl[:, c % 2], raw[:, c % 2], wh[:, c % 2].bitcast(F32), ALU.subtract).then_inc(lo_ready, 1)

            dve.wait_ge(s_gt, 3)
            dve.tensor_copy(gcol, ps[:, 4, 0:G_CB + CT]).then_inc(s_gc, 1)
            dve.tensor_copy(cwcol, ps[:, 5, 0:48]).then_inc(s_gc, 1)
            dve.tensor_copy(cst, ps[:, 6, 0:288].rearrange("p (t n) -> p t n", t=CT)).then_inc(s_gc, 1)
            dve.wait_ge(s_xsT, 1)
            dve.wait_ge(s_gc, 3)
            xs_T = ps[:, 7, 0:P].rearrange("p (k n) -> p k n", k=KT)
            g_bcast = gcol[:, G_MIX:G_MIX + KT].unsqueeze(2).to_broadcast([P, KT, NB])
            link(tt(xsg, xs_T, g_bcast, ALU.mult))
            link(dve.tensor_copy(uh[:, :, SEQ:T], xsg))
            tt(ul[:, :, SEQ:T], xsg, uh[:, :, SEQ:T].bitcast(F32), ALU.subtract).then_inc(s_us, 1)
            ts(gcol[:, G_SUB:G_SUB + 1], gcol[:, G_SUB:G_SUB + 1], 1.0 - LAM_INIT, None, ALU.mult)\
                .then_inc(s_gc, 1)
            dve.wait_ge(s_ss, 2)
            link(dve.reciprocal(ssx[:, 0:4], ssx[:, 0:4]))
            link(dve.reciprocal(ssx[0:NB, 4:5], ssx[0:NB, 4:5]))
            for q in range(QB):
                ts(rdiag[:, q, :], ident, ssx[:, q:q + 1], None, ALU.mult).then_inc(s_rt, 1)
            ts(junk[0:NB, 0:NB], ident[0:NB, 0:NB], ssx[0:NB, 4:5], None, ALU.mult).then_inc(s_rt, 1)
            for k in range(KT):
                dve.wait_ge(s_uh, k + 1)
                stt_(ul[:, k, 0:SEQ], ps[:, k % 4, :], gcol[:, G_MIX + k:G_MIX + k + 1],
                     uh[:, k, 0:SEQ].bitcast(F32), ALU.mult, ALU.subtract).then_inc(s_ul, 1)
                if k == 2:
                    lo(0)
                if k == 4:
                    lo(1)
            dve.wait_ge(s_rb, 1)
            dve.tensor_copy(rstd[:, 0:SEQ], ps[:, 4, :]).then_inc(s_rd, 1)
            dve.tensor_copy(rstd[:, SEQ:T], ps[:, 5, 0:NB]).then_inc(s_rd, 1)
            dve.wait_ge(s_rd, 2)
            dve.wait_ge(s_small, 16 * 15)
            for n in range(2):
                dve.tensor_tensor_reduce(lamc[:, 2 * n, :], lamc[:, 2 * n, :], lamc[:, 2 * n + 1, :], 1.0, 0.0,
                                         ALU.mult, ALU.add, lams[:, n:n + 1]).then_inc(s_lam, 1)
            dve.wait_ge(s_lame, 1)
            link(tt(lams[:, 2:3], lams[:, 1:2], lams[:, 0:1], ALU.subtract))
            link(ts(lams[:, 3:4], lams[:, 2:3], -LAM_INIT, None, ALU.add))
            r_b = halves(rstd).unsqueeze(1).to_broadcast([P, 2, 2, HALF])

            def evac(g, per, i, dst):
                dve.wait_ge(w_used, at(4 * (g + 1) + 2, 4 * per, i))
                tt(dst.rearrange("p m (h n) -> p m h n", h=2), group_view(g), r_b, ALU.mult)\
                    .then_inc(group_free, 1)

            def keys(b0, i, j):
                for pg in range(2 * j, 2 * j + 2):
                    dve.wait_ge(s_km, at(16 * b0 + pg + 2, 16, i))
                    dve.tensor_reduce(sc[:, bass.ds(at(b0, 1, i), 1), pg, :],
                                      kpage[:, pg % 4].rearrange("p (c n) -> p c n", n=DK).unsqueeze(1),
                                      AX, ALU.add).then_inc(s_kr, 1)

            def tiles(c, k, i):
                return pj[:, bass.ds(at(c, k, i), 2), :]

            with dve.Fori(0, 2) as i:
                for j in range(8):
                    lo(2 + j, 8, i)
                    if j % 4 == 3:
                        evac(j // 4, 2, i, tiles(2 * (j // 4), 4, i))
            with dve.Fori(0, 4) as i:
                for j in range(8):
                    lo(18 + j, 8, i)
                    keys(0, i, j)
                    if j % 4 == 3:
                        evac(4 + j // 4, 2, i, tiles(8 + 2 * (j // 4), 4, i))
            with dve.Fori(0, 2) as i:
                for j in range(8):
                    lo(50 + j, 8, i)
                    keys(4, i, j)
                    if j % 4 == 3:
                        m = j // 4
                        if m == 0:
                            dve.wait_ge(s_zout, at(16, 32, i))
                        else:
                            dve.wait_ge(s_zout, at(32, 32, i))
                        dve.wait_ge(w_used, at(4 * (12 + m + 1) + 2, 8, i))
                        tt(zst.rearrange("p m (h n) -> p m h n", h=2), group_view(m), r_b, ALU.mult)\
                            .then_inc(s_zst, 1)
                        dve.wait_ge(s_zst, at(m + 1, 2, i))
                        dve.sem_inc(group_free, 1)
            with dve.Fori(0, 2) as i:
                for j in range(8):
                    lo(66 + j, 8, i)
                    keys(6, i, j)
                    if j % 4 == 3:
                        evac(16 + j // 4, 2, i, tiles(24 + 2 * (j // 4), 4, i))
            for j in range(8):
                lo(82 + j)
                if j % 4 == 3:
                    evac(20 + j // 4, 0, None, pj[:, 32 + 2 * (j // 4):34 + 2 * (j // 4), :])
            dve.wait_ge(w_used, SL_OUT + 2)
            tt(halves(dtt[0:NSH]), ps[0:NSH, 0:2, 0:HALF], halves(rstd[0:NSH]), ALU.mult).then_inc(group_free, 1)
            dve.wait_ge(s_qre, 16)
            dve.wait_ge(s_kso, 1)
            link(tt(qtok[0:NB, :], qtok[0:NB, :], kstok[0:NB, :], ALU.mult))
            link(dve.tensor_reduce(sn[0:NB, :], qtok[0:NB, :].rearrange("p (c n) -> p c n", n=DK), AX, ALU.add))
            dve.wait_ge(s_dc, 12)
            dve.wait_ge(s_kr, 4 + NB * PAGES)
            scf = sc.rearrange("p b g c -> p b (g c)")
            link(tt(scf[:, :, 0:256], scf[:, :, 0:256],
                    dbias.rearrange("p g c -> p (g c)").unsqueeze(1).to_broadcast([P, NB, 256]), ALU.add))
            link(tt(sc[0:NB, :, PAGES, :], sn[0:NB, :].unsqueeze(1).to_broadcast([NB, NB, 16]),
                    rowm[0:NB, :].unsqueeze(2).to_broadcast([NB, NB, 16]), ALU.add))
            by_head = sc.rearrange("p b g c -> p b c g")
            dm = lambda t: t.rearrange("p (b c) -> p b c", b=NB)
            dve.tensor_reduce(dm(dmx), by_head, AX, ALU.max).then_inc(s_dv, 1)
            dve.wait_ge(s_dp, 1)
            link(dve.tensor_reduce(dm1, ps[:, 7, 0:P], AX, ALU.max))
            ts(ddiag, ident, dm1[:, 0:1], -1.0, ALU.mult, ALU.mult).then_inc(s_dv, 1)
            dve.wait_ge(s_dp, 2)
            nb = dm(ps[:, 4, 0:P]).unsqueeze(2).to_broadcast([P, NB, PAGES + 1, 16])
            tt(sc, sc, nb, ALU.add).then_inc(s_dv, 1)
            dve.wait_ge(s_dex, 1)
            dve.tensor_reduce(dm(dmx), by_head, AX, ALU.add).then_inc(s_dv, 1)
            dve.wait_ge(s_dp, 3)
            link(dve.reciprocal(drc, ps[:, 5, 0:P]))
            odd = drc.rearrange("p (n c) -> p n c", c=2)[:, :, 1]
            link(ts(odd, odd, lams[:, 3:4], None, ALU.mult))
            link(tt(sc, sc, dm(drc).unsqueeze(2).to_broadcast([P, NB, PAGES + 1, 16]), ALU.mult))
            pair = sc.rearrange("p b g (h c) -> p (b g h) c", c=2)
            tt(wd.rearrange("p b g h -> p (b g h)"), pair[:, :, 0], pair[:, :, 1], ALU.add).then_inc(s_dv, 1)
            dve.wait_ge(s_dv, 5)
            dve.wait_ge(s_zout, 16 * 5)
            UN = NH * QB

            def biased(u):
                h, q = u // QB, u % QB
                n = (q + 1) * P
                if q == 0:
                    link(ts(alibi, dist, SLOPES[h] / SCALE, None, ALU.mult))
                if u >= 3:
                    dve.wait_ge(a_t, u - 2)
                x0 = 384 - q * P
                for c in range(2):
                    dve.wait_ge(a_s, 2 * u + c + 1)
                    dve.tensor_tensor_reduce(se[:, u % 3, c, 0:n], ps[:, (2 * u + c) % 3, 0:n],
                                             alibi[:, x0:x0 + n], 1.0, LOW, ALU.add, ALU.max,
                                             nmx[:, u % 3, c:c + 1]).then_inc(a_b, 1)
                dve.wait_ge(a_b, 2 * u + 2)
                ts(nmx[:, u % 3, :], nmx[:, u % 3, :], -SCALE, None, ALU.mult).then_inc(a_nm, 1)

            def inverse(u):
                dve.wait_ge(a_e, 2 * u + 2)
                link(dve.reciprocal(rsum[:, u % 3, :], sums[:, u % 3, :]))
                ts(rsum[:, u % 3, 1:2], rsum[:, u % 3, 1:2], lams[:, 3:4], None, ALU.mult).then_inc(a_rs, 1)

            def weights(u):
                n = (u % QB + 1) * P
                dve.wait_ge(a_e1, u + 1)
                stt_(se[:, u % 3, 0, 0:n], se[:, u % 3, 0, 0:n], rsum[:, u % 3, 0:1], se[:, u % 3, 1, 0:n],
                     ALU.mult, ALU.add).then_inc(a_w, 1)

            def place(n):
                if n >= 2:
                    dve.wait_ge(s_vu, 4 + 4 * (n - 1))
                p0 = 4 * (n % 4)
                dve.tensor_copy(zpad[:, n % 2, :, 56:64], wd[:, n // 4, p0:p0 + 4, :]).then_inc(s_wz, 1)

            link(dve.memset(zpad, 0.0))
            dve.tensor_copy(wnew[0:NB].rearrange("p (b h) -> p b h", h=NH), wd[0:NB, :, PAGES, :])\
                .then_inc(s_wz, 1)
            place(0)

            lo(SL_OUT)
            lo(SL_OUT + 1)

            def taps(j):
                dve.wait_ge(c_i, j + 1)
                for k in (2, 1, 0):
                    back = 3 - k
                    y_ = yb[:, j % 3, back:SEQ]
                    ins = stt_(y_, pj[:, TX + j, 0:SEQ - back], cwcol[:, k * CT + j:k * CT + j + 1], y_,
                               ALU.mult, ALU.add)
                    if k:
                        link(ins)
                    else:
                        ins.then_inc(c_v, 1)

            def silu(j):
                dve.wait_ge(c_p, j + 1)
                n = SEQ if j < CT else T
                e_ = eb[:, j % 2, 0:n]
                link(dve.reciprocal(e_, e_))
                if j < CT:
                    tt(pj[:, TX + j, 0:SEQ], yb[:, j % 3, 0:SEQ], e_, ALU.mult).then_inc(c_m, 1)
                else:
                    z_ = pj[:, TZ + j - CT, :]
                    tt(z_, z_, e_, ALU.mult).then_inc(c_m, 1)

            def head_norm(h, o_, q_):
                dve.wait_ge(n_rt, h + 1)
                link(dve.reciprocal(q_, q_))
                if h == NH:
                    q_ = q_.rearrange("p (h b) -> p h b", b=NB)
                stt_(o_, o_, gcol[:, G_SUB:G_SUB + 1], q_, ALU.mult, ALU.mult).then_inc(n_o, 1)

            X, E, U, L, M = [v[0:NSH] for v in sp5]

            def dt_step(k):
                if k == 0:
                    link(ts(X, dtt[0:NSH], hcol[0:NSH, 0:1], None, ALU.add))
                    stt_(E, X, -1.0, X, ALU.mult, ALU.max).then_inc(d_v, 1)
                elif k == 1:
                    dve.wait_ge(d_s, 2)
                    ts(U, E, 1.0, None, ALU.add).then_inc(d_v, 1)
                elif k == 2:
                    dve.wait_ge(d_s, 3)
                    link(ts(U, U, -1.0, None, ALU.add))
                    link(ts(M, U, 0.0, None, ALU.is_equal))
                    link(tt(U, U, M, ALU.add))
                    link(tt(L, L, M, ALU.add))
                elif k == 3:
                    link(dve.reciprocal(U, U))
                    link(tt(L, L, U, ALU.mult))
                    link(tt(L, L, E, ALU.mult))
                elif k == 4:
                    link(stt_(dtt[0:NSH], X, 0.0, L, ALU.max, ALU.add))
                    link(ts(hcol[0:NSH, 2:3], hcol[0:NSH, 2:3], -1.0, None, ALU.mult))
                    ts(M, dtt[0:NSH], hcol[0:NSH, 2:3], None, ALU.mult).then_inc(d_v, 1)
                else:
                    dve.wait_ge(d_v, 3)
                    link(dve.memset(U, 1.0))
                    for c in range(QB):
                        link(dve.tensor_tensor_scan(acs[0:NSH, c * P:(c + 1) * P], U[:, c * P:(c + 1) * P],
                                                    M[:, c * P:(c + 1) * P], 0.0, ALU.mult, ALU.add))
                    link(dve.tensor_copy(ecat[0:NSH, NB:2 * NB], dtt[0:NSH, SEQ:T]))
                    dve.tensor_copy(ecat[0:NSH, 16:17], hcol[0:NSH, 3:4]).then_inc(d_v, 1)

            def columns():
                dve.wait_ge(e_t, 1)
                dve.tensor_copy(dtk, ps[:, 0, 0:64].rearrange("p (c h) -> p c h", h=NSH)).then_inc(e_c, 1)
                dve.tensor_copy(ack, ps[:, 0, 64:128].rearrange("p (c h) -> p c h", h=NSH)).then_inc(e_c, 1)
                dve.wait_ge(e_t, 3)
                dve.wait_ge(e_dx, 1)
                dve.tensor_copy(ecol, ps[:, 1, 0:136].rearrange("p (t n) -> p t n", n=17)).then_inc(e_c, 1)
                dve.wait_ge(e_c, 2)
                tt(dsk, ps[:, 1, 256:320].rearrange("p (h c) -> p c h", c=QB), ack, ALU.subtract).then_inc(e_c, 1)
                dve.wait_ge(e_c, 4)
                tt(xdt, pj[:, CX:CX + 8, SEQ:T], ecol[:, :, NB:2 * NB], ALU.mult).then_inc(g_xd, 1)

            cw = cwcol.rearrange("p (j t) -> p t j", t=CT)
            xnew = pj[:, TX:TX + CT, SEQ:T]

            for s in range(UN + 7):
                if s < UN:
                    biased(s)
                if 1 <= s <= UN:
                    inverse(s - 1)
                if 2 <= s < UN + 2:
                    weights(s - 2)
                if s + 1 < 4 * NB:
                    place(s + 1)
                if s == 3:
                    dve.wait_ge(s_out, 16 * 6)
                    dve.wait_ge(s_nv, 1)
                    link(tt(cs4, cst.rearrange("p t (b j) -> p t b j", j=3),
                            cw[:, :, 0:3].unsqueeze(2).to_broadcast([P, CT, NB, 3]), ALU.mult))
                    link(dve.tensor_reduce(csr, cs4, AX, ALU.add))
                    link(tt(csr, csr, gcol[:, G_CB:G_CB + CT].unsqueeze(2).to_broadcast([P, CT, NB]), ALU.add))
                    link(tt(xnew, xnew, cw[:, :, 3:4].to_broadcast([P, CT, NB]), ALU.mult))
                    tt(xnew, xnew, csr, ALU.add).then_inc(c_dv, 1)
                if s == 5:
                    dve.wait_ge(c_de, 1)
                    link(ts(csr, csr, 3.0e38, 1.0, ALU.min, ALU.add))
                    link(dve.reciprocal(csr, csr))
                    link(tt(xnew, xnew, csr, ALU.mult))
                if 4 <= s < CT + 4:
                    taps(s - 4)
                if 6 <= s < JOBS + 6:
                    silu(s - 6)
                if s in (26, 28, 30, 31, 32, 33):
                    dt_step((26, 28, 30, 31, 32, 33).index(s))
                if s == UN + 3:
                    dve.wait_ge(s_vu, 4 + NB * PAGES)
                    dve.tensor_copy(oacc[0:64].rearrange("p (f n) -> p f n", f=2), ps[0:64, 6:8, :])\
                        .then_inc(s_dor, 1)
                if s == UN + 5:
                    dve.wait_ge(s_dos, 1)
                    dve.tensor_copy(pj[:, TQ:TQ + NH, SEQ:T],
                                    ps[:, 7, 0:64].rearrange("p (h b) -> p h b", h=NH)).then_inc(s_dor, 1)
                if s == UN + 6:
                    columns()
                if 8 <= s < UN + 4 and s % QB == 3:
                    h = s // QB - 2
                    head_norm(h, pj[:, TQ + h, 0:SEQ], hq)
            for t in range(8):
                dve.wait_ge(e_xt, t + 1)
                tt(xd[:, :, t * P:(t + 1) * P].rearrange("p c (h n) -> p c h n", h=2),
                   ps[:, 2 + t % 2, :].rearrange("p (c h n) -> p c h n", c=QB, h=2),
                   dtk[:, :, 2 * t:2 * t + 2].unsqueeze(3).to_broadcast([P, QB, 2, HD]), ALU.mult)\
                    .then_inc(e_xd, 1)
            for g in range(2):
                dve.wait_ge(e_cb, g + 1)
                dve.tensor_copy(cbt[:, g], ps[:, 4 + g, :].rearrange("p (c n) -> p c n", c=QB)).then_inc(e_cbc, 1)
            head_norm(NH - 1, pj[:, TQ + NH - 1, 0:SEQ], hq)
            head_norm(NH, pj[:, TQ:TQ + NH, SEQ:T], tmp[:, 0, 0:64])
            for c in range(QB):
                src = ps[:, 2 * (c % 2):2 * (c % 2) + 2, :]
                dst = sall[:, c].rearrange("p (b n) -> p b n", b=2)
                dve.wait_ge(e_st, c + 1)
                if c == 0:
                    dve.tensor_copy(dst, src).then_inc(e_sc, 1)
                else:
                    dve.wait_ge(e_sm, c)
                    tt(dst, dst, src, ALU.add).then_inc(e_sc, 1)
            for s in range(NSH + 3):
                if s < NSH:
                    h = s
                    dve.wait_ge(f_a, h + 1)
                    if h >= 3:
                        dve.wait_ge(f_y, h - 2)
                    for c in range(QB):
                        ins = stt_(dl[h % 3][:, c], ps[:, 4 + h % 4, c * P:(c + 1) * P], ack[:, c, h:h + 1],
                                   causal, ALU.subtract, ALU.add)
                    ins.then_inc(f_d, 1)
                if s % 2 == 0 and s >= 4:
                    t = (s - 4) // 2
                    dve.wait_ge(f_y, 2 * t + 2)
                    stt_(pj[:, TY + t, 0:SEQ], pj[:, CX + t, 0:SEQ], ecol[:, t, 16:17], ps[:, 2 + t % 2, :],
                         ALU.mult, ALU.add).then_inc(f_yc, 1)
                if s % 2 == 1 and s < NSH:
                    t = s // 2
                    dve.wait_ge(g_in[t % 2], 16 * (t // 2 + 1))
                    link(tt(stt[:, t % 2], stt[:, t % 2],
                            ecol[:, t, 0:NB].unsqueeze(2).to_broadcast([P, NB, NS]), ALU.mult))
                    dve.wait_ge(g_b, t + 1)
                    tt(stt[:, t % 2], stt[:, t % 2], bx, ALU.add).then_inc(g_n, 1)
                if s % 2 == 0 and 2 <= s <= NSH:
                    t = s // 2 - 1
                    dve.wait_ge(g_n, t + 1)
                    tt(bx, stt[:, t % 2], bcb[:, 2 + t // 4], ALU.mult).then_inc(g_c, 1)
                    dve.wait_ge(g_c, t + 1)
                    dve.tensor_reduce(ysd[:, t], bx, AX, ALU.add).then_inc(g_r, 1)
                    dve.wait_ge(g_r, t + 1)
                    stt_(pj[:, TY + t, SEQ:T], pj[:, CX + t, SEQ:T], ecol[:, t, 16:17], ysd[:, t],
                         ALU.mult, ALU.add).then_inc(g_y, 1)
            def mix_low(src, dst, k):
                dve.wait_ge(z_h, k + 1)
                tt(ul[:, dst], pj[:, src, :], uh[:, dst].bitcast(F32), ALU.subtract).then_inc(z_l, 1)

            def gated_norm(g):
                for t in range(4 * g, 4 * g + 4):
                    y_ = pj[:, TY + t, :]
                    stt_(y_, y_, gcol[:, G_SSM + t:G_SSM + t + 1], tmp[:, g], ALU.mult, ALU.mult).then_inc(z_o, 1)

            dve.wait_ge(f_y, NSH)
            for t in range(4):
                mix_low(TQ + t, t, t)
            dve.wait_ge(z_rt, 1)
            link(dve.reciprocal(tmp[:, 0], tmp[:, 0]))
            gated_norm(0)
            dve.wait_ge(s_out, 16 * 7)
            for t in range(4, 8):
                mix_low(TQ + t, t, t)
            dve.wait_ge(z_rt, 2)
            link(dve.reciprocal(tmp[:, 1], tmp[:, 1]))
            gated_norm(1)
            for t in range(8):
                mix_low(TY + t, 8 + t, 8 + t)
            for k in range(2):
                dve.wait_ge(h_pc, 2 * k + 2)
                tt(pl[:, k, 0:SEQ], ps[:, 2 * k, :], ph[:, k, 0:SEQ].bitcast(F32), ALU.subtract).then_inc(h_pl, 1)
                tt(pl[:, k, SEQ:T], ps[:, 2 * k + 1, 0:NB], ph[:, k, SEQ:T].bitcast(F32), ALU.subtract)\
                    .then_inc(h_pl, 1)
            for g in range(8):
                for j in range(4):
                    lo(SL_OUT + 2 + 4 * g + j)
                dve.wait_ge(w_used, SL_OUT + 4 * (g + 1) + 2)
                dve.tensor_copy(hT[:, 2 * g:2 * g + 2].rearrange("p m (h n) -> p m h n", h=2),
                                group_view(G_OUT + g)).then_inc(h_e, 1)
                dve.wait_ge(h_e, g + 1)
                dve.sem_inc(group_free, 1)
            for k in range(KT):
                dve.wait_ge(s_uh, KT + k + 1)
                stt_(ul[:, k], hT[:, k], gcol[:, G_FFN + k:G_FFN + k + 1], uh[:, k].bitcast(F32),
                     ALU.mult, ALU.subtract).then_inc(s_ul, 1)
            dve.sem_inc(m_l, 1)

            def relu(n, g, c, per_n, per_c, i):
                dve.wait_ge(w_used, at(n, per_n, i))
                for m in range(2):
                    stt_(halves(tm[:, m]), bank_view(g, m), 0.0, halves(rstd), ALU.max, ALU.mult)\
                        .then_inc(m_t, 1)
                dve.wait_ge(m_t, at(2 * c + 2, 2 * per_c, i))
                dve.sem_inc(group_free, 1)

            def hidden_lo(c, per_c, i, slot, m):
                dve.wait_ge(m_q, at(c + 1, per_c, i))
                tt(hl[:, slot, 2 * m:2 * m + 2], sq, hh[:, slot, 2 * m:2 * m + 2].bitcast(F32), ALU.subtract)\
                    .then_inc(m_l, 1)

            def up(n, g, c, per_n, per_c, i, slot, first=False):
                for m in range(2):
                    for j in range(1, 4):
                        lo(n + 4 * m + j, per_n, i)
                    if first and m == 0:
                        dve.wait_ge(h_rt, 1)
                        link(dve.reciprocal(rstd, rstd))
                    relu(n + 4 * m + 4, g + m, c + m, per_n, per_c, i)
                    lo(n + 4 * m + 4, per_n, i)
                    hidden_lo(c + m, per_c, i, slot, m)

            def down_add(n, g, j, per_n, i):
                dve.wait_ge(w_used, at(n + j + 1, per_n, i))
                x_ = hT[:, 2 * j:2 * j + 2].rearrange("p m (h n) -> p m h n", h=2)
                tt(x_, x_, group_view(g + j), ALU.add).then_inc(group_free, 1)

            def down(n, g, per_n, i):
                for j in range(8):
                    down_add(n, g, j, per_n, i)
                    lo(n + j + 1, per_n, i)

            b = SL_MLP + 2
            lo(b)
            up(b, G_MLP, 0, 0, 0, None, 0, first=True)
            with dve.Fori(0, (CHUNKS - 2) // 2) as i:
                g = G_MLP + 2
                up(b + 8, g, 2, 32, 4, i, 1)
                down(b + 16, g + 2, 32, i)
                up(b + 24, g + 10, 4, 32, 4, i, 0)
                down(b + 32, g + 12, 32, i)
            g = G_PLE - 18
            up(SL_PLE - 22, g, 2 * CHUNKS - 2, 0, 0, None, 1)
            down(SL_PLE - 14, g + 2, 0, None)
            def h_split(j):
                dve.wait_ge(s_uh, 2 * KT + j + 1)
                tt(ul[:, 2 * j:2 * j + 2], hT[:, 2 * j:2 * j + 2], uh[:, 2 * j:2 * j + 2].bitcast(F32),
                   ALU.subtract).then_inc(s_ul, 1)

            for j in range(8):
                down_add(SL_PLE - 6, g + 10, j, 0, None)
                if j < 7:
                    lo(SL_PLE - 6 + j + 1)
                if j:
                    h_split(j - 1)
            h_split(7)
            for g in range(8):
                lo(SL_PLE + 2 + g)
                dve.wait_ge(h_q, 8 + g + 1)
                for m in range(2):
                    k = 2 * g + m
                    ts(halves(eT[:, k]), bank_view(G_PLE + g, m), gcol[:, G_PLN + k:G_PLN + k + 1], None,
                       ALU.mult).then_inc(p_e, 1)
                dve.wait_ge(p_e, 2 * (g + 1))
                dve.sem_inc(group_free, 1)
            lo(SL_GATE + 2)
            lo(SL_GATE + 3)
            dve.sem_inc(x_h, 1)

            def gate(c, per, i):
                dve.wait_ge(w_used, at(SL_GATE + 4 * (c + 1) + 2, 4 * per, i))
                dve.wait_ge(x_h, at(c + 1, per, i))
                ts(tm.rearrange("p m (h n) -> p m h n", h=2), group_view(G_GATE + c), -87.0, None, ALU.max)\
                    .then_inc(x_c, 1)
                dve.wait_ge(x_c, at(c + 1, per, i))
                dve.sem_inc(group_free, 1)

            def gate_recip(c, per, i):
                dve.wait_ge(x_e, at(c + 1, per, i))
                stt_(tm, tm, 1.0, rstd.unsqueeze(1).to_broadcast([P, 2, T]), ALU.add, ALU.mult).then_inc(x_p, 1)
                dve.wait_ge(x_p, at(c + 1, per, i))
                dve.reciprocal(tm, tm).then_inc(x_r, 1)

            def gate_add(c, per, i):
                dve.wait_ge(x_m, at(c + 1, per, i))
                x_ = hT[:, bass.ds(at(2 * c, 2 * per, i), 2), :] if i is not None else hT[:, 2 * c:2 * c + 2, :]
                tt(x_, x_, tm, ALU.add).then_inc(x_h, 1)

            lo(SL_GATE + 4)
            lo(SL_GATE + 5)
            dve.wait_ge(h_rt, 2)
            with dve.Fori(0, 3) as i:
                for m in range(2):
                    gate(m, 2, i)
                    lo(SL_GATE + 6 + 4 * m, 8, i)
                    gate_recip(m, 2, i)
                    lo(SL_GATE + 7 + 4 * m, 8, i)
                    gate_add(m, 2, i)
                    for j in range(2, 4):
                        lo(SL_GATE + 6 + 4 * m + j, 8, i)
            for m in range(2):
                gate(6 + m, 0, None)
                if m == 0:
                    lo(SL_ALL - 2)
                gate_recip(6 + m, 0, None)
                if m == 0:
                    lo(SL_ALL - 1)
                gate_add(6 + m, 0, None)
            dve.wait_ge(h_rt, 4)
            dve.reciprocal(ssx[:, 0:QB], ssx[:, 0:QB]).then_inc(y_s, 1)
            dve.reciprocal(ssx[0:NB, QB:QB + 1], ssx[0:NB, QB:QB + 1]).then_inc(y_s, 1)
            dve.wait_ge(y_s, 2)
            dve.wait_ge(y_g, 16)
            for u in range(4 * (QB + 1)):
                if u % 4:
                    dve.wait_ge(y_t, u + 1)
                    src, dst, rms, gain = y_quarter(u)
                    stt_(dst, src, rms, gain, ALU.mult, ALU.mult).then_inc(y_d, 1)


INPUTS = ["x_prompt", "x_sample", "p_prompt", "p_sample", "cache_k", "cache_v", "page_table", "state_ssm",
          "state_conv", "g_mix", "w_in", "lambda_q1", "lambda_k1", "lambda_q2", "lambda_k2", "w_subln",
          "conv_w", "conv_b", "dt_bias", "a_log", "d_skip", "w_ssm_norm", "w_out", "g_ffn", "w_up",
          "w_down", "w_ple", "w_ple_norm", "w_ple_gate", "g_final"]
OUTPUTS = [("y_prompt", (1, SEQ, D_MODEL)), ("y_sample", (NB, 1, D_MODEL)),
           ("k_prompt", (1, 1, SEQ, NH, P)), ("v_prompt", (1, 1, SEQ, NH, P)),
           ("ssm_prompt", (1, 1, NSH, HD, NS)), ("conv_prompt", (1, 1, CW - 1, CONV_DIM)),
           ("k_sample", (1, NB, 1, NH, P)), ("v_sample", (1, NB, 1, NH, P)),
           ("ssm_sample", (1, NB, NSH, HD, NS)), ("conv_sample", (1, NB, CW - 1, CONV_DIM))]


def kernel(**inputs):
    import numpy as np
    import concourse.bacc as bacc
    from concourse.bass_utils import run_bass_kernel_spmd

    nc = bacc.Bacc("TRN2", target_bir_lowering=False, num_devices=1)
    arrays, ins, outs = {}, {}, {}
    for name in INPUTS:
        a = np.ascontiguousarray(inputs[name])
        arrays[f"in_{name}"] = a
        ins[name] = nc.dram_tensor(f"in_{name}", a.shape, mybir.dt.from_np(a.dtype), kind="ExternalInput").ap()
    for name, shape in OUTPUTS:
        outs[name] = nc.dram_tensor(f"out_{name}", shape, F32, kind="ExternalOutput").ap()
    build(nc, ins, outs)
    r = run_bass_kernel_spmd(nc, [arrays], core_ids=[0])
    return tuple(r.results[0][f"out_{name}"] for name, _ in OUTPUTS)
```
